# Optimizing a Trainium2 kernel written in Bass

```python
import jax, jax.numpy as jnp
from jax import lax
import numpy as np
import jax
import jax.numpy as jnp

D_MODEL = 1024
BATCH = 1
SEQ = 512
DEPTH = 2

HEAD_DIM = 64
N_Q_HEADS = 8
N_KV_HEADS = 2
ATTN_WIDTH = N_Q_HEADS * HEAD_DIM
KV_WIDTH = N_KV_HEADS * HEAD_DIM
LRU_HEADS = 4
LRU_WIDTH = LRU_HEADS * HEAD_DIM
CONV_GROUPS = 4
CONV_WIDTH = CONV_GROUPS * HEAD_DIM
MIX_WIDTH = ATTN_WIDTH + LRU_WIDTH + CONV_WIDTH
IN_SPLITS = (ATTN_WIDTH, KV_WIDTH, KV_WIDTH, LRU_WIDTH, LRU_WIDTH, CONV_WIDTH, CONV_WIDTH, CONV_WIDTH)
IN_PROJ_WIDTH = sum(IN_SPLITS)
WINDOW = 128
BLOCK = 128
LRU_CONV_K = 4
SHORT_CONV_K = 3
LRU_C = 8.0
D_FF = ((8 * D_MODEL // 3 + 127) // 128) * 128
N_SUBLAYERS = 3
N_MOD = 3 * N_SUBLAYERS
EPS = 1e-6
NEG_INF = -1e30


def rmsnorm(x, g):
    xf = x.astype(jnp.float32)
    y = xf * lax.rsqrt(jnp.mean(xf * xf, axis=-1, keepdims=True) + EPS)
    return (y * g.astype(jnp.float32)).astype(x.dtype)

def modulate(x, g, shift, scale):
    return rmsnorm(x, g) * (1.0 + scale[:, None, :]) + shift[:, None, :]

def swiglu(h, w_gu, w_down):
    gu = h @ w_gu
    g, u = jnp.split(gu, 2, axis=-1)
    return (jax.nn.silu(g) * u) @ w_down

def causal_depthwise_conv(x, w, b=None):
    K = w.shape[0]
    S = x.shape[1]
    xp = jnp.pad(x, ((0, 0), (K - 1, 0), (0, 0)))
    y = xp[:, 0:S] * w[0]
    for k in range(1, K):
        y = y + xp[:, k:k + S] * w[k]
    if b is not None:
        y = y + b
    return y

def alibi_slopes(n_heads):
    return jnp.asarray(2.0 ** (-8.0 * np.arange(1, n_heads + 1) / n_heads), dtype=jnp.float32)

def sliding_window_attention(q, k, v, sinks):
    b, s = q.shape[:2]
    nb = s // BLOCK
    G = N_Q_HEADS // N_KV_HEADS
    qb = q.reshape(b, nb, BLOCK, N_KV_HEADS, G, HEAD_DIM)

    def band(t):
        tb = t.reshape(b, nb, BLOCK, N_KV_HEADS, HEAD_DIM)
        prev = jnp.pad(tb[:, :-1], ((0, 0), (1, 0), (0, 0), (0, 0), (0, 0)))
        return jnp.concatenate([prev, tb], axis=2)

    kb, vb = band(k), band(v)
    scores = jnp.einsum('bnqkgd,bnskd->bnkgqs', qb, kb).astype(jnp.float32) * (HEAD_DIM ** -0.5)
    qi = jnp.arange(BLOCK)[:, None]
    kj = jnp.arange(2 * BLOCK)[None, :]
    dist = qi + BLOCK - kj
    in_window = (dist >= 0) & (dist < WINDOW)
    blk = jnp.arange(nb)[:, None, None]
    valid = in_window[None] & ((blk > 0) | (kj[None] >= BLOCK))
    slopes = alibi_slopes(N_Q_HEADS).reshape(N_KV_HEADS, G)
    bias = -slopes[:, :, None, None] * dist.astype(jnp.float32)
    scores = jnp.where(valid[None, :, None, None], scores + bias[None, None], NEG_INF)
    sink = sinks.astype(jnp.float32).reshape(N_KV_HEADS, G)[None, None, :, :, None, None]
    m = jnp.maximum(jnp.max(scores, axis=-1, keepdims=True), sink)
    p = jnp.exp(scores - m)
    denom = jnp.sum(p, axis=-1, keepdims=True) + jnp.exp(sink - m)
    out = jnp.einsum('bnkgqs,bnskd->bnqkgd', (p / denom).astype(v.dtype), vb)
    return out.reshape(b, s, ATTN_WIDTH)

def rg_lru(x, gate_a_w, gate_a_b, gate_x_w, gate_x_b, lam):
    b, s, _ = x.shape
    xh = x.reshape(b, s, LRU_HEADS, HEAD_DIM)
    r = jax.nn.sigmoid(jnp.einsum('bshd,hde->bshe', xh, gate_a_w).reshape(b, s, LRU_WIDTH) + gate_a_b)
    i = jax.nn.sigmoid(jnp.einsum('bshd,hde->bshe', xh, gate_x_w).reshape(b, s, LRU_WIDTH) + gate_x_b)
    log_a = -LRU_C * r.astype(jnp.float32) * jax.nn.softplus(-lam.astype(jnp.float32))
    a = jnp.exp(log_a)
    mult = jnp.sqrt(-jnp.expm1(2.0 * log_a))
    first = (jnp.arange(s) == 0)[None, :, None]
    mult = jnp.where(first, 1.0, mult)
    u = mult * (i * x).astype(jnp.float32)

    def combine(left, right):
        a1, b1 = left
        a2, b2 = right
        return a1 * a2, a2 * b1 + b2

    _, h = lax.associative_scan(combine, (a, u), axis=1)
    return h.astype(x.dtype)

def hybrid_mixer(h, w_in, w_out, sinks, lru_conv_w, lru_conv_b, lru_gate_a_w, lru_gate_a_b,
                 lru_gate_x_w, lru_gate_x_b, lru_lambda, sc_conv_w):
    proj = h @ w_in
    offs = np.cumsum(IN_SPLITS)[:-1].tolist()
    q, k, v, lx, lg, sb, sc, sx = jnp.split(proj, offs, axis=-1)
    y_attn = sliding_window_attention(q, k, v, sinks)
    lx = causal_depthwise_conv(lx, lru_conv_w, lru_conv_b)
    y_lru = jax.nn.gelu(lg) * rg_lru(lx, lru_gate_a_w, lru_gate_a_b, lru_gate_x_w, lru_gate_x_b, lru_lambda)
    y_sc = sb * causal_depthwise_conv(sc * sx, sc_conv_w)
    y = jnp.concatenate([y_attn, y_lru, y_sc], axis=-1)
    return y @ w_out

def first_inputs(seed: int = 0) -> dict:
    key = jax.random.key(seed)
    ks = jax.random.split(key, 24)
    f32 = jnp.float32

    def nrm(k, shape, scale):
        return jax.random.normal(k, shape, f32) * scale

    u = jax.random.uniform(ks[17], (DEPTH, LRU_WIDTH), f32, 0.9, 0.999)
    a0 = u ** (1.0 / LRU_C)
    lru_lambda = jnp.log(a0) - jnp.log1p(-a0)
    return {
        "x": nrm(ks[0], (BATCH, SEQ, D_MODEL), 1.0),
        "c": nrm(ks[1], (BATCH, D_MODEL), 1.0),
        "w_mod": nrm(ks[2], (DEPTH, D_MODEL, N_MOD * D_MODEL), D_MODEL ** -0.5),
        "b_mod": nrm(ks[3], (DEPTH, N_MOD * D_MODEL), 0.02),
        "g_norm": 1.0 + nrm(ks[4], (DEPTH, N_SUBLAYERS, D_MODEL), 0.02),
        "w_ffn1_gu": nrm(ks[5], (DEPTH, D_MODEL, 2 * D_FF), D_MODEL ** -0.5),
        "w_ffn1_down": nrm(ks[6], (DEPTH, D_FF, D_MODEL), D_FF ** -0.5),
        "w_ffn2_gu": nrm(ks[7], (DEPTH, D_MODEL, 2 * D_FF), D_MODEL ** -0.5),
        "w_ffn2_down": nrm(ks[8], (DEPTH, D_FF, D_MODEL), D_FF ** -0.5),
        "w_in": nrm(ks[9], (DEPTH, D_MODEL, IN_PROJ_WIDTH), D_MODEL ** -0.5),
        "w_out": nrm(ks[10], (DEPTH, MIX_WIDTH, D_MODEL), MIX_WIDTH ** -0.5),
        "attn_sinks": nrm(ks[11], (DEPTH, N_Q_HEADS), 0.5),
        "lru_conv_w": nrm(ks[12], (DEPTH, LRU_CONV_K, LRU_WIDTH), LRU_CONV_K ** -0.5),
        "lru_conv_b": nrm(ks[13], (DEPTH, LRU_WIDTH), 0.02),
        "lru_gate_a_w": nrm(ks[14], (DEPTH, LRU_HEADS, HEAD_DIM, HEAD_DIM), HEAD_DIM ** -0.5),
        "lru_gate_a_b": nrm(ks[15], (DEPTH, LRU_WIDTH), 0.02),
        "lru_gate_x_w": nrm(ks[16], (DEPTH, LRU_HEADS, HEAD_DIM, HEAD_DIM), HEAD_DIM ** -0.5),
        "lru_gate_x_b": nrm(ks[18], (DEPTH, LRU_WIDTH), 0.02),
        "lru_lambda": lru_lambda,
        "sc_conv_w": nrm(ks[19], (DEPTH, SHORT_CONV_K, CONV_WIDTH), SHORT_CONV_K ** -0.5),
        "g_final": 1.0 + nrm(ks[20], (D_MODEL,), 0.02),
    }

def first_block(x, c, w_mod, b_mod, g_norm, w_ffn1_gu, w_ffn1_down, w_ffn2_gu, w_ffn2_down,
              w_in, w_out, attn_sinks, lru_conv_w, lru_conv_b, lru_gate_a_w, lru_gate_a_b,
              lru_gate_x_w, lru_gate_x_b, lru_lambda, sc_conv_w, g_final):
    c_act = jax.nn.silu(c)
    for l in range(DEPTH):
        mod = (c_act @ w_mod[l] + b_mod[l]).reshape(c.shape[0], N_MOD, D_MODEL)
        h = modulate(x, g_norm[l, 0], mod[:, 0], mod[:, 1])
        x = x + 0.5 * mod[:, 2][:, None, :] * swiglu(h, w_ffn1_gu[l], w_ffn1_down[l])
        h = modulate(x, g_norm[l, 1], mod[:, 3], mod[:, 4])
        x = x + mod[:, 5][:, None, :] * hybrid_mixer(
            h, w_in[l], w_out[l], attn_sinks[l], lru_conv_w[l], lru_conv_b[l],
            lru_gate_a_w[l], lru_gate_a_b[l], lru_gate_x_w[l], lru_gate_x_b[l],
            lru_lambda[l], sc_conv_w[l])
        h = modulate(x, g_norm[l, 2], mod[:, 6], mod[:, 7])
        x = x + 0.5 * mod[:, 8][:, None, :] * swiglu(h, w_ffn2_gu[l], w_ffn2_down[l])
    return rmsnorm(x, g_final)


DEPTH_2 = 1

GRID_W = 64
CTX_LEN = 256
MLA_HEADS = 8
MLA_NOPE = 64
MLA_ROPE = 32
MLA_V_HEAD = 64
MLA_Q_LORA = 384
MLA_KV_LORA = 256
MLA_WIDTH = MLA_HEADS * MLA_V_HEAD
MLA_SCALE = (MLA_NOPE + MLA_ROPE) ** -0.5
ROPE_AXIS_DIM = MLA_ROPE // 2
ROPE_THETA = 10000.0
Q_BLOCK = 128
GLA_HEADS = 4
GLA_HEAD_K = 128
GLA_HEAD_V = 128
GLA_KEY = GLA_HEADS * GLA_HEAD_K
GLA_VALUE = GLA_HEADS * GLA_HEAD_V
GLA_QSCALE = GLA_HEAD_K ** -0.5
GATE_RANK = 16
GATE_NORM = 16.0
GLA_CHUNK = 64
D_FF_2 = 2816
CONV_W = 3
IN_SPLITS_2 = (MLA_Q_LORA, MLA_KV_LORA, MLA_ROPE, GLA_KEY, GLA_KEY, GLA_VALUE, GLA_VALUE, 2 * GATE_RANK, 2 * D_MODEL)
IN_COLS = sum(IN_SPLITS_2)


def rms_norm(x, g):
    xf = x.astype(jnp.float32)
    y = xf * lax.rsqrt(jnp.mean(xf * xf, axis=-1, keepdims=True) + EPS)
    return (y * g.astype(jnp.float32)).astype(x.dtype)

def modulate_2(h, shift, scale):
    return h * (1 + scale) + shift

def split_columns(z):
    offsets = [int(o) for o in np.cumsum(IN_SPLITS_2)[:-1]]
    return jnp.split(z, offsets, axis=-1)

def heads(z, n_heads):
    return z.reshape(z.shape[:-1] + (n_heads, z.shape[-1] // n_heads))

def axial_angles(length):
    t = jnp.arange(length, dtype=jnp.int32)
    row = (t // GRID_W).astype(jnp.float32)
    col = (t % GRID_W).astype(jnp.float32)
    inv_freq = ROPE_THETA ** (-jnp.arange(0, ROPE_AXIS_DIM, 2, dtype=jnp.float32) / ROPE_AXIS_DIM)
    return row[:, None] * inv_freq, col[:, None] * inv_freq

def rotate_axis(x, ang):
    x1, x2 = jnp.split(x, 2, axis=-1)
    cos, sin = jnp.cos(ang), jnp.sin(ang)
    return jnp.concatenate([x1 * cos - x2 * sin, x2 * cos + x1 * sin], axis=-1)

def rope_2d(x, ang_row, ang_col):
    xf = x.astype(jnp.float32)
    xr, xc = xf[..., :ROPE_AXIS_DIM], xf[..., ROPE_AXIS_DIM:]
    return jnp.concatenate([rotate_axis(xr, ang_row), rotate_axis(xc, ang_col)], axis=-1).astype(x.dtype)

def mla_queries(q_c, q_norm_g, w_uq):
    q = heads(rms_norm(q_c, q_norm_g) @ w_uq, MLA_HEADS)
    return q[..., :MLA_NOPE], q[..., MLA_NOPE:]

def mla_keys_values(kv_c, kv_norm_g, w_ukv):
    kv = heads(rms_norm(kv_c, kv_norm_g) @ w_ukv, MLA_HEADS)
    return kv[..., :MLA_NOPE], kv[..., MLA_NOPE:]

def attention(q_nope, q_rope, k_nope, k_rope, v):
    b, lq = q_nope.shape[:2]
    nb = lq // Q_BLOCK

    def blocks(z):
        return jnp.moveaxis(z.reshape((b, nb, Q_BLOCK) + z.shape[2:]), 1, 0)

    def one_block(qs):
        qn, qr = qs
        s = jnp.einsum('bqhd,bkhd->bhqk', qn, k_nope) + jnp.einsum('bqhr,bkr->bhqk', qr, k_rope)
        p = jax.nn.softmax(s.astype(jnp.float32) * MLA_SCALE, axis=-1).astype(v.dtype)
        return jnp.einsum('bhqk,bkhd->bqhd', p, v)

    o = lax.map(one_block, (blocks(q_nope), blocks(q_rope)))
    return jnp.moveaxis(o, 0, 1).reshape(b, lq, MLA_WIDTH)

def to_chunks(z):
    b, l, h, d = z.shape
    return z.reshape(b, l // GLA_CHUNK, GLA_CHUNK, h, d).transpose(0, 3, 1, 2, 4)

def from_chunks(z):
    b, h, n, c, d = z.shape
    return z.transpose(0, 2, 3, 1, 4).reshape(b, n * c, h, d)

def chunk_state_terms(kc, vc, b_cum):
    b_last = b_cum[..., -1:, :]
    u = jnp.einsum('bhncd,bhncv->bhndv', kc * jnp.exp(b_last - b_cum), vc)
    decay = jnp.exp(b_last[..., 0, :])
    return decay, u

def scan_states(decay, u, s0):
    def step(s, inp):
        d, du = inp
        return d[..., None] * s + du, s

    s_final, s_in = lax.scan(step, s0, (jnp.moveaxis(decay, 2, 0), jnp.moveaxis(u, 2, 0)))
    return s_final, jnp.moveaxis(s_in, 0, 2)

def gla_direction(q, k, v, g, s0):
    qc, kc, vc = (to_chunks(z.astype(jnp.float32)) for z in (q, k, v))
    b_cum = jnp.cumsum(to_chunks(g), axis=3)
    decay, u = chunk_state_terms(kc, vc, b_cum)
    s_final, s_in = scan_states(decay, u, s0)
    qe = qc * jnp.exp(b_cum)
    mask = jnp.tril(jnp.ones((GLA_CHUNK, GLA_CHUNK), jnp.float32))
    a = jnp.einsum('bhncd,bhnsd->bhncs', qe, kc * jnp.exp(-b_cum)) * mask
    o = jnp.einsum('bhncs,bhnsv->bhncv', a, vc) + jnp.einsum('bhncd,bhndv->bhncv', qe, s_in)
    return from_chunks(o), s_final

def gla_final_state(k, v, g, s0):
    kc, vc = to_chunks(k.astype(jnp.float32)), to_chunks(v.astype(jnp.float32))
    decay, u = chunk_state_terms(kc, vc, jnp.cumsum(to_chunks(g), axis=3))
    s_final, _ = scan_states(decay, u, s0)
    return s_final

def flip(z):
    return jnp.flip(z, axis=1)

def gla_bidirectional(q, k, v, g_f, g_b, s_f, s_b):
    o_f, s_f_out = gla_direction(q, k, v, g_f, s_f)
    o_b, s_b_out = gla_direction(flip(q), flip(k), flip(v), flip(g_b), s_b)
    return o_f + flip(o_b), s_f_out, s_b_out

def gla_inputs(gq, gk, gv, glow, w_decay, b_decay):
    lf, lb = glow[..., :GATE_RANK], glow[..., GATE_RANK:]
    g_f = jax.nn.log_sigmoid((lf @ w_decay[0] + b_decay[0]).astype(jnp.float32)) / GATE_NORM
    g_b = jax.nn.log_sigmoid((lb @ w_decay[1] + b_decay[1]).astype(jnp.float32)) / GATE_NORM
    return (heads(gq, GLA_HEADS) * GLA_QSCALE, heads(gk, GLA_HEADS), heads(gv, GLA_HEADS),
            heads(g_f, GLA_HEADS), heads(g_b, GLA_HEADS))

def gla_branch(o, r, norm_g, w_br):
    y = rms_norm(o, norm_g).reshape(o.shape[0], o.shape[1], GLA_VALUE).astype(r.dtype) * jax.nn.silu(r)
    return y @ w_br

def merge_branches(br_mla, br_gla, gate_logits, w_out):
    g = jax.nn.sigmoid(gate_logits.astype(jnp.float32)).astype(br_mla.dtype)
    g_mla, g_gla = jnp.split(g, 2, axis=-1)
    return (g_mla * br_mla + g_gla * br_gla) @ w_out

def token_mixer(h, hc, w_in, q_norm_g, w_uq, kv_norm_g, w_ukv, w_decay, b_decay, gla_norm_g,
                w_br_mla, w_br_gla, w_out, ang_row, ang_col, update_ctx):
    q_c, kv_c, k_rope, gq, gk, gv, gr, glow, gate_logits = split_columns(h @ w_in)
    q_cc, kv_cc, k_rope_c, gq_c, gk_c, gv_c, gr_c, glow_c, gate_logits_c = split_columns(hc @ w_in)

    k_nope_c, v_c = mla_keys_values(kv_cc, kv_norm_g, w_ukv)
    k_nope, v = mla_keys_values(kv_c, kv_norm_g, w_ukv)
    q_nope, q_rope = mla_queries(q_c, q_norm_g, w_uq)
    q_rope = rope_2d(q_rope, ang_row[:, None, :], ang_col[:, None, :])
    k_rope = rope_2d(k_rope, ang_row, ang_col)
    o_mla = attention(q_nope, q_rope,
                      jnp.concatenate([k_nope, k_nope_c], axis=1),
                      jnp.concatenate([k_rope, k_rope_c], axis=1),
                      jnp.concatenate([v, v_c], axis=1))

    b = h.shape[0]
    s0 = jnp.zeros((b, GLA_HEADS, GLA_HEAD_K, GLA_HEAD_V), jnp.float32)
    qg_c, kg_c, vg_c, gf_c, gb_c = gla_inputs(gq_c, gk_c, gv_c, glow_c, w_decay, b_decay)
    qg, kg, vg, gf, gb = gla_inputs(gq, gk, gv, glow, w_decay, b_decay)
    if update_ctx:
        o_gla_c, s_f, s_b = gla_bidirectional(qg_c, kg_c, vg_c, gf_c, gb_c, s0, s0)
    else:
        s_f = gla_final_state(kg_c, vg_c, gf_c, s0)
        s_b = gla_final_state(flip(kg_c), flip(vg_c), flip(gb_c), s0)
    o_gla, _, _ = gla_bidirectional(qg, kg, vg, gf, gb, s_f, s_b)

    out_lat = merge_branches(o_mla @ w_br_mla, gla_branch(o_gla, gr, gla_norm_g, w_br_gla), gate_logits, w_out)
    out_ctx = None
    if update_ctx:
        q_nope_c, q_rope_c = mla_queries(q_cc, q_norm_g, w_uq)
        o_mla_c = attention(q_nope_c, q_rope_c, k_nope_c, k_rope_c, v_c)
        out_ctx = merge_branches(o_mla_c @ w_br_mla, gla_branch(o_gla_c, gr_c, gla_norm_g, w_br_gla),
                                 gate_logits_c, w_out)
    return out_lat, out_ctx

def depthwise_conv_grid(u, w, bias, rows, cols):
    b, l, ch = u.shape
    grid = u.reshape(b, rows, cols, ch)
    y = lax.conv_general_dilated(grid, w[:, :, None, :].astype(u.dtype), (1, 1), 'SAME',
                                 dimension_numbers=('NHWC', 'HWIO', 'NHWC'), feature_group_count=ch)
    return y.reshape(b, l, ch) + bias

def conv_ffn(h, w_up, conv_w, conv_b, w_down, rows, cols):
    val, gate = jnp.split(h @ w_up, 2, axis=-1)
    gate = depthwise_conv_grid(gate, conv_w, conv_b, rows, cols)
    return (jax.nn.gelu(gate, approximate=False) * val) @ w_down

def second_inputs(seed: int = 0) -> dict:
    key = jax.random.key(seed)
    ks = jax.random.split(key, 24)
    f32 = jnp.float32

    def normal(k, shape, s=1.0):
        return s * jax.random.normal(k, shape, f32)

    def dense(k, shape, fan_in, gain=1.0):
        return normal(k, shape, gain * fan_in ** -0.5)

    def norm_gain(k, shape):
        return 1.0 + normal(k, shape, 0.05)

    return {
        "x": normal(ks[0], (BATCH, SEQ, D_MODEL)),
        "c": normal(ks[1], (BATCH, D_MODEL)),
        "ctx": normal(ks[2], (BATCH, CTX_LEN, D_MODEL)),
        "c_ctx": normal(ks[3], (D_MODEL,)),
        "w_ada": dense(ks[4], (DEPTH_2, D_MODEL, 6 * D_MODEL), D_MODEL, 0.5),
        "b_ada": normal(ks[5], (DEPTH_2, 6 * D_MODEL), 0.01),
        "norm1_g": norm_gain(ks[6], (DEPTH_2, D_MODEL)),
        "w_in": dense(ks[7], (DEPTH_2, D_MODEL, IN_COLS), D_MODEL),
        "q_norm_g": norm_gain(ks[8], (DEPTH_2, MLA_Q_LORA)),
        "w_uq": dense(ks[9], (DEPTH_2, MLA_Q_LORA, MLA_HEADS * (MLA_NOPE + MLA_ROPE)), MLA_Q_LORA),
        "kv_norm_g": norm_gain(ks[10], (DEPTH_2, MLA_KV_LORA)),
        "w_ukv": dense(ks[11], (DEPTH_2, MLA_KV_LORA, MLA_HEADS * (MLA_NOPE + MLA_V_HEAD)), MLA_KV_LORA),
        "gla_w_decay": dense(ks[12], (DEPTH_2, 2, GATE_RANK, GLA_KEY), GATE_RANK),
        "gla_b_decay": normal(ks[13], (DEPTH_2, 2, GLA_KEY), 0.1),
        "gla_norm_g": norm_gain(ks[14], (DEPTH_2, GLA_HEAD_V)),
        "w_br_mla": dense(ks[15], (DEPTH_2, MLA_WIDTH, D_MODEL), MLA_WIDTH),
        "w_br_gla": dense(ks[16], (DEPTH_2, GLA_VALUE, D_MODEL), GLA_VALUE),
        "w_out": dense(ks[17], (DEPTH_2, D_MODEL, D_MODEL), D_MODEL),
        "norm2_g": norm_gain(ks[18], (DEPTH_2, D_MODEL)),
        "w_up": dense(ks[19], (DEPTH_2, D_MODEL, 2 * D_FF_2), D_MODEL),
        "conv_w": dense(ks[20], (DEPTH_2, CONV_W, CONV_W, D_FF_2), CONV_W * CONV_W),
        "conv_b": normal(ks[21], (DEPTH_2, D_FF_2), 0.01),
        "w_down": dense(ks[22], (DEPTH_2, D_FF_2, D_MODEL), D_FF_2),
        "final_g": norm_gain(ks[23], (D_MODEL,)),
    }

def second_block(x, c, ctx, c_ctx, w_ada, b_ada, norm1_g, w_in, q_norm_g, w_uq, kv_norm_g, w_ukv,
              gla_w_decay, gla_b_decay, gla_norm_g, w_br_mla, w_br_gla, w_out, norm2_g, w_up,
              conv_w, conv_b, w_down, final_g):
    length = x.shape[1]
    rows = length // GRID_W
    ang_row, ang_col = axial_angles(length)
    x_lat, x_ctx = x, ctx
    for layer in range(DEPTH_2):
        update_ctx = layer + 1 < DEPTH_2
        mod = jax.nn.silu(c) @ w_ada[layer] + b_ada[layer]
        mod_c = jax.nn.silu(c_ctx) @ w_ada[layer] + b_ada[layer]
        sh1, sc1, gt1, sh2, sc2, gt2 = jnp.split(mod[:, None, :], 6, axis=-1)
        sh1c, sc1c, gt1c, sh2c, sc2c, gt2c = jnp.split(mod_c, 6, axis=-1)

        h = modulate_2(rms_norm(x_lat, norm1_g[layer]), sh1, sc1)
        hc = modulate_2(rms_norm(x_ctx, norm1_g[layer]), sh1c, sc1c)
        mix, mix_c = token_mixer(h, hc, w_in[layer], q_norm_g[layer], w_uq[layer], kv_norm_g[layer],
                                 w_ukv[layer], gla_w_decay[layer], gla_b_decay[layer], gla_norm_g[layer],
                                 w_br_mla[layer], w_br_gla[layer], w_out[layer], ang_row, ang_col, update_ctx)
        x_lat = x_lat + gt1 * mix
        h = modulate_2(rms_norm(x_lat, norm2_g[layer]), sh2, sc2)
        x_lat = x_lat + gt2 * conv_ffn(h, w_up[layer], conv_w[layer], conv_b[layer], w_down[layer], rows, GRID_W)
        if update_ctx:
            x_ctx = x_ctx + gt1c * mix_c
            hc = modulate_2(rms_norm(x_ctx, norm2_g[layer]), sh2c, sc2c)
            x_ctx = x_ctx + gt2c * conv_ffn(hc, w_up[layer], conv_w[layer], conv_b[layer], w_down[layer],
                                            1, x_ctx.shape[1])
    return rms_norm(x_lat, final_g)


def setup_inputs(seed=0):
    out = dict(first_inputs(seed))
    for name, value in second_inputs(seed + 1).items():
        if name != "x":
            out[name + "_2"] = value
    return out


def reference(
    x, c, w_mod, b_mod, g_norm, w_ffn1_gu, w_ffn1_down, w_ffn2_gu, w_ffn2_down, w_in, w_out,
    attn_sinks, lru_conv_w, lru_conv_b, lru_gate_a_w, lru_gate_a_b, lru_gate_x_w, lru_gate_x_b,
    lru_lambda, sc_conv_w, g_final, c_2, ctx_2, c_ctx_2, w_ada_2, b_ada_2, norm1_g_2, w_in_2,
    q_norm_g_2, w_uq_2, kv_norm_g_2, w_ukv_2, gla_w_decay_2, gla_b_decay_2, gla_norm_g_2,
    w_br_mla_2, w_br_gla_2, w_out_2, norm2_g_2, w_up_2, conv_w_2, conv_b_2, w_down_2, final_g_2,
):
    x = first_block(
        x, c, w_mod, b_mod, g_norm, w_ffn1_gu, w_ffn1_down, w_ffn2_gu, w_ffn2_down, w_in, w_out,
        attn_sinks, lru_conv_w, lru_conv_b, lru_gate_a_w, lru_gate_a_b, lru_gate_x_w,
        lru_gate_x_b, lru_lambda, sc_conv_w, g_final,
    )
    return second_block(
        x, c_2, ctx_2, c_ctx_2, w_ada_2, b_ada_2, norm1_g_2, w_in_2, q_norm_g_2, w_uq_2,
        kv_norm_g_2, w_ukv_2, gla_w_decay_2, gla_b_decay_2, gla_norm_g_2, w_br_mla_2,
        w_br_gla_2, w_out_2, norm2_g_2, w_up_2, conv_w_2, conv_b_2, w_down_2, final_g_2,
    )


_drawn_inputs = setup_inputs


def setup_inputs(seed=0):
    import zlib

    import numpy as np

    out = dict(_drawn_inputs(seed))
    spreads = {}
    factors = {'attn_sinks': 2.805,
     'lru_gate_a_b': 8.0,
     'lru_gate_x_b': 8.0,
     'g_final': 2.683,
     'ctx_2': 4.192,
     'c_ctx_2': 3.052,
     'b_ada_2': 5.354,
     'norm1_g_2': 4.107,
     'q_norm_g_2': 8.0,
     'w_uq_2': 3.132,
     'kv_norm_g_2': 8.0,
     'gla_b_decay_2': 6.725,
     'gla_norm_g_2': 8.0,
     'norm2_g_2': 3.468,
     'conv_b_2': 44.511}
    for name, (base, spread) in spreads.items():
        noise = np.random.default_rng([zlib.crc32(name.encode()), seed]).standard_normal(out[name].shape)
        drawn = base * np.exp(spread * noise) if base else spread * noise
        out[name] = jnp.asarray(drawn.astype(out[name].dtype))
    for name, factor in factors.items():
        out[name] = (out[name] * factor).astype(out[name].dtype)
    return out
```

```python
from contextlib import ExitStack

import concourse.bass as bass
from concourse import mybir

ALU = mybir.AluOpType
ACT = mybir.ActivationFunctionType
AX = mybir.AxisListType
F32 = mybir.dt.float32
F32R = mybir.dt.float32r

P = 128
D = 1024
DC = D // P
T = 512
DEPTH = 2
EPS = 1e-6
D_FF = 2816
FC = D_FF // P
THIRDS = (8, 8, 6)
WINDOW = 128
HEADS = 8
LRU_TILES = 2

KC = 8
BLOCK_COLS = 256
BLOCK = KC * BLOCK_COLS
RAW_SLOTS = 4
FFN_BLOCKS = FC + 3 * (D // BLOCK_COLS)
MIX_IN_BLOCKS = 8
MIX_BLOCKS = MIX_IN_BLOCKS + D // BLOCK_COLS
LAYER_BLOCKS = 2 * FFN_BLOCKS + MIX_BLOCKS

MOD_COLS = 512
MOD_K = 2
MOD_PIECES = DC // MOD_K
LAYER_MODS = 24

TC = 256
TK = T + TC
MLA_HEADS, NOPE, ROPE = 8, 64, 32
MLA_SCALE = (NOPE + ROPE) ** -0.5
Q_LORA_C, KV_LORA_C = 3, 2
GLA_HEADS, GLA_CHUNK = 4, 64
GLA_QSCALE = 128 ** -0.5
GATE_NORM = 16.0
GRID_W = 64
CONV_COLS = 10
CTX_K, X_K, V_K, PAIR_K, GLA_K, MERGE_K, OUT_K, FFN_K = 0, 6, 9, 10, 14, 22, 34, 38
R_FINAL1, R_CTX, R_X1, R_KVC, R_KVX, R_QX, R_GLA, R_X2, R_FINAL2 = 6, 7, 8, 9, 10, 11, 12, 16, 17


def alibi_slope(h):
    return 2.0 ** (-8.0 * (h + 1) / HEADS)


def layer_columns():
    at, cols = 0, {}
    for name, n in (("sink", 8), ("lru_w", 8), ("lru_b", 2), ("gate_a_b", 2), ("gate_x_b", 2), ("lam", 2), ("sc_w", 6)):
        cols[name] = at
        at += n
    return cols, at


def second_columns():
    at, cols = 0, {}
    for name, n in (("q_norm", 3), ("kv_norm", 2), ("gla_norm", 1), ("b_decay", 8), ("conv", FC * CONV_COLS)):
        cols[name] = at
        at += n
    return cols, at


def program(nc, a):
    LC, NLP = layer_columns()
    C2, NP2 = second_columns()
    G2 = DEPTH * LAYER_BLOCKS // 4
    NPOS = a["mod_w"].shape[0]
    NBLK = a["weights"].shape[0]
    with ExitStack() as ctx:
        def sb(name, shape, dt=F32):
            return ctx.enter_context(nc.sbuf_tensor(name, shape, dt))

        def region(specs):
            out = []
            with ExitStack() as inner:
                for name, shape, dt in specs:
                    out.append(inner.enter_context(nc.sbuf_tensor(name, shape, dt)))
            return out

        def sem(name):
            return ctx.enter_context(nc.semaphore(name))

        h_hi = sb("h_hi", [P, DC, T], F32R)
        h_lo = sb("h_lo", [P, DC, T], F32R)
        raw = sb("raw", [P, RAW_SLOTS, BLOCK])
        w_hi = sb("w_hi", [P, 2, BLOCK], F32R)
        w_lo = sb("w_lo", [P, 2, BLOCK], F32R)
        mod_raw = sb("mod_raw", [P, 2, MOD_K, MOD_COLS])
        mod_acc = sb("mod_acc", [P, MOD_COLS])
        t_ring = sb("t_ring", [P, 2, T])
        sq = sb("sq", [P, 2, T])
        ssq = sb("ssq", [P, T])
        diag = sb("diag", [P, 4, P])
        act_ring = sb("act_ring", [P, 2, T])
        prod = sb("prod", [P, 2, T])
        ident = sb("ident", [P, P])
        ones = sb("ones", [P, P])
        alibi = sb("alibi", [P, 2 * WINDOW])
        cond = sb("cond", [P, NPOS * 8])
        mod_b = sb("mod_b", [P, NPOS * 4])
        mods = sb("mods", [P, NPOS * 4])
        gains = sb("gains", [P, a["gains"].shape[1]])
        layer_par = sb("layer_par", [P, DEPTH * NLP])
        par = sb("par", [P, NLP])
        gates_all = sb("gates_all", [P, DEPTH * 4 * P])
        gate_w = sb("gate_w", [P, 4, P])
        cond_now = sb("cond_now", [P, 8])
        a_col = sb("a_col", [P, DC])
        shift = sb("shift", [P, DC])
        gate = sb("gate", [P, DC])
        var = sb("var", [P, 4])
        rstd = sb("rstd", [P, 4])
        mhalf = sb("mhalf", [P, 4])
        small = sb("small", [P, 8, 8])
        par2 = sb("par2", [P, NP2])
        cpar = sb("cpar", [P, 8 * CONV_COLS])
        hid_hi, hid_lo, gpad, conv = region([("hid_hi", [P, 8, T], F32R), ("hid_lo", [P, 8, T], F32R), ("gpad", [P, 2, T], F32), ("conv", [P, 2, T], F32)])
        qT, k_dup, v_tok, lx, lg, z, sb_gate, probs, probsT, xc, x = region([
            ("qT", [P, 4, T], F32), ("k_dup", [P, 2, T], F32), ("v_tok", [P, 4, P], F32),
            ("lx", [P, 2, T], F32), ("lg", [P, 2, T], F32), ("z", [P, 2, T], F32),
            ("sb_gate", [P, 2, T], F32), ("probs", [P, 2, 4, 2 * WINDOW], F32),
            ("probsT", [P, 8, P], F32), ("xc", [P, 2, T], F32), ("x", [P, DC, T], F32)])
        kvn_hi, kvn_lo, keys, ch_hi, ch_lo, cx, glow_c, kvf_c = region([
            ("kvn_hi", [P, 2, TK], F32R), ("kvn_lo", [P, 2, TK], F32R), ("keys", [P, 2, TK], F32),
            ("ch_hi", [P, DC, TC], F32R), ("ch_lo", [P, DC, TC], F32R), ("cx", [P, DC, TC], F32),
            ("glow_c", [P, TC], F32), ("kvf_c", [P, 2, TC], F32)])
        _, cx_sq, _, kdT_c, vt_c, s_c, gk_c, gv_c = region([
            ("skip0", [P, 18 * 256], F32), ("cx_sq", [P, DC, TC], F32), ("skip1", [P, 4 * 256], F32),
            ("kdT_c", [P, 2, 2, P], F32), ("vt_c", [P, 2, P], F32), ("s_c", [P, 2, P], F32),
            ("gk_c", [P, GLA_HEADS, TC], F32), ("gv_c", [P, GLA_HEADS, TC], F32)])
        _, qn_hi, qn_lo, vals, mprobs, o_mla = region([
            ("skip2", [P, 18 * 256], F32), ("qn_hi", [P, 3, T], F32R), ("qn_lo", [P, 3, T], F32R),
            ("vals", [P, 6, T], F32), ("mprobs", [P, 4, TK], F32), ("o_mla", [P, 4, T], F32)])
        _, kvf, qf = region([("skip3", [P, 46 * 256], F32), ("kvf", [P, 2, T], F32), ("qf", [P, 3, T], F32)])
        gk, gq, gv, gr, gvt, qe, kn, kdT, states, am, o_sb, y_gla = region([
            ("gk", [P, 2, T], F32), ("gq", [P, 2, T], F32), ("gv", [P, 2, T], F32), ("gr", [P, 2, T], F32),
            ("gvt", [P, 4, P], F32), ("qe", [P, 2, T], F32), ("kn", [P, 2, T], F32), ("kdT", [P, 2, 4, P], F32),
            ("states", [P, 2, 8, P], F32), ("am", [P, 4, P], F32), ("o_sb", [P, T], F32), ("y_gla", [P, 4, T], F32)])
        om_hi, om_lo, yg_hi, yg_lo, merged = region([
            ("om_hi", [P, 4, T], F32R), ("om_lo", [P, 4, T], F32R), ("yg_hi", [P, 4, T], F32R),
            ("yg_lo", [P, 4, T], F32R), ("merged", [P, DC, T], F32)])
        s0 = mod_raw[:, 0, :, :].rearrange("p a (b c) -> p (a b) c", c=P)
        resets = mod_raw[:, 1, :, :]
        rot = sq[:, 0, :]
        krope = mod_acc
        w_decay = gates_all
        masks = gate_w
        x_spill = nc.dram_tensor("x_spill", [P, DC * T], F32, kind="Internal").ap()
        psum = ctx.enter_context(nc.psum_tensor("psum", [P, 8, T], F32))

        raw_landed = [sem(f"raw_landed{i}") for i in range(RAW_SLOTS)]
        hi_ready = sem("hi_ready")
        lo_ready = sem("lo_ready")
        block_done = sem("block_done")
        out_free = [sem(f"out_free{i}") for i in range(2)]
        mod_landed = [sem(f"mod_landed{i}") for i in range(2)]
        mod_used = sem("mod_used")
        macc_ready = sem("macc_ready")
        msum_ready = sem("msum_ready")
        consts_landed = sem("consts_landed")
        consts_ready = sem("consts_ready")
        cond_ready = sem("cond_ready")
        x_ready = sem("x_ready")
        sq_ready = sem("sq_ready")
        sq_used = sem("sq_used")
        ssq_ready = sem("ssq_ready")
        cols_ready = sem("cols_ready")
        var_ready = sem("var_ready")
        rstd_ready = sem("rstd_ready")
        diag_ready = sem("diag_ready")
        rb_ready = sem("rb_ready")
        t_ready = sem("t_ready")
        h_hi_ready = sem("h_hi_ready")
        h_ready = sem("h_ready")
        silu_ready = sem("silu_ready")
        hid_ready = sem("hid_ready")
        q_ready = sem("q_ready")
        k_ready = sem("k_ready")
        v_ready = sem("v_ready")
        vtok_ps = sem("vtok_ps")
        vtok_ready = sem("vtok_ready")
        lru_in = sem("lru_in")
        z_ready = sem("z_ready")
        xc_ready = sem("xc_ready")
        gates_ps = sem("gates_ps")
        gates_ready = sem("gates_ready")
        lam_abs = sem("lam_abs")
        decay_ready = sem("decay_ready")
        m2_ready = sem("m2_ready")
        mult_ready = sem("mult_ready")
        scores_ps = sem("scores_ps")
        s_ready = sem("s_ready")
        p_ready = sem("p_ready")
        pn_ready = sem("pn_ready")
        pT_ps = sem("pT_ps")
        pT_ready = sem("pT_ready")
        o_ps = sem("o_ps")
        y_ready = sem("y_ready")
        par_ready = sem("par_ready")
        stored = sem("stored")
        second_landed = sem("second_landed")
        ctx_landed = sem("ctx_landed")
        ctx_h_ready = sem("ctx_h_ready")
        ctx_out = sem("ctx_out")
        kvf_ready = sem("kvf_ready")
        rg_ready = sem("rg_ready")
        spilled = sem("spilled")
        rot_landed = sem("rot_landed")
        kvn_ready = sem("kvn_ready")
        qn_ready = sem("qn_ready")
        vals_ready = sem("vals_ready")
        krot_ready = sem("krot_ready")
        qh_ready = sem("qh_ready")
        keys_ps = sem("keys_ps")
        keys_ready = sem("keys_ready")
        m_scores = sem("m_scores")
        m_max = sem("m_max")
        m_exp = sem("m_exp")
        m_norm = sem("m_norm")
        m_turn = sem("m_turn")
        m_turned = [sem("m_turned_act"), sem("m_turned_dve")]
        m_pv = sem("m_pv")
        o_mla_ready = sem("o_mla_ready")
        g_in = sem("g_in")
        pre_ps = sem("pre_ps")
        ln_ready = sem("ln_ready")
        cum_ready = sem("cum_ready")
        exp_ready = sem("exp_ready")
        qk_ready = sem("qk_ready")
        turn_ps = sem("turn_ps")
        turn_ready = sem("turn_ready")
        u_ps = [sem("u_ps0"), sem("u_ps1")]
        chain_ready = sem("chain_ready")
        a_ps = sem("a_ps")
        am_ready = sem("am_ready")
        og_ps = sem("og_ps")
        og_ready = sem("og_ready")
        yg_ready = sem("yg_ready")
        branch_ready = sem("branch_ready")
        sig_ready = sem("sig_ready")
        merged_ready = sem("merged_ready")
        merged_split = sem("merged_split")
        x_back = sem("x_back")
        g_copied = sem("g_copied")
        conv_ready = sem("conv_ready")

        block = ctx.enter_context(nc.Block())
        M0, S_BANK, T_BANK, O_BANK = 0, 4, 6, 7

        @block.sync
        def _(sp):
            def load_block(g, k, static=None):
                s = k % RAW_SLOTS
                sp.wait_ge(lo_ready, 4 * g + k + 1)
                sp.dma_start(raw[:, s:s + 1, :], a["weights"][bass.ds(4 * g + k, 1)].rearrange("b p n -> p b n")
                             ).then_inc(raw_landed[s], 16)

            def load_mod(pos):
                for piece in range(MOD_PIECES):
                    sp.wait_ge(mod_used, MOD_PIECES * pos + piece + 1)
                    sp.dma_start(mod_raw[:, piece % 2:piece % 2 + 1, :, :].rearrange("p s k n -> p s (k n)"),
                                 a["mod_w"][bass.ds(pos, 1), piece].rearrange("b p n -> p b n")
                                 ).then_inc(mod_landed[piece % 2], 16)

            def ffn(g, k0, pos=None, skip=0):
                def third(g, k0, pos, n, skip=0):
                    for j in range(n + 4 - skip):
                        load_block(g, k0 + j + 3)
                        if pos is not None and j in (0, 2, 4, 6):
                            load_mod(pos + j // 2)
                with sp.Fori(0, 2) as i:
                    third(g + 3 * i, k0, None if pos is None else pos + 4 * i, 8)
                third(g, k0 + 24, None if pos is None else pos + 8, 6, skip)

            for name, t in (("xT", x), ("cond", cond), ("mod_b", mod_b), ("gains", gains), ("layer_par", layer_par),
                            ("lru_gates", gates_all), ("ident", ident), ("alibi", alibi)):
                dst = t[:, :, :].rearrange("p c n -> p (c n)") if t is x else t[:, :]
                sp.dma_start(dst, a[name]).then_inc(consts_landed, 16)
            sp.wait_ge(consts_ready, 1)
            with sp.Fori(0, 6) as i:
                load_mod(i)
            for k in range(3):
                load_block(0, k)
            with sp.Fori(0, DEPTH) as l:
                g = l * (LAYER_BLOCKS // 4)
                ffn(g, 0, l * LAYER_MODS + 6)
                for j in range(MIX_BLOCKS):
                    load_block(g, FFN_BLOCKS + j + 3)
                ffn(g, FFN_BLOCKS + MIX_BLOCKS, l * LAYER_MODS + 18)
            sp.wait_ge(mod_used, MOD_PIECES * NPOS + 2)
            sp.dma_start(cx[:, :, :].rearrange("p c n -> p (c n)"), a["ctxT"]).then_inc(ctx_landed, 16)
            for name, dst in (("par2", par2[:, :]), ("w_decay", w_decay[0:32, :]), ("masks", masks[:, 0:2, :].rearrange("p a b -> p (a b)")),
                              ("resets", resets.rearrange("p a b -> p (a b)"))):
                sp.dma_start(dst, a[name]).then_inc(second_landed, 16)
            for k in range(FFN_K):
                load_block(G2, k + 3)
            ffn(G2, FFN_K, skip=3)
            for c in range(2):
                sp.wait_ge(x_ready, 8 * 9 + 8 + 4 * c + 4)
                sp.dma_start(a["out"][:, 4 * c * T:4 * (c + 1) * T], x[:, 4 * c:4 * c + 4, :].rearrange("p c n -> p (c n)")).then_inc(stored, 16)
            sp.wait_ge(stored, 32)

        @block.gpsimd
        def _(pool):
            nc.gpsimd.memset(ones[:, :], 1.0)
            nc.gpsimd.memset(mhalf[:, :], -0.5)
            pool.drain().then_inc(consts_ready, 1)

            def split_lo(g, k, inc=1):
                pool.wait_ge(hi_ready, 4 * g + k + 1)
                pool.tensor_tensor(w_lo[:, k % 2, :], raw[:, k % 4, :], w_hi[:, k % 2, :].bitcast(F32),
                                   ALU.subtract).then_inc(lo_ready, 1)

            def rms(n):
                pool.wait_ge(var_ready, n + 1)
                pool.tensor_tensor(rstd[:, :], var[:, :], mhalf[:, :], ALU.pow).then_inc(rstd_ready, 1)

            def splits(g, k0, n):
                for j in range(n):
                    split_lo(g, k0 + j)

            pool.drain().then_inc(lo_ready, RAW_SLOTS)
            splits(0, 0, 2)
            with pool.Fori(0, DEPTH) as l:
                g = l * (LAYER_BLOCKS // 4)
                for n, (k0, blocks) in enumerate(((0, FFN_BLOCKS), (FFN_BLOCKS, MIX_BLOCKS),
                                                  (FFN_BLOCKS + MIX_BLOCKS, FFN_BLOCKS))):
                    rms(3 * l + n)
                    if blocks == FFN_BLOCKS:
                        with pool.Fori(0, 2) as i:
                            splits(g + 3 * i, k0 + 2, 12)
                        splits(g, k0 + 26, 10)
                    else:
                        splits(g, k0 + 2, blocks)
            for r, k, n in ((R_FINAL1, 2, 0), (R_CTX, 2, 4), (R_X1, 6, 2), (R_KVC, 8, 3), (R_KVX, 11, 0), (R_QX, 11, 5)):
                rms(r)
                splits(G2, k, n)
            for h in range(GLA_HEADS):
                splits(G2, 16 + 2 * h, 2)
                rms(R_GLA + h)
            splits(G2, 24, 16)
            rms(R_X2)
            with pool.Fori(0, 2) as i:
                splits(G2 + 3 * i, FFN_K + 2, 12)
            splits(G2, FFN_K + 26, 8)
            rms(R_FINAL2)

        @block.tensor
        def _(pe):
            pe.drain().then_inc(block_done, 2)

            def products(g, k, rhs, ks=range(KC), waits=None, width=T):
                pe.wait_ge(lo_ready, 4 * g + k + 1 + RAW_SLOTS)
                pe.wait_ge(out_free[k % 2], 2 * g + k // 2 + 1)
                rhs_hi, rhs_lo = rhs
                for t in range(2):
                    for c in ks:
                        if waits and t == 0:
                            pe.wait_ge(waits[0], waits[1] + c + 1)
                        wh, wl = (w[:, k % 2, c * 256 + t * P:c * 256 + (t + 1) * P] for w in (w_hi, w_lo))
                        out = psum[:, 2 * (k % 2) + t, 0:width]
                        pe.matmul(out, wh, rhs_hi[:, c, :], start=(c == ks[0]), stop=False)
                        pe.matmul(out, wh, rhs_lo[:, c, :], start=False, stop=False)
                        mm = pe.matmul(out, wl, rhs_hi[:, c, :], start=False, stop=(c == ks[-1]))
                mm.then_inc(block_done, 1)

            def mod_sum(pos):
                pe.wait_ge(macc_ready, pos + 1)
                pe.matmul(psum[:, O_BANK, :], ones[:, :], mod_acc[:, :], start=True, stop=True).then_inc(msum_ready, 1)

            def rms(n, width=T):
                pe.wait_ge(ssq_ready, n + 1)
                for t in range(width // P):
                    mm = pe.matmul(psum[:, S_BANK, t:t + 1], ssq[:, t * P:(t + 1) * P], ones[:, 0:1], start=True, stop=True)
                mm.then_inc(cols_ready, 1)
                pe.wait_ge(diag_ready, n + 1)
                pe.matmul(psum[:, S_BANK + 1, 0:width], ones[:, :], diag[:, :, :].rearrange("p a b -> p (a b)")[:, 0:width],
                          start=True, stop=True).then_inc(rb_ready, 1)

            def ffn(g, k0, n, f, pos, r=None):
                def third(g, k0, h0, pos, count):
                    for j in range(count + 4):
                        if j < count:
                            products(g, k0 + j, (h_hi, h_lo), waits=(h_ready, 8 * n) if j == 0 else None)
                        else:
                            products(g, k0 + j, (hid_hi, hid_lo), ks=range(count), waits=(hid_ready, h0 + 2) if j == count else None)
                        if pos is not None and j in (1, 3, 5, 7):
                            mod_sum(pos + j // 2)
                rms(n if r is None else r)
                with pe.Fori(0, 2) as i:
                    third(g + 3 * i, k0, FC * f + 8 * i, None if pos is None else pos + 4 * i, 8)
                third(g, k0 + 24, FC * f + 16, None if pos is None else pos + 8, 6)

            def mixer(l, g, k0, n):
                rms(n)
                for j in range(3):
                    products(g, k0 + j, (h_hi, h_lo), waits=(h_ready, 8 * n) if j == 0 else None)
                pe.wait_ge(v_ready, l + 1)
                for t in range(4):
                    mm = pe.transpose(psum[:, T_BANK, t * P:(t + 1) * P], prod[:, 0, t * P:(t + 1) * P], ident[:, :])
                mm.then_inc(vtok_ps, 1)
                for j in range(3, MIX_IN_BLOCKS):
                    products(g, k0 + j, (h_hi, h_lo))
                    if j == 5:
                        pe.wait_ge(xc_ready, l + 1)
                        pe.wait_ge(vtok_ready, l + 1)
                        for w in range(2):
                            for t in range(2):
                                mm = pe.matmul(psum[:, S_BANK + 2 * w + t, :], gate_w[:, 2 * w + t, :], xc[:, t, :],
                                               start=True, stop=True)
                        mm.then_inc(gates_ps, 1)
                pe.wait_ge(gates_ready, l + 1)
                pe.wait_ge(q_ready, 4 * l + 4)
                pe.wait_ge(k_ready, l + 1)

                def scores(i):
                    n, kv = i // 2, i % 2
                    if i:
                        pe.wait_ge(s_ready, 8 * l + i)
                    k0, nk = max(n - 1, 0) * P, P * min(n + 1, 2)
                    for hh in range(4):
                        r = 64 * (hh % 2)
                        c0 = (hh // 2) * 2 * WINDOW
                        mm = pe.matmul(psum[:, S_BANK + hh % 2, c0:c0 + nk],
                                       qT[r:r + 64, 2 * kv + hh // 2, n * P:(n + 1) * P],
                                       k_dup[r:r + 64, kv, k0:k0 + nk], start=True, stop=True)
                    mm.then_inc(scores_ps, 1)

                def values(i):
                    n, kv = i // 2, i % 2
                    blocks = min(n + 1, 2)
                    for half in range(2):
                        e = 16 * l + 2 * i + half
                        pe.wait_ge(pn_ready, 8 * l + i + 1)
                        if i or half:
                            pe.wait_ge(pT_ready, e)
                        for u in range(2):
                            for b in range(blocks):
                                mm = pe.transpose(psum[:, T_BANK, (2 * u + b) * P:(2 * u + b + 1) * P],
                                                  probs[:, i % 2, 2 * half + u, b * P:(b + 1) * P], ident[:, :])
                        mm.then_inc(pT_ps, 1)
                    pe.wait_ge(pT_ready, 16 * l + 2 * i + 2)
                    if i:
                        pe.wait_ge(y_ready, 12 * l + 4 + i)
                    for hh in range(4):
                        for b in range(blocks):
                            mm = pe.matmul(psum[64 * (hh % 2):64 * (hh % 2) + 64, O_BANK, (hh // 2) * P:(hh // 2 + 1) * P],
                                           v_tok[:, max(n - 1, 0) + b, 64 * kv:64 * kv + 64], probsT[:, 2 * hh + b, :],
                                           start=(b == 0), stop=(b == blocks - 1))
                    mm.then_inc(o_ps, 1)

                scores(0)
                for i in range(8):
                    if i < 7:
                        scores(i + 1)
                    values(i)
                pe.wait_ge(y_ready, 12 * l + 12)
                for j in range(4):
                    products(g, k0 + MIX_IN_BLOCKS + j, (h_hi, h_lo))

            pe.wait_ge(consts_ready, 1)
            with pe.Fori(0, 6) as i:
                mod_sum(i)
            with pe.Fori(0, DEPTH) as l:
                g = l * (LAYER_BLOCKS // 4)
                ffn(g, 0, 3 * l, 2 * l, LAYER_MODS * l + 6)
                mixer(l, g, FFN_BLOCKS, 3 * l + 1)
                ffn(g, FFN_BLOCKS + MIX_BLOCKS, 3 * l + 2, 2 * l + 1, LAYER_MODS * l + 18)

            ch = (ch_hi, ch_lo)
            hx = (h_hi, h_lo)

            def turn(dst, src, n):
                for t in range(n):
                    mm = pe.transpose(dst[:, t * P:(t + 1) * P], src[:, t * P:(t + 1) * P], ident[:, :])
                return mm

            def gla(u, k_src, v_src, glow, q_src):
                h, width = u % 4, T if q_src else TC
                pairs = width // P
                vt = gvt if q_src else vt_c
                kt = kdT if q_src else kdT_c
                for d in range(2):
                    mm = pe.matmul(psum[:, S_BANK + d, 0:width], w_decay[0:32, (4 * d + h) * P:(4 * d + h + 1) * P],
                                   glow[0:32, 0:width], start=True, stop=True)
                mm.then_inc(pre_ps, 1)
                pe.wait_ge(qk_ready, u + 1)
                for d in range(2):
                    turn(psum[:, T_BANK + d, :], t_ring[:, d, :], pairs)
                turn(psum[:, S_BANK, :], v_src, pairs).then_inc(turn_ps, 1)
                pe.wait_ge(turn_ready, u + 1)
                for d in range(2):
                    for c in range(2 * pairs):
                        r = GLA_CHUNK * (c % 2)
                        mm = pe.matmul(psum[:, S_BANK + 2 * d + c % 2, (c // 2) * P:(c // 2 + 1) * P],
                                       kt[r:r + GLA_CHUNK, d, c // 2, :], vt[r:r + GLA_CHUNK, c // 2, :], start=True, stop=True)
                    mm.then_inc(u_ps[d], 1)
                if not q_src:
                    pe.wait_ge(chain_ready, 2 * u + 2)
                    return
                pe.wait_ge(chain_ready, 2 * u + 1)
                for d in range(2):
                    for p in range(pairs):
                        mm = pe.matmul(psum[:, S_BANK + d, p * P:(p + 1) * P], kn[:, d, p * P:(p + 1) * P],
                                       qe[:, d, p * P:(p + 1) * P], start=True, stop=True)
                mm.then_inc(a_ps, 1)
                pe.wait_ge(chain_ready, 2 * u + 2)
                pe.wait_ge(am_ready, h + 1)
                out = psum[:, T_BANK, :]
                for p in range(pairs):
                    pe.matmul(out[:, p * P:(p + 1) * P], gvt[:, p, :], am[:, p, :], start=(p == 0), stop=False, skip_group_check=True)
                for d in range(2):
                    for c in range(2 * pairs):
                        cs = slice(c * GLA_CHUNK, (c + 1) * GLA_CHUNK)
                        mm = pe.matmul(out[:, cs], states[:, d, c, :], qe[:, d, cs], start=False,
                                       stop=(d == 1), skip_group_check=True)
                mm.then_inc(og_ps, 1)
                rms(R_GLA + h)

            rms(R_FINAL1)
            rms(R_CTX, TC)
            pe.wait_ge(ctx_h_ready, 8)
            products(G2, 0, ch, width=TC)
            products(G2, 1, ch, width=TC)
            products(G2, 2, ch, width=TC)
            products(G2, 3, ch, width=TC)
            rms(R_X1)
            products(G2, 4, ch, width=TC)
            products(G2, 5, ch, width=TC)
            rms(R_KVC, TC)
            pe.wait_ge(second_landed, 64)
            for u in range(4):
                if u < 3:
                    products(G2, X_K + u, hx, waits=(h_ready, 48) if u == 0 else None)
                if u == 0:
                    pe.wait_ge(ctx_out, 6)
                    pe.wait_ge(kvn_ready, 1)
                gla(u, gk_c[:, u, :], gv_c[:, u, :], glow_c, False)
            rms(R_KVX)
            rms(R_QX)
            pe.wait_ge(kvn_ready, 2)
            pe.wait_ge(qn_ready, 1)
            pe.wait_ge(lo_ready, 4 * G2 + V_K + 1 + RAW_SLOTS)
            for k in (V_K, V_K + 1):
                pe.wait_ge(out_free[k % 2], 2 * G2 + k // 2 + 1)
            for t in range(TK // P):
                for c in range(KV_LORA_C):
                    wh, wl = (w[:, V_K % 2, c * T:(c + 1) * T] for w in (w_hi, w_lo))
                    kh, kl = (k[:, c, t * P:(t + 1) * P] for k in (kvn_hi, kvn_lo))
                    pe.matmul(psum[:, t, :], kh, wh, start=(c == 0), stop=False)
                    pe.matmul(psum[:, t, :], kh, wl, start=False, stop=False)
                    mm = pe.matmul(psum[:, t, :], kl, wh, start=False, stop=(c == 1))
            mm.then_inc(block_done, 1)
            pe.wait_ge(vals_ready, 1)

            def mla_pair(p):
                k = PAIR_K + p
                if p:
                    pe.wait_ge(m_exp, 8 * p)
                    for s in range(2):
                        pe.wait_ge(m_turned[s], 3 * (2 * p - 1))
                pe.wait_ge(lo_ready, 4 * G2 + k + 1 + RAW_SLOTS)
                for c in range(KV_LORA_C):
                    wh, wl = (w[:, k % 2, (3 + c) * 256:(3 + c) * 256 + P] for w in (w_hi, w_lo))
                    for bank, lo, hi in ((S_BANK, 0, T), (S_BANK + 1, T, TK)):
                        out = psum[:, bank, 0:hi - lo]
                        pe.matmul(out, wh, kvn_hi[:, c, lo:hi], start=(c == 0), stop=False)
                        pe.matmul(out, wh, kvn_lo[:, c, lo:hi], start=False, stop=False)
                        mm = pe.matmul(out, wl, kvn_hi[:, c, lo:hi], start=False, stop=(c == 1))
                mm.then_inc(keys_ps, 1)
                products(G2, k, (qn_hi, qn_lo), ks=range(Q_LORA_C))

            def mla_scores(h, qb):
                u = 4 * h + qb
                if u >= 2:
                    pe.wait_ge(m_exp, u - 1)
                for bank, lo, hi in ((0, 0, T), (1, T, TK)):
                    mm = pe.matmul(psum[:, 2 * (u % 2) + bank, 0:hi - lo], act_ring[0:96, h % 2, qb * P:(qb + 1) * P],
                                   keys[0:96, h % 2, lo:hi], start=True, stop=True)
                mm.then_inc(m_scores, 1)

            def mla_values(h):
                pe.wait_ge(m_norm, h + 1)

                def turn_keys(kt):
                    n = 3 * h + kt // 2
                    if n:
                        pe.wait_ge(m_turned[kt % 2], n)
                    for qb in range(4):
                        mm = pe.transpose(psum[:, S_BANK + kt % 2, qb * P:(qb + 1) * P], mprobs[:, qb, kt * P:(kt + 1) * P], ident[:, :])
                    mm.then_inc(m_turn, 1)

                turn_keys(0)
                turn_keys(1)
                r = 64 * (h % 2)
                for kt in range(6):
                    pe.wait_ge(m_turned[kt % 2], 3 * h + kt // 2 + 1)
                    if kt == 0 and h % 2 == 0 and h >= 4:
                        pe.wait_ge(o_mla_ready, h // 2 - 1)
                    pe.matmul(psum[r:r + 64, T_BANK + (h // 2) % 2, :], vals[:, kt, 64 * h:64 * h + 64], prod[:, kt % 2, :],
                              start=(kt == 0), stop=(kt == 5)).then_inc(m_pv, 1)
                    if kt < 4:
                        turn_keys(kt + 2)

            for h in range(MLA_HEADS):
                if h % 2 == 0:
                    mla_pair(h // 2)
                    pe.wait_ge(keys_ready, h // 2 + 1)
                    pe.wait_ge(qh_ready, h // 2 + 1)
                    pe.wait_ge(krot_ready, 1)
                mla_scores(h, 0)
                mla_scores(h, 1)
                if h:
                    mla_values(h - 1)
                mla_scores(h, 2)
                mla_scores(h, 3)
            mla_values(MLA_HEADS - 1)

            pe.wait_ge(m_exp, 32)
            for h in range(GLA_HEADS):
                for hh in ([0, 1] if h == 0 else [h + 1]):
                    if hh < GLA_HEADS:
                        for j in range(2):
                            products(G2, GLA_K + 2 * hh + j, hx)
                pe.wait_ge(g_in, h + 1)
                if h == 0:
                    pe.wait_ge(o_mla_ready, 4)
                else:
                    pe.wait_ge(yg_ready, h)
                gla(4 + h, gk[:, h % 2, :], gv[:, h % 2, :], krope, True)

            for mp in range(4):
                for j in range(2):
                    products(G2, MERGE_K + 3 * mp + j, hx)
                k = MERGE_K + 3 * mp + 2
                pe.wait_ge(lo_ready, 4 * G2 + k + 1 + RAW_SLOTS)
                pe.wait_ge(out_free[k % 2], 2 * G2 + k // 2 + 1)
                pe.wait_ge(branch_ready, 1)
                pe.wait_ge(yg_ready, 4)
                if mp:
                    pe.wait_ge(merged_ready, 2 * mp)
                for j in range(2):
                    for which, (bh, bl) in enumerate(((om_hi, om_lo), (yg_hi, yg_lo))):
                        out = psum[:, (2 * (k % 2) if j == 0 else S_BANK) + which, :]
                        for c in range(4):
                            at = ((j * 2 + which) * 4 + c) * P
                            wh, wl = (w[:, k % 2, at:at + P] for w in (w_hi, w_lo))
                            pe.matmul(out, wh, bh[:, c, :], start=(c == 0), stop=False)
                            pe.matmul(out, wh, bl[:, c, :], start=False, stop=False)
                            mm = pe.matmul(out, wl, bh[:, c, :], start=False, stop=(c == 3))
                mm.then_inc(block_done, 1)
            for j in range(4):
                products(G2, OUT_K + j, hx, waits=(merged_split, 0) if j == 0 else None)
            ffn(G2, FFN_K, 7, 4, None, R_X2)
            rms(R_FINAL2)

        @block.scalar
        def _(act):
            def split_hi(g, k):
                act.wait_ge(raw_landed[k % 4], 16 * g + 16 * (k // 4 + 1))
                act.wait_ge(block_done, 4 * g + k + 1)
                act.copy(w_hi[:, k % 2, :], raw[:, k % 4, :]).then_inc(hi_ready, 1)

            def squares(n, q):
                act.wait_ge(sq_used, 4 * n + q + 1)
                for t in range(2):
                    act.wait_ge(x_ready, 8 * n + 2 * q + t + 1)
                    act.activation(sq[:, t, :], x[:, 2 * q + t, :], ACT.Square).then_inc(sq_ready, 1)

            def norm(n):
                for c in range(DC):
                    act.wait_ge(t_ready, 8 * n + c + 1)
                    act.activation(h_hi[:, c, :], t_ring[:, c % 2, :], ACT.Identity, bias=shift[:, c:c + 1]
                                   ).then_inc(h_hi_ready, 1)

            def ffn(g, k0, n, f):
                def third(g, k0, h0, count, last):
                    for j in range(count + 4):
                        k = k0 + j
                        if j < count:
                            act.wait_ge(block_done, 4 * g + k + 3)
                            act.wait_ge(hid_ready, h0 + j + 1)
                            act.activation(act_ring[:, j % 2, :], psum[:, 2 * (k % 2), :], ACT.Silu).then_inc(silu_ready, 1)
                        elif last:
                            squares(n + 1, j - count)
                        split_hi(g, k + 2)
                norm(n)
                with act.Fori(0, 2) as i:
                    third(g + 3 * i, k0, FC * f + 8 * i, 8, False)
                third(g, k0 + 24, FC * f + 16, 6, True)

            def copies(g, k, out, done, func=ACT.Copy, free=True):
                act.wait_ge(block_done, 4 * g + k + 3)
                for t in range(2):
                    o = act.activation(out[:, t, :], psum[:, 2 * (k % 2) + t, :], func)
                    o.then_inc(done, 1)
                act.drain().then_inc(out_free[k % 2], 1)

            def mixer(l, g, k0, n):
                norm(n)
                for j in range(MIX_IN_BLOCKS):
                    k = k0 + j
                    if j < 2:
                        copies(g, k, qT[:, 2 * j:2 * j + 2, :], q_ready)
                    elif j == 2:
                        act.wait_ge(k_ready, l + 1)
                        act.copy(prod[:, 0, :], psum[:, 2 * (k % 2) + 1, :]).then_inc(v_ready, 1)
                        act.drain().then_inc(out_free[k % 2], 1)
                    elif j == 3:
                        copies(g, k, lx, lru_in)
                        act.wait_ge(vtok_ps, l + 1)
                        act.copy(v_tok[:, :, :].rearrange("p a b -> p (a b)"), psum[:, T_BANK, :]).then_inc(vtok_ready, 1)
                    elif j == 4:
                        copies(g, k, z, lru_in)
                        lam = par[:, LC["lam"]:LC["lam"] + 2]
                        act.wait_ge(par_ready, l + 1)
                        act.activation(small[:, 6, 0:2], lam, ACT.Abs)
                        act.drain()
                        act.activation(small[:, 6, 2:4], small[:, 6, 0:2], ACT.Exp, scale=-1.0)
                        act.drain()
                        act.activation(small[:, 6, 4:6], small[:, 6, 2:4], ACT.Ln, bias=1.0).then_inc(lam_abs, 1)
                    elif j == 6:
                        copies(g, k, sb_gate, lru_in)
                    elif j == 7:
                        copies(g, k, lg, lru_in, ACT.Gelu_apprx_tanh)
                    split_hi(g, k + 2)
                act.wait_ge(gates_ps, l + 1)
                for w, name, out in ((0, "gate_a_b", act_ring), (1, "gate_x_b", prod)):
                    for t in range(2):
                        o = act.activation(out[:, t, :], psum[:, S_BANK + 2 * w + t, :], ACT.Sigmoid,
                                           bias=par[:, LC[name] + t:LC[name] + t + 1])
                act.drain().then_inc(gates_ready, 1)
                act.wait_ge(m2_ready, 3 * l + 1)
                for t in range(2):
                    act.activation(lx[:, t, :], act_ring[:, t, :], ACT.Exp, scale=small[:, 7, t:t + 1])
                    o = act.activation(t_ring[:, t, :], act_ring[:, t, :], ACT.Tanh, scale=small[:, 7, t:t + 1])
                act.drain().then_inc(decay_ready, 1)
                act.wait_ge(m2_ready, 3 * l + 2)
                act.activation(t_ring[:, :, :], t_ring[:, :, :], ACT.Sqrt, scale=-1.0).then_inc(mult_ready, 1)

                def expo(i):
                    nk = P * min(i // 2 + 1, 2)
                    act.wait_ge(s_ready, 8 * l + i + 1)
                    for hh in range(4):
                        act.activation(probs[:, i % 2, hh, 0:nk], probs[:, i % 2, hh, 0:nk], ACT.Exp,
                                       bias=small[:, i % 2, hh:hh + 1], scale=0.125,
                                       accum_out=small[:, 2 + i % 2, hh:hh + 1])
                    act.activation(small[:, 2 + i % 2, 4:8], small[:, i % 2, 4:8], ACT.Exp)
                    act.drain().then_inc(p_ready, 1)

                def turned(i):
                    blocks = min(i // 2 + 1, 2)
                    for half in range(2):
                        act.wait_ge(pT_ps, 16 * l + 2 * i + half + 1)
                        if half == 0 and i:
                            act.wait_ge(o_ps, 8 * l + i)
                        pt = probsT[:, 4 * half:4 * half + 4, :].rearrange("p (u b) q -> p u b q", b=2)
                        ps = psum[:, T_BANK, :].rearrange("p (u b q) -> p u b q", u=2, b=2)
                        act.copy(pt[:, :, 0:blocks, :], ps[:, :, 0:blocks, :]).then_inc(pT_ready, 1)

                expo(0)
                for i in range(8):
                    if i < 7:
                        expo(i + 1)
                    turned(i)
                for j in range(4):
                    squares(n + 1, j)
                    split_hi(g, k0 + MIX_IN_BLOCKS + j + 2)

            def evac(k, outs, done):
                act.wait_ge(block_done, 4 * G2 + k + 3)
                for t, (dst, func) in enumerate(outs):
                    w = dst.shape[-1]
                    act.activation(dst, psum[:, 2 * (k % 2) + t, 0:w], func)
                act.drain().then_inc(out_free[k % 2], 1)
                if done is not None:
                    act.drain().then_inc(done, 1)
                split_hi(G2, k + 2)

            def gla_act(u, width):
                h, pairs, full = u % 4, width // P, width == T
                b = lambda d: par2[:, C2["b_decay"] + 4 * d + h:C2["b_decay"] + 4 * d + h + 1]
                act.wait_ge(pre_ps, u + 1)
                ring = act_ring[:, :, 0:width]
                for d in range(2):
                    act.activation(act_ring[:, d, 0:width], psum[:, S_BANK + d, 0:width], ACT.Abs, bias=b(d))
                act.drain()
                act.activation(ring, ring, ACT.Exp, scale=-1.0)
                act.drain()
                act.activation(ring, ring, ACT.Ln, bias=1.0).then_inc(ln_ready, 1)
                act.wait_ge(cum_ready, u + 1)
                act.activation(t_ring[:, :, 0:width], t_ring[:, :, 0:width], ACT.Exp, scale=1.0 / GATE_NORM)
                if full:
                    act.activation(kn[:, :, :], ring, ACT.Exp, scale=-1.0 / GATE_NORM)
                act.activation(prod[:, :, 0:width], ring, ACT.Exp, scale=1.0 / GATE_NORM)
                act.drain().then_inc(exp_ready, 1)
                act.wait_ge(turn_ps, u + 1)
                kt, vt = (kdT, gvt) if full else (kdT_c, vt_c)
                for d in range(2):
                    act.copy(kt[:, d, :, :].rearrange("p a b -> p (a b)"), psum[:, T_BANK + d, 0:width])
                act.copy(vt[:, :, :].rearrange("p a b -> p (a b)"), psum[:, S_BANK, 0:width])
                act.drain().then_inc(turn_ready, 1)
                if full:
                    act.wait_ge(og_ps, h + 1)
                    act.activation(ssq[:, :], psum[:, T_BANK, :], ACT.Square)
                    act.copy(o_sb[:, :], psum[:, T_BANK, :])
                    act.drain().then_inc(og_ready, 1)
                    act.drain().then_inc(ssq_ready, 1)

            def mla_act():
                act.wait_ge(block_done, 4 * G2 + V_K + 3)
                for t in range(6):
                    act.copy(vals[:, t, :], psum[:, t, :])
                act.drain().then_inc(out_free[V_K % 2], 1)
                act.drain().then_inc(vals_ready, 1)
                split_hi(G2, V_K + 2)

                def take_turned(h, kt):
                    act.wait_ge(m_turn, 6 * h + kt + 1)
                    if kt >= 2:
                        act.wait_ge(m_pv, 6 * h + kt - 1)
                    act.copy(prod[:, kt % 2, :], psum[:, S_BANK + kt % 2, :]).then_inc(m_turned[0], 1)

                def take_out(p):
                    act.wait_ge(m_pv, 12 * p + 12)
                    act.copy(o_mla[:, p, :], psum[:, T_BANK + p % 2, :]).then_inc(o_mla_ready, 1)

                for h in range(MLA_HEADS):
                    if h % 2 == 0:
                        p = h // 2
                        act.wait_ge(keys_ps, p + 1)
                        for e in range(2):
                            act.copy(keys[0:64, e, 0:T], psum[64 * e:64 * e + 64, S_BANK, :])
                            act.copy(keys[0:64, e, T:TK], psum[64 * e:64 * e + 64, S_BANK + 1, 0:TC])
                        act.drain().then_inc(keys_ready, 1)
                        act.wait_ge(qh_ready, p + 1)
                        split_hi(G2, PAIR_K + p + 2)
                    if h:
                        for kt in (0, 2, 4):
                            take_turned(h - 1, kt)
                        if h % 2 == 0:
                            take_out(h // 2 - 1)
                        act.wait_ge(m_turn, 6 * h)
                    for qb in range(4):
                        act.wait_ge(m_max, 4 * h + qb + 1)
                        s = 2 * (qb % 2)
                        act.activation(mprobs[:, qb, :], psum[:, s:s + 2, :].rearrange("p a b -> p (a b)")[:, 0:TK], ACT.Exp,
                                       bias=small[:, 0, qb:qb + 1], scale=MLA_SCALE, accum_out=small[:, 1, qb:qb + 1]
                                       )
                        act.drain().then_inc(m_exp, 1)
                for kt in (0, 2, 4):
                    take_turned(MLA_HEADS - 1, kt)
                take_out(3)

            def second():
                cpy = ACT.Copy
                for q in range(4):
                    squares(7, q)
                evac(0, [(kvf_c[:, 0, :], cpy), (kvf_c[:, 1, :], cpy)], ctx_out)
                evac(1, [(gk_c[:, 0, :], cpy), (gk_c[:, 1, :], cpy)], ctx_out)
                evac(2, [(gk_c[:, 2, :], cpy), (gk_c[:, 3, :], cpy)], ctx_out)
                evac(3, [(gv_c[:, 0, :], cpy), (gv_c[:, 1, :], cpy)], ctx_out)
                norm(6)
                act.dma_start(x_spill, x[:, :, :].rearrange("p c n -> p (c n)")).then_inc(spilled, 16)
                act.dma_start(rot, a["rot"]).then_inc(rot_landed, 16)
                evac(4, [(gv_c[:, 2, :], cpy), (gv_c[:, 3, :], cpy)], ctx_out)
                evac(5, [(glow_c[:, :], cpy)], None)
                for e in range(2):
                    act.copy(keys[64:96, e, T:TK], glow_c[64:96, :])
                act.drain().then_inc(ctx_out, 1)
                act.wait_ge(spilled, 16)
                act.wait_ge(second_landed, 64)
                evac(6, [(kvf[:, 0, :], cpy), (kvf[:, 1, :], cpy)], kvf_ready)
                gla_act(0, TC)
                evac(7, [(krope[:, :], cpy), (qf[:, 0, :], cpy)], rg_ready)
                gla_act(1, TC)
                evac(8, [(qf[:, 1, :], cpy), (qf[:, 2, :], cpy)], kvf_ready)
                gla_act(2, TC)
                gla_act(3, TC)
                mla_act()
                for h in range(GLA_HEADS):
                    for hh in ([0, 1] if h == 0 else [h + 1]):
                        if hh < GLA_HEADS:
                            if hh >= 2:
                                act.wait_ge(yg_ready, hh - 1)
                            s = hh % 2
                            evac(GLA_K + 2 * hh, [(gk[:, s, :], cpy), (gq[:, s, :], cpy)], None)
                            evac(GLA_K + 2 * hh + 1, [(gv[:, s, :], cpy), (gr[:, s, :], ACT.Silu)], g_in)
                    gla_act(4 + h, T)
                for mp in range(4):
                    if mp:
                        act.wait_ge(merged_ready, 2 * mp)
                    else:
                        act.wait_ge(yg_ready, 4)
                    for j, dst in enumerate((act_ring, prod)):
                        evac(MERGE_K + 3 * mp + j, [(dst[:, 0, :], ACT.Sigmoid), (dst[:, 1, :], ACT.Sigmoid)], sig_ready)
                    split_hi(G2, MERGE_K + 3 * mp + 4)
                act.wait_ge(merged_split, 8)
                act.dma_start(x[:, :, :].rearrange("p c n -> p (c n)"), x_spill).then_inc(x_back, 16)
                for j in range(4):
                    squares(8, j)
                    split_hi(G2, OUT_K + j + 2)
                norm(7)

                def third(g, k0, c0, count, last):
                    for j in range(count + 4):
                        k = k0 + j
                        if j < count:
                            act.wait_ge(block_done, 4 * g + k + 3)
                            act.wait_ge(conv_ready, c0 + j + 1)
                            act.copy(gpad[:, j % 2, :], psum[:, 2 * (k % 2), :]).then_inc(g_copied, 1)
                        elif last:
                            squares(9, j - count)
                        if not last or j < count + 2:
                            split_hi(g, k + 2)
                        if j < count:
                            act.wait_ge(conv_ready, c0 + j + 3)
                            act.wait_ge(hid_ready, FC * 4 + c0 + j + 1)
                            act.activation(act_ring[:, j % 2, :], conv[:, j % 2, :], ACT.Gelu,
                                           bias=cpar[:, CONV_COLS * j + 9:CONV_COLS * j + 10]).then_inc(silu_ready, 1)
                with act.Fori(0, 2) as i:
                    third(G2 + 3 * i, FFN_K, 8 * i, 8, False)
                third(G2, FFN_K + 24, 16, 6, True)

            act.wait_ge(cond_ready, 1)
            act.activation(cond[:, :], cond[:, :], ACT.Silu).then_inc(cond_ready, 1)
            for q in range(4):
                squares(0, q)
            for k in range(2):
                split_hi(0, k)
            with act.Fori(0, DEPTH) as l:
                g = l * (LAYER_BLOCKS // 4)
                ffn(g, 0, 3 * l, 2 * l)
                mixer(l, g, FFN_BLOCKS, 3 * l + 1)
                ffn(g, FFN_BLOCKS + MIX_BLOCKS, 3 * l + 2, 2 * l + 1)
            second()

        @block.vector
        def _(dve):
            def mod_partial(pos):
                dve.tensor_copy(cond_now[:, :], cond[:, bass.ds(8 * pos, 8)])
                for piece in range(MOD_PIECES):
                    for u in range(MOD_K):
                        k = MOD_K * piece + u
                        dve.drain()
                        if u == 0:
                            dve.wait_ge(mod_landed[piece % 2], 32 * pos + 16 * (piece // 2 + 1))
                        w = mod_raw[:, piece % 2, u, :]
                        if k == 0:
                            o = dve.tensor_scalar(mod_acc[:, :], w, cond_now[:, 0:1], None, ALU.mult)
                        else:
                            o = dve.scalar_tensor_tensor(mod_acc[:, :], w, cond_now[:, k:k + 1], mod_acc[:, :], ALU.mult, ALU.add)
                    if piece < MOD_PIECES - 1:
                        o.then_inc(mod_used, 1)
                o.then_inc(mod_used, 1)
                dve.drain().then_inc(macc_ready, 1)

            def mod_take(pos):
                dve.wait_ge(msum_ready, pos + 1)
                for t in range(4):
                    dve.tensor_tensor_reduce(mod_acc[:, t * P:(t + 1) * P], psum[:, O_BANK, t * P:(t + 1) * P], ident[:, :],
                                             1.0, 0.0, ALU.mult, ALU.add, cond_now[:, t:t + 1])
                dve.drain()
                dve.tensor_tensor(mods[:, bass.ds(4 * pos, 4)], cond_now[:, 0:4], mod_b[:, bass.ds(4 * pos, 4)], ALU.add)
                dve.drain()

            def add_squares(n, q):
                dve.wait_ge(sq_ready, 8 * n + 2 * q + 2)
                if q == 0:
                    dve.tensor_tensor(ssq[:, :], sq[:, 0, :], sq[:, 1, :], ALU.add)
                else:
                    dve.tensor_tensor(ssq[:, :], ssq[:, :], sq[:, 0, :], ALU.add)
                    dve.drain()
                    dve.tensor_tensor(ssq[:, :], ssq[:, :], sq[:, 1, :], ALU.add)
                o = dve.drain().then_inc(sq_used, 1)
                if q == 3:
                    dve.drain().then_inc(ssq_ready, 1)

            def rms(n, width=T, dim=D):
                tiles = width // P
                dve.wait_ge(cols_ready, n + 1)
                dve.tensor_scalar(var[:, 0:tiles], psum[:, S_BANK, 0:tiles], 1.0 / dim, EPS, ALU.mult, ALU.add).then_inc(var_ready, 1)
                dve.wait_ge(rstd_ready, n + 1)
                for t in range(tiles):
                    dve.tensor_scalar(diag[:, t, :], ident[:, :], rstd[:, t:t + 1], None, ALU.mult)
                dve.drain().then_inc(diag_ready, 1)
                dve.wait_ge(rb_ready, n + 1)

            def norm(n, at, gain, half, r=None, cols=None):
                at_shift, at_scale, at_gate = cols or (at, at + 8, at + 16)
                dve.tensor_copy(shift[:, :], mods[:, bass.ds(at_shift, 8)])
                dve.tensor_copy(gate[:, :], mods[:, bass.ds(at_gate, 8)])
                dve.tensor_scalar(a_col[:, :], mods[:, bass.ds(at_scale, 8)], 1.0, None, ALU.add)
                dve.drain()
                dve.tensor_tensor(a_col[:, :], a_col[:, :], gains[:, bass.ds(gain, 8)], ALU.mult)
                if half:
                    dve.tensor_scalar(gate[:, :], gate[:, :], 0.5, None, ALU.mult)
                rms(n if r is None else r)

                def lo(c):
                    dve.wait_ge(h_hi_ready, 8 * n + c + 1)
                    dve.scalar_tensor_tensor(h_lo[:, c, :], t_ring[:, c % 2, :], shift[:, c:c + 1], h_hi[:, c, :].bitcast(F32),
                                             ALU.add, ALU.subtract).then_inc(h_ready, 1)
                for c in range(DC):
                    dve.scalar_tensor_tensor(t_ring[:, c % 2, :], x[:, c, :], a_col[:, c:c + 1], psum[:, S_BANK + 1, :],
                                             ALU.mult, ALU.mult).then_inc(t_ready, 1)
                    if c:
                        lo(c - 1)
                    dve.drain()
                lo(DC - 1)

            def add_to_x(g, k, q, n=None):
                dve.drain()
                dve.wait_ge(block_done, 4 * g + k + 3)
                for t in range(2):
                    m = 2 * q + t
                    o = dve.scalar_tensor_tensor(x[:, m, :], psum[:, 2 * (k % 2) + t, :], gate[:, m:m + 1], x[:, m, :],
                                                 ALU.mult, ALU.add)
                    if n is not None:
                        o.then_inc(x_ready, 1)
                dve.drain().then_inc(out_free[k % 2], 1)
                if n is not None:
                    add_squares(n, q)

            def ffn(g, k0, n, f, pos):
                def third(g, k0, h0, pos, count, last):
                    for j in range(count + 4):
                        k = k0 + j
                        if j < count:
                            dve.wait_ge(silu_ready, h0 + j + 1)
                            dve.tensor_tensor(prod[:, j % 2, :], act_ring[:, j % 2, :], psum[:, 2 * (k % 2) + 1, :],
                                              ALU.mult).then_inc(out_free[k % 2], 1)
                            dve.drain()
                            dve.tensor_copy(hid_hi[:, j, :], prod[:, j % 2, :])
                            dve.drain()
                            dve.tensor_tensor(hid_lo[:, j, :], prod[:, j % 2, :], hid_hi[:, j, :].bitcast(F32),
                                              ALU.subtract).then_inc(hid_ready, 1)
                        else:
                            add_to_x(g, k, j - count, n + 1 if last else None)
                        if j in (1, 3, 5, 7):
                            mod_take(pos + j // 2)
                        if j in (0, 2, 4, 6):
                            mod_partial(pos + j // 2)
                with dve.Fori(0, 2) as i:
                    third(g + 3 * i, k0, FC * f + 8 * i, pos + 4 * i, 8, False)
                third(g, k0 + 24, FC * f + 16, pos + 8, 6, True)

            def split_y(c, src, done):
                dve.tensor_copy(h_hi[:, c, :], src)
                dve.drain()
                dve.tensor_tensor(h_lo[:, c, :], src, h_hi[:, c, :].bitcast(F32), ALU.subtract).then_inc(done, 1)

            def mixer(l, g, k0, n):
                kv, kx = k0 + 2, k0 + 5
                pcol = lambda name, j: par[:, LC[name] + j:LC[name] + j + 1]
                dve.wait_ge(block_done, 4 * g + kv + 3)
                ps = psum[:, 2 * (kv % 2), :]
                for e in range(2):
                    for r in range(2):
                        dve.tensor_copy(k_dup[64 * r:64 * r + 64, e, :], ps[64 * e:64 * e + 64, :])
                dve.drain().then_inc(k_ready, 1)
                dve.wait_ge(lru_in, 8 * l + 2)
                for t in range(2):
                    dve.tensor_scalar(xc[:, t, :], lx[:, t, :], pcol("lru_w", 3 * 2 + t), pcol("lru_b", t), ALU.mult, ALU.add)
                for s in range(1, 4):
                    dve.drain()
                    for t in range(2):
                        dve.scalar_tensor_tensor(xc[:, t, s:T], lx[:, t, 0:T - s], pcol("lru_w", (3 - s) * 2 + t), xc[:, t, s:T],
                                                 ALU.mult, ALU.add)
                dve.drain().then_inc(xc_ready, 1)
                dve.wait_ge(lam_abs, l + 1)
                lam = par[:, LC["lam"]:LC["lam"] + 2]
                dve.tensor_scalar(small[:, 7, 2:4], lam, -1.0, 0.0, ALU.mult, ALU.max)
                dve.drain()
                dve.tensor_tensor(small[:, 7, 4:6], small[:, 7, 2:4], small[:, 6, 4:6], ALU.add)
                dve.drain()
                dve.tensor_scalar(small[:, 7, 0:2], small[:, 7, 4:6], -8.0, None, ALU.mult)
                dve.drain().then_inc(m2_ready, 1)
                dve.wait_ge(lru_in, 8 * l + 4)
                dve.wait_ge(block_done, 4 * g + kx + 3)
                for t in range(2):
                    dve.tensor_tensor(z[:, t, :], z[:, t, :], psum[:, 2 * (kx % 2) + t, :], ALU.mult)
                dve.drain().then_inc(out_free[kx % 2], 1)
                for t in range(2):
                    dve.tensor_scalar(sq[:, t, :], z[:, t, :], pcol("sc_w", 2 * 2 + t), None, ALU.mult)
                for s in range(1, 3):
                    dve.drain()
                    for t in range(2):
                        dve.scalar_tensor_tensor(sq[:, t, s:T], z[:, t, 0:T - s], pcol("sc_w", (2 - s) * 2 + t), sq[:, t, s:T],
                                                 ALU.mult, ALU.add)
                dve.drain()
                dve.wait_ge(lru_in, 8 * l + 6)
                dve.tensor_tensor(z[:, :, :], sq[:, :, :], sb_gate[:, :, :], ALU.mult)
                dve.drain()
                dve.wait_ge(block_done, 4 * g + k0 + 7 + 3)
                for t in range(2):
                    split_y(6 + t, z[:, t, :], y_ready)
                dve.wait_ge(decay_ready, l + 1)
                dve.tensor_tensor(sq[:, :, :], lx[:, :, :], lx[:, :, :], ALU.mult)
                dve.drain()
                dve.scalar_tensor_tensor(t_ring[:, :, :], sq[:, :, :], 1.0, t_ring[:, :, :], ALU.add, ALU.mult)
                dve.drain().then_inc(m2_ready, 1)
                dve.tensor_tensor(prod[:, :, :], prod[:, :, :], xc[:, :, :], ALU.mult)
                dve.wait_ge(mult_ready, l + 1)
                dve.memset(t_ring[:, :, 0:1], 1.0)
                dve.drain()
                dve.tensor_tensor(prod[:, :, :], prod[:, :, :], t_ring[:, :, :], ALU.mult)
                dve.drain()
                for t in range(2):
                    dve.tensor_tensor_scan(sq[:, t, :], lx[:, t, :], prod[:, t, :], 0.0, ALU.mult, ALU.add)
                dve.drain()
                dve.wait_ge(lru_in, 8 * l + 8)
                dve.tensor_tensor(lg[:, :, :], lg[:, :, :], sq[:, :, :], ALU.mult)
                dve.drain()
                for t in range(2):
                    split_y(4 + t, lg[:, t, :], y_ready)
                dve.drain().then_inc(m2_ready, 1)

                def bias_max(i):
                    n, kv = i // 2, i % 2
                    nk = P * min(n + 1, 2)
                    dve.wait_ge(scores_ps, 8 * l + i + 1)
                    if i >= 2:
                        dve.wait_ge(pT_ps, 16 * l + 2 * (i - 2) + 2)
                    for hh in range(4):
                        c0 = (hh // 2) * 2 * WINDOW
                        dve.scalar_tensor_tensor(probs[:, i % 2, hh, 0:nk], alibi[:, 2 * WINDOW - nk:], -8.0 * alibi_slope(4 * kv + hh),
                                                 psum[:, S_BANK + hh % 2, c0:c0 + nk], ALU.mult, ALU.add)
                    dve.drain()
                    mx, sink = small[:, 4, 0:4], par[:, LC["sink"] + 4 * kv:LC["sink"] + 4 * kv + 4]
                    dve.tensor_reduce(mx, probs[:, i % 2, :, 0:nk], AX.X, ALU.max)
                    dve.drain()
                    dve.scalar_tensor_tensor(small[:, 4, 4:8], mx, 0.125, sink, ALU.mult, ALU.max)
                    dve.drain()
                    dve.tensor_scalar(small[:, i % 2, 0:4], small[:, 4, 4:8], -1.0, None, ALU.mult)
                    dve.tensor_tensor(small[:, i % 2, 4:8], sink, small[:, 4, 4:8], ALU.subtract)
                    dve.drain().then_inc(s_ready, 1)

                def normalise(i):
                    nk = P * min(i // 2 + 1, 2)
                    dve.wait_ge(p_ready, 8 * l + i + 1)
                    dve.tensor_tensor(small[:, 5, 0:4], small[:, 2 + i % 2, 0:4], small[:, 2 + i % 2, 4:8], ALU.add)
                    dve.drain()
                    dve.reciprocal(small[:, 5, 4:8], small[:, 5, 0:4])
                    dve.drain()
                    for hh in range(4):
                        dve.tensor_scalar(probs[:, i % 2, hh, 0:nk], probs[:, i % 2, hh, 0:nk], small[:, 5, 4 + hh:5 + hh],
                                          None, ALU.mult)
                    dve.drain().then_inc(pn_ready, 1)

                def take_out(i):
                    n, kv = i // 2, i % 2
                    dve.wait_ge(o_ps, 8 * l + i + 1)
                    o = psum[:, O_BANK, 0:2 * P].rearrange("p (c q) -> p c q", c=2)
                    hi, lo = (t[:, 2 * kv:2 * kv + 2, n * P:(n + 1) * P] for t in (h_hi, h_lo))
                    dve.tensor_copy(hi, o)
                    dve.drain()
                    dve.tensor_tensor(lo, o, hi.bitcast(F32), ALU.subtract).then_inc(y_ready, 1)

                bias_max(0)
                for i in range(8):
                    if i < 7:
                        bias_max(i + 1)
                    normalise(i)
                    if i:
                        take_out(i - 1)
                take_out(7)
                for j in range(4):
                    add_to_x(g, k0 + MIX_IN_BLOCKS + j, j, n + 1)

            def split(hi, lo, src):
                dve.tensor_copy(hi, src)
                dve.drain()
                return dve.tensor_tensor(lo, src, hi.bitcast(F32), ALU.subtract)

            def norm_split(r, src, hi, lo, gain, chunks, width, dim, done):
                for c in range(chunks):
                    if c == 0:
                        dve.tensor_tensor(ssq[:, 0:width], src[:, 0, :], src[:, 0, :], ALU.mult)
                    else:
                        dve.drain()
                        dve.tensor_tensor(t_ring[:, 0, 0:width], src[:, c, :], src[:, c, :], ALU.mult)
                        dve.drain()
                        dve.tensor_tensor(ssq[:, 0:width], ssq[:, 0:width], t_ring[:, 0, 0:width], ALU.add)
                dve.drain().then_inc(ssq_ready, 1)
                rms(r, width, dim)
                for c in range(chunks):
                    dve.scalar_tensor_tensor(src[:, c, :], src[:, c, :], par2[:, gain + c:gain + c + 1],
                                             psum[:, S_BANK + 1, 0:width], ALU.mult, ALU.mult)
                dve.drain()
                split(hi, lo, src)
                dve.drain().then_inc(done, 1)

            def ctx_norm():
                dve.wait_ge(ctx_landed, 16)
                dve.tensor_tensor(cx_sq[:, :, :], cx[:, :, :], cx[:, :, :], ALU.mult)
                dve.tensor_scalar(a_col[:, :], mods[:, 80:88], 1.0, None, ALU.add)
                dve.drain()
                dve.tensor_tensor(a_col[:, :], a_col[:, :], gains[:, 56:64], ALU.mult)
                dve.tensor_reduce(ssq[:, 0:TC], cx_sq[:, :, :].rearrange("p c t -> p t c"), AX.X, ALU.add)
                dve.drain().then_inc(ssq_ready, 1)
                rms(R_CTX, TC)
                for c in range(DC):
                    dve.drain()
                    dve.scalar_tensor_tensor(cx[:, c, :], cx[:, c, :], a_col[:, c:c + 1], psum[:, S_BANK + 1, 0:TC], ALU.mult, ALU.mult)
                    dve.drain()
                    dve.tensor_scalar(ch_hi[:, c, :], cx[:, c, :], mods[:, 72 + c:73 + c], None, ALU.add)
                    dve.drain()
                    dve.scalar_tensor_tensor(ch_lo[:, c, :], cx[:, c, :], mods[:, 72 + c:73 + c], ch_hi[:, c, :].bitcast(F32),
                                             ALU.add, ALU.subtract).then_inc(ctx_h_ready, 1)

            def whole_norm(r, gain):
                rms(r)
                for c in range(DC):
                    dve.scalar_tensor_tensor(x[:, c, :], x[:, c, :], gains[:, gain + c:gain + c + 1], psum[:, S_BANK + 1, :],
                                             ALU.mult, ALU.mult).then_inc(x_ready, 1)

            def gla(u, width, ks, qs):
                h, pairs, chunks, full = u % 4, width // P, width // GLA_CHUNK, width == T
                b = lambda d: par2[:, C2["b_decay"] + 4 * d + h:C2["b_decay"] + 4 * d + h + 1]
                W = slice(0, width)
                dve.wait_ge(ln_ready, u + 1)
                for d in range(2):
                    dve.tensor_scalar(t_ring[:, d, W], psum[:, S_BANK + d, W], b(d), 0.0, ALU.add, ALU.min)
                dve.drain()
                dve.tensor_tensor(prod[:, :, W], t_ring[:, :, W], act_ring[:, :, W], ALU.subtract)
                dve.drain()
                dve.tensor_tensor_scan(act_ring[:, 0, W], resets[:, 0, W], prod[:, 0, W], 0.0, ALU.mult, ALU.add)
                back = slice(width - 1, None, -1)
                dve.tensor_tensor_scan(act_ring[:, 1, back], resets[:, 1, back], prod[:, 1, back], 0.0, ALU.mult, ALU.add)
                dve.drain()
                for d in range(2):
                    cum = act_ring[:, d, W].rearrange("p (c t) -> p c t", t=GLA_CHUNK)
                    total = cum[:, :, GLA_CHUNK - 1:GLA_CHUNK] if d == 0 else cum[:, :, 0:1]
                    dve.tensor_tensor(t_ring[:, d, W].rearrange("p (c t) -> p c t", t=GLA_CHUNK),
                                      total.broadcast_to([P, chunks, GLA_CHUNK]), cum, ALU.subtract)
                dve.drain().then_inc(cum_ready, 1)
                dve.wait_ge(exp_ready, u + 1)
                if full:
                    for d in range(2):
                        dve.scalar_tensor_tensor(qe[:, d, :], qs, GLA_QSCALE, prod[:, d, :], ALU.mult, ALU.mult)
                        dve.tensor_tensor(kn[:, d, :], kn[:, d, :], ks, ALU.mult)
                for d in range(2):
                    dve.tensor_tensor(t_ring[:, d, W], t_ring[:, d, W], ks, ALU.mult)
                dve.drain().then_inc(qk_ready, 1)
                for d in range(2):
                    dve.wait_ge(u_ps[d], u + 1)
                    order = list(range(chunks)) if d == 0 else list(range(chunks))[::-1]
                    last = s0[:, 4 * d + h, :]
                    if full:
                        dve.tensor_copy(states[:, d, order[0], :], last)
                        dve.drain()
                    for i, c in enumerate(order):
                        kv = psum[:, S_BANK + 2 * d + c % 2, (c // 2) * P:(c // 2 + 1) * P]
                        e = c * GLA_CHUNK + (GLA_CHUNK - 1 if d == 0 else 0)
                        if full:
                            if i + 1 < chunks:
                                dve.scalar_tensor_tensor(states[:, d, order[i + 1], :], states[:, d, c, :], prod[:, d, e:e + 1], kv,
                                                         ALU.mult, ALU.add)
                                dve.drain()
                        elif i == 0:
                            dve.tensor_copy(last, kv)
                            dve.drain()
                        else:
                            dve.scalar_tensor_tensor(last, last, prod[:, d, e:e + 1], kv, ALU.mult, ALU.add)
                            dve.drain()
                    dve.drain().then_inc(chain_ready, 1)
                if not full:
                    return
                dve.wait_ge(a_ps, h + 1)
                for d, out in ((0, am[:, :, :]), (1, t_ring[:, 0, :].rearrange("p (a b) -> p a b", b=P))):
                    dve.tensor_tensor(out, psum[:, S_BANK + d, :].rearrange("p (a b) -> p a b", b=P),
                                      masks[:, d:d + 1, :].broadcast_to([P, 4, P]), ALU.mult)
                dve.drain()
                dve.tensor_tensor(am[:, :, :], am[:, :, :], t_ring[:, 0, :].rearrange("p (a b) -> p a b", b=P), ALU.add
                                  ).then_inc(am_ready, 1)
                dve.wait_ge(og_ready, h + 1)
                rms(R_GLA + h, T, P)
                dve.scalar_tensor_tensor(y_gla[:, h, :], o_sb[:, :], par2[:, C2["gla_norm"]:C2["gla_norm"] + 1],
                                         psum[:, S_BANK + 1, :], ALU.mult, ALU.mult)
                dve.drain()
                dve.tensor_tensor(y_gla[:, h, :], y_gla[:, h, :], gr[:, h % 2, :], ALU.mult)
                dve.drain().then_inc(yg_ready, 1)

            def rotate(dst, src, src2):
                dve.tensor_tensor(t_ring[64:96, 0, :], src, rot[64:96, :], ALU.mult)
                dve.tensor_tensor(t_ring[64:96, 1, :], src2, rot[96:128, :], ALU.mult)
                dve.drain()
                dve.tensor_tensor(dst, t_ring[64:96, 0, :], t_ring[64:96, 1, :], ALU.add)
                dve.drain()

            def mla():
                dve.wait_ge(rot_landed, 16)
                for e in range(2):
                    rotate(keys[64:96, e, 0:T], krope[64:96, :], krope[96:128, :])
                dve.drain().then_inc(krot_ready, 1)

                def row_max(h, qb):
                    u = 4 * h + qb
                    dve.wait_ge(m_scores, u + 1)
                    s = 2 * (u % 2)
                    dve.tensor_reduce(small[:, 2, qb:qb + 1], psum[:, s:s + 2, :].rearrange("p a b -> p (a b)")[:, 0:TK], AX.X, ALU.max)
                    dve.drain()
                    dve.tensor_scalar(small[:, 0, qb:qb + 1], small[:, 2, qb:qb + 1], -MLA_SCALE, None, ALU.mult).then_inc(m_max, 1)

                def take_turned(h, kt):
                    dve.wait_ge(m_turn, 6 * h + kt + 1)
                    if kt >= 2:
                        dve.wait_ge(m_pv, 6 * h + kt - 1)
                    dve.tensor_copy(prod[:, kt % 2, :], psum[:, S_BANK + kt % 2, :]).then_inc(m_turned[1], 1)

                for h in range(MLA_HEADS):
                    if h % 2 == 0:
                        k = PAIR_K + h // 2
                        dve.wait_ge(block_done, 4 * G2 + k + 3)
                        for e in range(2):
                            ps = psum[:, 2 * (k % 2) + e, :]
                            dve.tensor_copy(act_ring[0:64, e, :], ps[0:64, :])
                            rotate(act_ring[64:96, e, :], ps[64:96, :], ps[96:128, :])
                        dve.drain().then_inc(out_free[k % 2], 1)
                        dve.drain().then_inc(qh_ready, 1)
                    row_max(h, 0)
                    row_max(h, 1)
                    if h:
                        for kt in (1, 3, 5):
                            take_turned(h - 1, kt)
                    row_max(h, 2)
                    row_max(h, 3)
                    dve.wait_ge(m_exp, 4 * h + 4)
                    dve.reciprocal(small[:, 3, 0:4], small[:, 1, 0:4])
                    dve.drain()
                    for qb in range(4):
                        dve.tensor_scalar(mprobs[:, qb, :], mprobs[:, qb, :], small[:, 3, qb:qb + 1], None, ALU.mult)
                    dve.drain().then_inc(m_norm, 1)
                for kt in (1, 3, 5):
                    take_turned(MLA_HEADS - 1, kt)

            def merge():
                for c in range(4):
                    split(om_hi[:, c, :], om_lo[:, c, :], o_mla[:, c, :])
                    split(yg_hi[:, c, :], yg_lo[:, c, :], y_gla[:, c, :])
                dve.drain().then_inc(branch_ready, 1)
                for mp in range(4):
                    k = MERGE_K + 3 * mp + 2
                    dve.wait_ge(sig_ready, 2 * mp + 2)
                    dve.wait_ge(block_done, 4 * G2 + k + 3)
                    for j, sig in enumerate((act_ring, prod)):
                        bank = 2 * (k % 2) if j == 0 else S_BANK
                        for which in range(2):
                            dve.tensor_tensor(t_ring[:, which, :], sig[:, which, :], psum[:, bank + which, :], ALU.mult)
                        dve.drain()
                        dve.tensor_tensor(merged[:, 2 * mp + j, :], t_ring[:, 0, :], t_ring[:, 1, :], ALU.add)
                        dve.drain().then_inc(merged_ready, 1)
                    dve.drain().then_inc(out_free[k % 2], 1)
                for c in range(DC):
                    split(h_hi[:, c, :], h_lo[:, c, :], merged[:, c, :]).then_inc(merged_split, 1)

            def conv_ffn():
                def third(g, k0, c0, count, last):
                    cols = CONV_COLS * count
                    dve.tensor_copy(cpar[:, 0:cols], par2[:, bass.ds(C2["conv"] + CONV_COLS * c0, cols)])
                    for j in range(count + 4):
                        k = k0 + j
                        if j < count:
                            tap = lambda i: cpar[:, CONV_COLS * j + i:CONV_COLS * j + i + 1]
                            src = gpad[:, j % 2, :].rearrange("p (r c) -> p r c", c=GRID_W)
                            dst = conv[:, j % 2, :].rearrange("p (r c) -> p r c", c=GRID_W)
                            rows = T // GRID_W
                            dve.drain()
                            dve.wait_ge(g_copied, c0 + j + 1)
                            dve.tensor_scalar(conv[:, j % 2, :], gpad[:, j % 2, :], tap(4), None, ALU.mult)
                            for dy in (-1, 0, 1):
                                for dx in (-1, 0, 1):
                                    if dy or dx:
                                        rs, cs = slice(max(0, -dy), rows - max(0, dy)), slice(max(0, -dx), GRID_W - max(0, dx))
                                        rr = slice(max(0, dy), rows - max(0, -dy))
                                        cc = slice(max(0, dx), GRID_W - max(0, -dx))
                                        dve.drain()
                                        dve.scalar_tensor_tensor(dst[:, rs, cs], src[:, rr, cc], tap(3 * (dy + 1) + dx + 1),
                                                                 dst[:, rs, cs], ALU.mult, ALU.add)
                            dve.drain().then_inc(conv_ready, 1)
                            dve.wait_ge(silu_ready, FC * 4 + c0 + j + 1)
                            dve.tensor_tensor(prod[:, j % 2, :], act_ring[:, j % 2, :], psum[:, 2 * (k % 2) + 1, :],
                                              ALU.mult).then_inc(out_free[k % 2], 1)
                            dve.drain()
                            split(hid_hi[:, j, :], hid_lo[:, j, :], prod[:, j % 2, :]).then_inc(hid_ready, 1)
                        else:
                            add_to_x(g, k, j - count, 9 if last else None)
                with dve.Fori(0, 2) as i:
                    third(G2 + 3 * i, FFN_K, 8 * i, 8, False)
                third(G2, FFN_K + 24, 16, 6, True)

            def second():
                whole_norm(R_FINAL1, 48)
                ctx_norm()
                for q in range(4):
                    add_squares(7, q)
                norm(6, None, 56, False, R_X1, (192, 200, 208))
                dve.wait_ge(ctx_out, 1)
                dve.wait_ge(second_landed, 64)
                norm_split(R_KVC, kvf_c[:, :, :], kvn_hi[:, :, T:TK], kvn_lo[:, :, T:TK], C2["kv_norm"], 2, TC, 2 * P, kvn_ready)
                for u in range(4):
                    gla(u, TC, gk_c[:, u, :], None)
                dve.wait_ge(kvf_ready, 2)
                norm_split(R_KVX, kvf[:, :, :], kvn_hi[:, :, 0:T], kvn_lo[:, :, 0:T], C2["kv_norm"], 2, T, 2 * P, kvn_ready)
                norm_split(R_QX, qf[:, :, :], qn_hi[:, :, :], qn_lo[:, :, :], C2["q_norm"], 3, T, 3 * P, qn_ready)
                mla()
                for h in range(GLA_HEADS):
                    gla(4 + h, T, gk[:, h % 2, :], gq[:, h % 2, :])
                merge()
                dve.wait_ge(x_back, 16)
                for j in range(4):
                    add_to_x(G2, OUT_K + j, j, 8)
                norm(7, None, 64, False, R_X2, (88, 168, 176))
                conv_ffn()
                whole_norm(R_FINAL2, 72)

            dve.drain().then_inc(mod_used, 2)
            dve.drain().then_inc(conv_ready, 2)
            dve.drain().then_inc(out_free[0], 1)
            dve.drain().then_inc(out_free[1], 1)
            dve.drain().then_inc(sq_used, 1)
            dve.drain().then_inc(hid_ready, 2)
            dve.wait_ge(consts_landed, 16 * 8)
            dve.drain().then_inc(x_ready, 8)
            dve.drain().then_inc(cond_ready, 1)
            dve.wait_ge(cond_ready, 2)
            for q in range(4):
                add_squares(0, q)
            with dve.Fori(0, 6) as i:
                mod_partial(i)
                mod_take(i)
            with dve.Fori(0, DEPTH) as l:
                g = l * (LAYER_BLOCKS // 4)
                at = 4 * LAYER_MODS * l
                dve.tensor_copy(par[:, :], layer_par[:, bass.ds(NLP * l, NLP)])
                dve.tensor_copy(gate_w[:, :, :].rearrange("p a b -> p (a b)"), gates_all[:, bass.ds(4 * P * l, 4 * P)])
                dve.drain().then_inc(par_ready, 1)
                norm(3 * l, at, 24 * l, True)
                ffn(g, 0, 3 * l, 2 * l, LAYER_MODS * l + 6)
                norm(3 * l + 1, at + 24, 24 * l + 8, False)
                mixer(l, g, FFN_BLOCKS, 3 * l + 1)
                norm(3 * l + 2, at + 48, 24 * l + 16, True)
                ffn(g, FFN_BLOCKS + MIX_BLOCKS, 3 * l + 2, 2 * l + 1, LAYER_MODS * l + 18)
            second()


def columns(np, v):
    return np.asarray(v).reshape(-1, P).T


def pair_blocks(np, w):
    return w.reshape(KC, P, -1, BLOCK_COLS).transpose(2, 1, 0, 3).reshape(-1, P, BLOCK)


def ffn_blocks(np, gu, down, first=0, second=D_FF):
    both = np.stack([gu[:, first:first + D_FF].reshape(D, FC, P), gu[:, second:second + D_FF].reshape(D, FC, P)], 2)
    ups = pair_blocks(np, both.reshape(D, FC * BLOCK_COLS))
    out, at = [], 0
    for n in THIRDS:
        rows = down[at * P:(at + n) * P]
        if n < KC:
            rows = np.concatenate([rows, np.zeros(((KC - n) * P, D), rows.dtype)], 0)
        out += [ups[at:at + n], pair_blocks(np, rows)]
        at += n
    return out


def second_blocks(np, i):
    w = i["w_in_2"][0]
    at, parts = 0, {}
    for name, n in (("q", 384), ("kv", 256), ("rope", 32), ("gq", 512), ("gk", 512), ("gv", 512), ("gr", 512), ("glow", 32), ("gate", 2048)):
        parts[name] = w[:, at:at + n]
        at += n
    partner = np.concatenate([np.arange(8, 16), np.arange(0, 8), np.arange(24, 32), np.arange(16, 24)])
    rg = np.concatenate([parts["glow"], parts["glow"], parts["rope"], parts["rope"][:, partner]], 1)
    blocks = [pair_blocks(np, np.concatenate([parts["kv"], parts["gk"], parts["gv"], rg, rg], 1)),
              pair_blocks(np, np.concatenate([parts["kv"], rg, parts["q"]], 1))]
    ukv = i["w_ukv_2"][0].reshape(2, P, MLA_HEADS, 2, 64)
    v = np.zeros((P, 4, T), w.dtype)
    v[:, 0:2] = ukv[:, :, :, 1].reshape(2, P, T).transpose(1, 0, 2)
    blocks.append(v.reshape(1, P, BLOCK))
    uq = i["w_uq_2"][0].reshape(3, P, MLA_HEADS, NOPE + ROPE)
    for p in range(4):
        b = np.zeros((P, KC, 2, P), w.dtype)
        for e in range(2):
            q = uq[:, :, 2 * p + e]
            b[:, 0:3, e, :] = np.concatenate([q, q[:, :, NOPE:][:, :, partner]], 2).transpose(1, 0, 2)
        b[:, 3:5, 0, :] = ukv[:, :, 2 * p:2 * p + 2, 0].reshape(2, P, P).transpose(1, 0, 2)
        blocks.append(b.reshape(1, P, BLOCK))
    for h in range(GLA_HEADS):
        blocks.append(pair_blocks(np, np.concatenate([parts[n][:, h * P:(h + 1) * P] for n in ("gk", "gq", "gv", "gr")], 1)))
    gates = parts["gate"].reshape(D, 2, DC, P)
    branches = [i[n][0].reshape(4, P, DC, P) for n in ("w_br_mla_2", "w_br_gla_2")]
    for mp in range(4):
        for j in range(2):
            blocks.append(pair_blocks(np, gates[:, :, 2 * mp + j].reshape(D, 2 * P)))
        blocks.append(np.stack([branches[which][:, :, 2 * mp + j].transpose(1, 0, 2) for j in range(2) for which in range(2)], 1)
                      .reshape(1, P, BLOCK))
    blocks.append(pair_blocks(np, i["w_out_2"][0]))
    return blocks + ffn_blocks(np, i["w_up_2"][0], i["w_down_2"][0], first=D_FF, second=0)


def second_tables(np, i):
    a = {}
    a["ctxT"] = i["ctx_2"].reshape(TC, DC, P).transpose(2, 1, 0).reshape(P, DC * TC)
    conv = np.concatenate([i["conv_w_2"][0].reshape(9, D_FF), i["conv_b_2"]], 0).reshape(CONV_COLS, FC, P).transpose(2, 1, 0)
    a["par2"] = np.concatenate([columns(np, i["q_norm_g_2"]), columns(np, i["kv_norm_g_2"]), columns(np, i["gla_norm_g_2"]),
                                columns(np, i["gla_b_decay_2"]), conv.reshape(P, FC * CONV_COLS)], 1)
    wd = np.zeros((2, 16, 2, 512), i["x"].dtype)
    for d in range(2):
        wd[d, :, d] = i["gla_w_decay_2"][0, d]
    a["w_decay"] = wd.reshape(32, 1024)
    t = np.arange(P)
    same = t[:, None] // GLA_CHUNK == t[None] // GLA_CHUNK
    a["masks"] = np.concatenate([same & (t[:, None] <= t[None]), same & (t[:, None] >= t[None])], 1).astype(np.float32)
    tt = np.arange(T) % GLA_CHUNK
    a["resets"] = np.broadcast_to(np.concatenate([tt != 0, tt != GLA_CHUNK - 1])[None], (P, 2 * T)).astype(np.float32)
    tok = np.arange(T)
    inv = (np.float32(10000.0) ** (-np.arange(0, 16, 2, dtype=np.float32) / np.float32(16))).astype(np.float32)
    ang = [(p.astype(np.float32)[None] * inv[:, None]) for p in (tok // GRID_W, tok % GRID_W)]
    rot = np.zeros((P, T), np.float32)
    for ax in range(2):
        for half in range(2):
            r = 64 + 16 * ax + 8 * half
            rot[r:r + 8] = np.cos(ang[ax])
            rot[32 + r:40 + r] = np.sin(ang[ax]) * (1 if half else -1)
    a["rot"] = rot
    return a


def layout(np, i):
    a = {}
    a["xT"] = np.asarray(i["x"]).reshape(T, DC, P).transpose(2, 1, 0).reshape(P, DC * T)
    blocks = []
    for l in range(DEPTH):
        blocks += ffn_blocks(np, i["w_ffn1_gu"][l], i["w_ffn1_down"][l])
        w = i["w_in"][l]
        blocks.append(pair_blocks(np, np.concatenate([w[:, 0:1024], w[:, 1536:1792], w[:, 1792:2048], w[:, 1280:1536], w[:, 1024:1280]], 1)))
        blocks.append(pair_blocks(np, i["w_out"][l]))
        blocks += ffn_blocks(np, i["w_ffn2_gu"][l], i["w_ffn2_down"][l])
    blocks += second_blocks(np, i)
    a["weights"] = np.concatenate(blocks, 0)

    pos = []
    for l in range(DEPTH):
        pos += [("w_mod", l, c) for c in range(18)]
        extra = [(2, 0), (2, 1), (2, 2), (2, 3), (1, 6), (1, 7)] if l == 0 else [(1, 8), (1, 9), (1, 10), (1, 11), (1, 11), (1, 11)]
        pos += [("w_ada_2", who, c) for who, c in extra]
    pos += [("w_ada_2", 1, c) for c in range(6)]
    ws, bs, cs = [], [], []
    for name, l, c in pos:
        first = name == "w_mod"
        w, b = (i["w_mod"][l], i["b_mod"][l]) if first else (i["w_ada_2"][0], i["b_ada_2"][0])
        cond = i["c"] if first else (i["c_2"] if l == 1 else i["c_ctx_2"])
        ws.append(w[:, c * MOD_COLS:(c + 1) * MOD_COLS].reshape(MOD_PIECES, MOD_K, P, MOD_COLS).transpose(0, 2, 1, 3)
                  .reshape(MOD_PIECES, P, MOD_K * MOD_COLS))
        bs.append(columns(np, b[c * MOD_COLS:(c + 1) * MOD_COLS]))
        cs.append(columns(np, cond))
    a["mod_w"] = np.stack(ws)
    a["mod_b"] = np.concatenate(bs, 1)
    a["cond"] = np.concatenate(cs, 1)
    a["gains"] = np.concatenate([columns(np, i["g_norm"][l, s]) for l in range(DEPTH) for s in range(3)]
                                + [columns(np, i[n]) for n in ("g_final", "norm1_g_2", "norm2_g_2", "final_g_2")], 1)
    lp, gw = [], []
    for l in range(DEPTH):
        lp += [np.broadcast_to(i["attn_sinks"][l][None], (P, HEADS)), columns(np, i["lru_conv_w"][l]), columns(np, i["lru_conv_b"][l]),
               columns(np, i["lru_gate_a_b"][l]), columns(np, i["lru_gate_x_b"][l]), columns(np, i["lru_lambda"][l]),
               columns(np, i["sc_conv_w"][l])]
        for w in (i["lru_gate_a_w"][l], i["lru_gate_x_w"][l]):
            for t in range(2):
                m = np.zeros((P, P), w.dtype)
                m[:64, :64], m[64:, 64:] = w[2 * t], w[2 * t + 1]
                gw.append(m)
    a["layer_par"] = np.concatenate(lp, 1)
    a["lru_gates"] = np.concatenate(gw, 1)
    a.update(second_tables(np, i))
    a["ident"] = np.eye(P, dtype=np.float32)
    dist = np.arange(P)[:, None] + WINDOW - np.arange(2 * WINDOW)[None]
    a["alibi"] = np.where((dist >= 0) & (dist < WINDOW), dist, 1e30).astype(np.float32)
    return {k: np.ascontiguousarray(v) for k, v in a.items()}


_OUTS = [((P, DC * T), "float32")]


def kernel(**inputs):
    import numpy as np
    import concourse.bacc as bacc
    from concourse.bass_utils import run_bass_kernel_spmd

    nc = bacc.Bacc("TRN2", target_bir_lowering=False, num_devices=1)
    arrays = layout(np, {k: np.asarray(v) for k, v in inputs.items()})
    args = {k: nc.dram_tensor(f"in_{k}_dram", v.shape, mybir.dt.from_np(v.dtype), kind="ExternalInput").ap()
            for k, v in arrays.items()}
    args["out"] = nc.dram_tensor("out_0_dram", _OUTS[0][0], F32, kind="ExternalOutput").ap()
    program(nc, args)
    r = run_bass_kernel_spmd(nc, [{f"in_{k}_dram": v for k, v in arrays.items()}], core_ids=[0])
    y = r.results[0]["out_0_dram"]
    return y.reshape(P, DC, T).transpose(2, 1, 0).reshape(1, T, D)
```

```python
from contextlib import ExitStack

import concourse.bass as bass
from concourse import mybir

ALU = mybir.AluOpType
ACT = mybir.ActivationFunctionType
AX = mybir.AxisListType
F32 = mybir.dt.float32
F32R = mybir.dt.float32r

P = 128
D = 1024
DC = D // P
T = 512
DEPTH = 2
EPS = 1e-6
D_FF = 2816
FC = D_FF // P
THIRDS = (8, 8, 6)
WINDOW = 128
HEADS = 8
LRU_TILES = 2

KC = 8
BLOCK_COLS = 256
BLOCK = KC * BLOCK_COLS
RAW_SLOTS = 4
FFN_BLOCKS = FC + 3 * (D // BLOCK_COLS)
MIX_IN_BLOCKS = 8
MIX_BLOCKS = MIX_IN_BLOCKS + D // BLOCK_COLS
LX_J, Q_J, KV_J, SC_J, SX_J, SB_J, LG_J = 0, 1, 3, 4, 5, 6, 7
LAYER_BLOCKS = 2 * FFN_BLOCKS + MIX_BLOCKS

MOD_COLS = 512
MOD_K = 2
MOD_PIECES = DC // MOD_K
LAYER_MODS = 24
FIRST_MODS = 4

TC = 256
TK = T + TC
MLA_HEADS, NOPE, ROPE = 8, 64, 32
MLA_SCALE = (NOPE + ROPE) ** -0.5
Q_LORA_C, KV_LORA_C = 3, 2
GLA_HEADS, GLA_CHUNK = 4, 64
GLA_QSCALE = 128 ** -0.5
GATE_NORM = 16.0
GRID_W = 64
CONV_COLS = 10
CTX_K, X_K, V_K, PAIR_K, GLA_K, BRANCH_K, OUT_K, FFN_K = 0, 6, 14, 15, 19, 30, 34, 38
GATE_K = (9, 10, 11, 12, 13, 27, 28, 29)
FILLERS = ((8, 9), (10,), (12,), (), (21, 22), (23, 24), (25, 26), (27, 28, 29))
KVX_FILLER, QX_FILLER = 11, 13
R_FINAL1, R_CTX, R_X1, R_KVC, R_KVX, R_QX, R_GLA, R_X2, R_FINAL2 = 6, 7, 8, 9, 10, 11, 12, 16, 17


def alibi_slope(h):
    return 2.0 ** (-8.0 * (h + 1) / HEADS)


def layer_columns():
    at, cols = 0, {}
    for name, n in (("sink", 8), ("lru_w", 8), ("lru_b", 2), ("gate_a_b", 2), ("gate_x_b", 2), ("lam", 2), ("sc_w", 6)):
        cols[name] = at
        at += n
    return cols, at


def second_columns():
    at, cols = 0, {}
    for name, n in (("q_norm", 3), ("kv_norm", 2), ("gla_norm", 1), ("b_decay", 8), ("conv", FC * CONV_COLS)):
        cols[name] = at
        at += n
    return cols, at


def program(nc, a):
    LC, NLP = layer_columns()
    C2, NP2 = second_columns()
    G2 = DEPTH * LAYER_BLOCKS // 4
    NPOS = a["mod_w"].shape[0]
    NBLK = a["weights"].shape[0]
    with ExitStack() as ctx:
        def sb(name, shape, dt=F32):
            return ctx.enter_context(nc.sbuf_tensor(name, shape, dt))

        def region(specs):
            out = []
            with ExitStack() as inner:
                for name, shape, dt in specs:
                    out.append(inner.enter_context(nc.sbuf_tensor(name, shape, dt)))
            return out

        def sem(name):
            return ctx.enter_context(nc.semaphore(name))

        first_mods_a, = region([("first_mods_a", [P, 2, DC, MOD_COLS], F32)])
        h_hi = sb("h_hi", [P, DC, T], F32R)
        h_lo = sb("h_lo", [P, DC, T], F32R)
        raw = sb("raw", [P, RAW_SLOTS, BLOCK])
        w_hi = sb("w_hi", [P, 2, BLOCK], F32R)
        w_lo = sb("w_lo", [P, 2, BLOCK], F32R)
        mod_raw = sb("mod_raw", [P, 2, MOD_K, MOD_COLS])
        mod_acc = sb("mod_acc", [P, MOD_COLS])
        mod_parts = sb("mod_parts", [P, 2, MOD_COLS], F32R)
        ones_r = sb("ones_r", [P, P], F32R)
        t_ring = sb("t_ring", [P, 2, T])
        sq = sb("sq", [P, 2, T])
        ssq = sb("ssq", [P, T])
        diag = sb("diag", [P, 4, P])
        cond_wide, = region([("cond_wide", [P, DC, P], F32)])
        act_ring = sb("act_ring", [P, 2, T])
        prod = sb("prod", [P, 2, T])
        ident = sb("ident", [P, P])
        ones = sb("ones", [P, P])
        alibi = sb("alibi", [P, 2 * WINDOW])
        cond = sb("cond", [P, NPOS * 8])
        mod_b = sb("mod_b", [P, NPOS * 4])
        mods = sb("mods", [P, NPOS * 4])
        gains = sb("gains", [P, a["gains"].shape[1]])
        layer_par = sb("layer_par", [P, DEPTH * NLP])
        par = sb("par", [P, NLP])
        gates_all = sb("gates_all", [P, DEPTH * 4 * P])
        gate_w = sb("gate_w", [P, 4, P])
        cond_now = sb("cond_now", [P, 8])
        a_col = sb("a_col", [P, DC])
        shift = sb("shift", [P, DC])
        gate = sb("gate", [P, DC])
        var = sb("var", [P, 4])
        rstd = sb("rstd", [P, 4])
        mhalf = sb("mhalf", [P, 4])
        small = sb("small", [P, 8, 8])
        par2 = sb("par2", [P, NP2])
        cpar = sb("cpar", [P, 8 * CONV_COLS])
        hid_hi, hid_lo, gpad, conv = region([("hid_hi", [P, 8, T], F32R), ("hid_lo", [P, 8, T], F32R), ("gpad", [P, 2, T], F32), ("conv", [P, 2, T], F32)])
        first_mods_b, = region([("first_mods_b", [P, 2, DC, MOD_COLS], F32)])
        qT, k_dup, v_tok, lx, lg, z, sb_gate, probs, probsT, xc, x = region([
            ("qT", [P, 4, T], F32), ("k_dup", [P, 2, T], F32), ("v_tok", [P, 4, P], F32),
            ("lx", [P, 2, T], F32), ("lg", [P, 2, T], F32), ("z", [P, 2, T], F32),
            ("sb_gate", [P, 2, T], F32), ("probs", [P, 2, 4, 2 * WINDOW], F32),
            ("probsT", [P, 8, P], F32), ("xc", [P, 2, T], F32), ("x", [P, DC, T], F32)])
        kvn_hi, kvn_lo, keys, ch_hi, ch_lo, cx, glow_c, kvf_c = region([
            ("kvn_hi", [P, 2, TK], F32R), ("kvn_lo", [P, 2, TK], F32R), ("keys", [P, 2, TK], F32),
            ("ch_hi", [P, DC, TC], F32R), ("ch_lo", [P, DC, TC], F32R), ("cx", [P, DC, TC], F32),
            ("glow_c", [P, TC], F32), ("kvf_c", [P, 2, TC], F32)])
        _, cx_sq, _, kdT_c, vt_c, s_c, gk_c, gv_c = region([
            ("skip0", [P, 18 * 256], F32), ("cx_sq", [P, DC, TC], F32), ("skip1", [P, 4 * 256], F32),
            ("kdT_c", [P, 2, 2, P], F32), ("vt_c", [P, 2, P], F32), ("s_c", [P, 2, P], F32),
            ("gk_c", [P, GLA_HEADS, TC], F32), ("gv_c", [P, GLA_HEADS, TC], F32)])
        _, qn_hi, qn_lo, vals, mprobs, o_mla = region([
            ("skip2", [P, 18 * 256], F32), ("qn_hi", [P, 3, T], F32R), ("qn_lo", [P, 3, T], F32R),
            ("vals", [P, 6, T], F32), ("mprobs", [P, 4, TK], F32), ("o_mla", [P, 4, T], F32)])
        _, kvf, qf = region([("skip3", [P, 46 * 256], F32), ("kvf", [P, 2, T], F32), ("qf", [P, 3, T], F32)])
        gk, gq, gv, kn, gvt, qe, kdT, states, am, gr, o_sb, y_gla, gate_out = region([
            ("gk", [P, 2, T], F32), ("gq", [P, 2, T], F32), ("gv", [P, 2, T], F32), ("kn", [P, 2, T], F32),
            ("gvt", [P, 4, P], F32), ("qe", [P, 2, T], F32), ("kdT", [P, 2, 4, P], F32),
            ("states", [P, 2, 8, P], F32), ("am", [P, 4, P], F32), ("gr", [P, 2, T], F32),
            ("o_sb", [P, T], F32), ("y_gla", [P, 4, T], F32), ("gate_out", [P, 2, T], F32)])
        om_hi, om_lo, yg_hi, yg_lo, merged = region([
            ("om_hi", [P, 4, T], F32R), ("om_lo", [P, 4, T], F32R), ("yg_hi", [P, 4, T], F32R),
            ("yg_lo", [P, 4, T], F32R), ("merged", [P, DC, T], F32)])
        _, gate_out_c = region([("skip4", [P, 56 * 256], F32), ("gate_out_c", [P, 2, T], F32)])
        s0 = mod_raw[:, 0, :, :].rearrange("p a (b c) -> p (a b) c", c=P)
        resets = mod_raw[:, 1, :, :]
        rot = sq[:, 0, :]
        krope = mod_acc
        w_decay = gates_all
        masks = gate_w
        sig = first_mods_a[:, :, :, :].rearrange("p a c n -> p a (c n)")
        gate_spill = nc.dram_tensor("gate_spill", [P, 2 * DC * T], F32, kind="Internal").ap()
        x_spill = nc.dram_tensor("x_spill", [P, DC * T], F32, kind="Internal").ap()
        psum = ctx.enter_context(nc.psum_tensor("psum", [P, 8, T], F32))

        raw_landed = [sem(f"raw_landed{i}") for i in range(RAW_SLOTS)]
        hi_ready = sem("hi_ready")
        lo_ready = sem("lo_ready")
        block_done = sem("block_done")
        out_free = [sem(f"out_free{i}") for i in range(2)]
        mod_landed = [sem(f"mod_landed{i}") for i in range(2)]
        first_landed = [sem(f"first_landed{i}") for i in range(FIRST_MODS)]
        wide_ready = sem("wide_ready")
        mod_used = sem("mod_used")
        macc_ready = sem("macc_ready")
        half_done = sem("half_done")
        msum_ready = sem("msum_ready")
        consts_landed = sem("consts_landed")
        consts_ready = sem("consts_ready")
        x_landed = sem("x_landed")
        cond_landed = sem("cond_landed")
        cond_ready = sem("cond_ready")
        x_ready = sem("x_ready")
        sq_ready = sem("sq_ready")
        sq_used = sem("sq_used")
        ssq_ready = sem("ssq_ready")
        cols_ready = sem("cols_ready")
        var_ready = sem("var_ready")
        rstd_ready = sem("rstd_ready")
        diag_ready = sem("diag_ready")
        rb_ready = sem("rb_ready")
        t_ready = sem("t_ready")
        h_hi_ready = sem("h_hi_ready")
        h_ready = sem("h_ready")
        silu_ready = sem("silu_ready")
        hid_ready = sem("hid_ready")
        q_ready = sem("q_ready")
        k_ready = sem("k_ready")
        v_ready = sem("v_ready")
        vtok_ps = sem("vtok_ps")
        vtok_ready = sem("vtok_ready")
        lru_in = sem("lru_in")
        xc_ready = sem("xc_ready")
        gates_ps = sem("gates_ps")
        gates_ready = sem("gates_ready")
        lam_abs = sem("lam_abs")
        decay_ready = sem("decay_ready")
        m2_ready = sem("m2_ready")
        mult_ready = sem("mult_ready")
        scores_ps = sem("scores_ps")
        s_ready = sem("s_ready")
        p_ready = sem("p_ready")
        pn_ready = sem("pn_ready")
        pT_ps = sem("pT_ps")
        pT_ready = sem("pT_ready")
        o_ps = sem("o_ps")
        o_taken = sem("o_taken")
        y_ready = sem("y_ready")
        par_ready = sem("par_ready")
        stored = sem("stored")
        second_landed = sem("second_landed")
        ctx_landed = sem("ctx_landed")
        ctx_sq_ready = sem("ctx_sq_ready")
        ctx_h_ready = sem("ctx_h_ready")
        ctx_out = sem("ctx_out")
        kvf_ready = sem("kvf_ready")
        rg_ready = sem("rg_ready")
        spilled = sem("spilled")
        rot_landed = sem("rot_landed")
        kvn_ready = sem("kvn_ready")
        qn_ready = sem("qn_ready")
        vals_ready = sem("vals_ready")
        krot_ready = sem("krot_ready")
        qh_ready = sem("qh_ready")
        keys_ps = sem("keys_ps")
        keys_ready = sem("keys_ready")
        m_scores = sem("m_scores")
        m_max = sem("m_max")
        m_exp = sem("m_exp")
        m_norm = sem("m_norm")
        m_turn = sem("m_turn")
        m_turned = [sem("m_turned_act"), sem("m_turned_dve")]
        m_pv = sem("m_pv")
        o_mla_ready = sem("o_mla_ready")
        g_in = sem("g_in")
        pre_ps = sem("pre_ps")
        ln_ready = sem("ln_ready")
        cum_ready = sem("cum_ready")
        exp_ready = sem("exp_ready")
        decays_ready = sem("decays_ready")
        qk_ready = sem("qk_ready")
        turn_ps = sem("turn_ps")
        turn_ready = sem("turn_ready")
        u_ps = [sem("u_ps0"), sem("u_ps1")]
        chain_ready = sem("chain_ready")
        a_ps = sem("a_ps")
        am_ready = sem("am_ready")
        og_ps = sem("og_ps")
        og_ready = sem("og_ready")
        yg_ready = sem("yg_ready")
        branch_ready = sem("branch_ready")
        sig_ready = sem("sig_ready")
        gate_spilled = sem("gate_spilled")
        sig_back = [sem(f"sig_back{i}") for i in range(4)]
        merged_ready = sem("merged_ready")
        merged_split = sem("merged_split")
        x_back = sem("x_back")
        g_copied = sem("g_copied")
        conv_ready = sem("conv_ready")

        block = ctx.enter_context(nc.Block())
        S_BANK, T_BANK, O_BANK = 4, 6, 7

        def pre(d, width):
            return psum[:, (S_BANK if width == T else T_BANK) + d, 0:width]

        def update(d, c, width):
            bank, at = (2 * d + c % 2, c // 2) if width == T else (c % 2, 2 * d + c // 2)
            return psum[:, S_BANK + bank, at * P:(at + 1) * P]

        def first_mod(pos):
            return (first_mods_a, first_mods_b)[pos // 2][:, pos % 2, :, :]

        @block.sync
        def _(sp):
            def load_block(g, k, static=None):
                s = k % RAW_SLOTS
                sp.wait_ge(lo_ready, 4 * g + k + 1)
                sp.dma_start(raw[:, s:s + 1, :], a["weights"][bass.ds(4 * g + k, 1)].rearrange("b p n -> p b n")
                             ).then_inc(raw_landed[s], 16)

            def load_mod(pos):
                for piece in range(MOD_PIECES):
                    sp.wait_ge(mod_used, MOD_PIECES * (pos - FIRST_MODS) + piece + 1)
                    sp.dma_start(mod_raw[:, piece % 2:piece % 2 + 1, :, :].rearrange("p s k n -> p s (k n)"),
                                 a["mod_w"][bass.ds(pos, 1), piece].rearrange("b p n -> p b n")
                                 ).then_inc(mod_landed[piece % 2], 16)

            def ffn(g, k0, pos=None, skip=0):
                def third(g, k0, pos, n, skip=0):
                    for j in range(n + 4 - skip):
                        load_block(g, k0 + j + 3)
                        if pos is not None and j in (0, 2, 4, 6):
                            load_mod(pos + j // 2)
                with sp.Fori(0, 2) as i:
                    third(g + 3 * i, k0, None if pos is None else pos + 4 * i, 8)
                third(g, k0 + 24, None if pos is None else pos + 8, 6, skip)

            for name, t in (("cond", cond), ("ident", ident)):
                sp.dma_start(t[:, :], a[name]).then_inc(cond_landed, 16)
            sp.dma_start(x[:, :, :].rearrange("p c n -> p (c n)"), a["xT"]).then_inc(x_landed, 16)
            for pos in range(FIRST_MODS):
                for piece in range(MOD_PIECES):
                    sp.dma_start(first_mod(pos)[:, MOD_K * piece:MOD_K * (piece + 1), :].rearrange("p k n -> p (k n)"),
                                 a["mod_w"][pos, piece]).then_inc(first_landed[pos], 16)
            for name, t in (("mod_b", mod_b), ("gains", gains), ("layer_par", layer_par),
                            ("lru_gates", gates_all), ("alibi", alibi)):
                sp.dma_start(t[:, :], a[name]).then_inc(consts_landed, 16)
            for k in range(3):
                load_block(0, k)
            with sp.Fori(0, DEPTH) as l:
                g = l * (LAYER_BLOCKS // 4)
                ffn(g, 0, l * LAYER_MODS + FIRST_MODS)
                for j in range(MIX_BLOCKS):
                    load_block(g, FFN_BLOCKS + j + 3)
                ffn(g, FFN_BLOCKS + MIX_BLOCKS, l * LAYER_MODS + FIRST_MODS + 12)
            sp.wait_ge(mod_used, MOD_PIECES * (NPOS - FIRST_MODS) + 2)
            sp.dma_start(cx[:, :, :].rearrange("p c n -> p (c n)"), a["ctxT"]).then_inc(ctx_landed, 16)
            for name, dst in (("par2", par2[:, :]), ("w_decay", w_decay[0:32, :]), ("masks", masks[:, 0:2, :].rearrange("p a b -> p (a b)")),
                              ("resets", resets.rearrange("p a b -> p (a b)"))):
                sp.dma_start(dst, a[name]).then_inc(second_landed, 16)
            for k in range(FFN_K):
                load_block(G2, k + 3)
            ffn(G2, FFN_K, skip=3)
            for c in range(2):
                sp.wait_ge(x_ready, 8 * 9 + 8 + 4 * c + 4)
                sp.dma_start(a["out"][:, 4 * c * T:4 * (c + 1) * T], x[:, 4 * c:4 * c + 4, :].rearrange("p c n -> p (c n)")).then_inc(stored, 16)
            sp.wait_ge(stored, 32)

        @block.gpsimd
        def _(pool):
            nc.gpsimd.memset(ones[:, :], 1.0)
            nc.gpsimd.memset(mhalf[:, :], -0.5)
            pool.drain().then_inc(consts_ready, 1)

            def split_lo(g, k, inc=1):
                pool.wait_ge(hi_ready, 4 * g + k + 1)
                pool.tensor_tensor(w_lo[:, k % 2, :], raw[:, k % 4, :], w_hi[:, k % 2, :].bitcast(F32),
                                   ALU.subtract).then_inc(lo_ready, 1)

            def rms(n):
                pool.wait_ge(var_ready, n + 1)
                pool.tensor_tensor(rstd[:, :], var[:, :], mhalf[:, :], ALU.pow).then_inc(rstd_ready, 1)

            def splits(g, k0, n):
                for j in range(n):
                    split_lo(g, k0 + j)

            pool.drain().then_inc(lo_ready, RAW_SLOTS)
            splits(0, 0, 1)
            with pool.Fori(0, DEPTH) as l:
                g = l * (LAYER_BLOCKS // 4)
                for n, (k0, blocks) in enumerate(((0, FFN_BLOCKS), (FFN_BLOCKS, MIX_BLOCKS),
                                                  (FFN_BLOCKS + MIX_BLOCKS, FFN_BLOCKS))):
                    rms(3 * l + n)
                    if blocks == FFN_BLOCKS:
                        with pool.Fori(0, 2) as i:
                            splits(g + 3 * i, k0 + 1, 12)
                        splits(g, k0 + 25, 10)
                    else:
                        splits(g, k0 + 1, blocks)
            for r, k, n in ((R_FINAL1, 1, 0), (R_CTX, 1, 4), (R_X1, 5, 3), (R_KVC, 8, 5), (R_KVX, 13, 2), (R_QX, 15, 8)):
                rms(r)
                splits(G2, k, n)
            for h in range(GLA_HEADS):
                splits(G2, 23 + 2 * h, 2)
                rms(R_GLA + h)
            splits(G2, 31, 8)
            rms(R_X2)
            with pool.Fori(0, 2) as i:
                splits(G2 + 3 * i, FFN_K + 1, 12)
            splits(G2, FFN_K + 25, 9)
            rms(R_FINAL2)

        @block.tensor
        def _(pe):
            pe.drain().then_inc(block_done, 2)

            def products(g, k, rhs, ks=range(KC), waits=None, width=T, between=None, half=False):
                pe.wait_ge(lo_ready, 4 * g + k + 1 + RAW_SLOTS)
                pe.wait_ge(out_free[k % 2], 2 * g + k // 2 + 1)
                rhs_hi, rhs_lo = rhs
                order = [(t, c) for c in ks for t in range(2)] if waits else [(t, c) for t in range(2) for c in ks]
                for t, c in order:
                    if between is not None and (t, c) == (1, ks[0]):
                        between()
                    if waits and t == 0:
                        pe.wait_ge(waits[0], waits[1] + c + 1)
                    wh, wl = (w[:, k % 2, c * 256 + t * P:c * 256 + (t + 1) * P] for w in (w_hi, w_lo))
                    out = psum[:, 2 * (k % 2) + t, 0:width]
                    pe.matmul(out, wh, rhs_hi[:, c, :], start=(c == ks[0]), stop=False)
                    pe.matmul(out, wh, rhs_lo[:, c, :], start=False, stop=False)
                    mm = pe.matmul(out, wl, rhs_hi[:, c, :], start=False, stop=(c == ks[-1]))
                    if half and (t, c) == (0, ks[-1]):
                        mm.then_inc(half_done, 1)
                mm.then_inc(block_done, 1)

            def mod_sum(pos):
                pe.wait_ge(macc_ready, pos - FIRST_MODS + 1)
                pe.matmul(psum[:, O_BANK, :], ones_r[:, :], mod_parts[:, 0, :], start=True, stop=False)
                pe.matmul(psum[:, O_BANK, :], ones_r[:, :], mod_parts[:, 1, :], start=False, stop=True).then_inc(msum_ready, 1)

            def rms_cols(n, width=T, src=ssq, bank=S_BANK):
                pe.wait_ge(ssq_ready, n + 1)
                for t in range(width // P):
                    mm = pe.matmul(psum[:, bank, t:t + 1], src[:, t * P:(t + 1) * P], ones[:, 0:1], start=True, stop=True)
                mm.then_inc(cols_ready, 1)

            def rms_rows(n, width=T, bank=S_BANK):
                pe.wait_ge(diag_ready, n + 1)
                pe.matmul(psum[:, bank + 1, 0:width], ones[:, :], diag[:, :, :].rearrange("p a b -> p (a b)")[:, 0:width],
                          start=True, stop=True).then_inc(rb_ready, 1)

            def rms(n, width=T):
                rms_cols(n, width)
                rms_rows(n, width)

            def ffn(g, k0, n, f, pos, r=None):
                def third(g, k0, h0, pos, count):
                    for j in range(count + 4):
                        if j < count:
                            products(g, k0 + j, (h_hi, h_lo), waits=(h_ready, 8 * n) if j == 0 else None)
                        else:
                            products(g, k0 + j, (hid_hi, hid_lo), ks=range(count), waits=(hid_ready, h0 + 2) if j == count else None,
                                     half=(count == THIRDS[-1] and j == count + 3))
                        if pos is not None and j in (2, 4, 6, 8):
                            mod_sum(pos + j // 2 - 1)
                rms(n if r is None else r)
                with pe.Fori(0, 2) as i:
                    third(g + 3 * i, k0, FC * f + 8 * i, None if pos is None else pos + 4 * i, 8)
                third(g, k0 + 24, FC * f + 16, None if pos is None else pos + 8, 6)

            def mixer(l, g, k0, n):
                rms(n)
                for j in range(KV_J):
                    products(g, k0 + j, (h_hi, h_lo), waits=(h_ready, 8 * n) if j == 0 else None)
                pe.wait_ge(xc_ready, l + 1)
                for w in range(2):
                    for t in range(2):
                        mm = pe.matmul(psum[:, S_BANK + 2 * w + t, :], gate_w[:, 2 * w + t, :], xc[:, t, :],
                                       start=True, stop=True)
                mm.then_inc(gates_ps, 1)
                products(g, k0 + KV_J, (h_hi, h_lo))
                products(g, k0 + SC_J, (h_hi, h_lo))
                pe.wait_ge(gates_ready, l + 1)
                pe.wait_ge(v_ready, l + 1)
                for t in range(4):
                    mm = pe.transpose(psum[:, T_BANK, t * P:(t + 1) * P], sq[:, 1, t * P:(t + 1) * P], ident[:, :])
                mm.then_inc(vtok_ps, 1)
                pe.wait_ge(q_ready, 4 * l + 4)
                pe.wait_ge(k_ready, l + 1)

                def scores(i):
                    n, kv = i // 2, i % 2
                    if i:
                        pe.wait_ge(s_ready, 8 * l + i)
                    k0, nk = max(n - 1, 0) * P, P * min(n + 1, 2)
                    for hh in range(4):
                        r = 64 * (hh % 2)
                        c0 = (hh // 2) * 2 * WINDOW
                        mm = pe.matmul(psum[:, S_BANK + hh % 2, c0:c0 + nk],
                                       qT[r:r + 64, 2 * kv + hh // 2, n * P:(n + 1) * P],
                                       k_dup[r:r + 64, kv, k0:k0 + nk], start=True, stop=True)
                    mm.then_inc(scores_ps, 1)

                def values(i):
                    n, kv = i // 2, i % 2
                    blocks = min(n + 1, 2)
                    for half in range(2):
                        e = 16 * l + 2 * i + half
                        pe.wait_ge(pn_ready, 8 * l + i + 1)
                        if i or half:
                            pe.wait_ge(pT_ready, e)
                        else:
                            pe.wait_ge(vtok_ready, l + 1)
                        for u in range(2):
                            for b in range(blocks):
                                mm = pe.transpose(psum[:, T_BANK, (2 * u + b) * P:(2 * u + b + 1) * P],
                                                  probs[:, i % 2, 2 * half + u, b * P:(b + 1) * P], ident[:, :])
                        mm.then_inc(pT_ps, 1)
                    pe.wait_ge(pT_ready, 16 * l + 2 * i + 2)
                    if i:
                        pe.wait_ge(o_taken, 8 * l + i)
                    for hh in range(4):
                        for b in range(blocks):
                            mm = pe.matmul(psum[64 * (hh % 2):64 * (hh % 2) + 64, O_BANK, (hh // 2) * P:(hh // 2 + 1) * P],
                                           v_tok[:, max(n - 1, 0) + b, 64 * kv:64 * kv + 64], probsT[:, 2 * hh + b, :],
                                           start=(b == 0), stop=(b == blocks - 1))
                    mm.then_inc(o_ps, 1)

                scores(0)
                for i in range(8):
                    if i < 3:
                        products(g, k0 + SX_J + i, (h_hi, h_lo))
                    if i < 7:
                        scores(i + 1)
                    values(i)
                pe.wait_ge(y_ready, 12 * l + 12)
                for j in range(4):
                    products(g, k0 + MIX_IN_BLOCKS + j, (h_hi, h_lo), half=(j == 3))

            pe.wait_ge(consts_ready, 1)
            pe.wait_ge(wide_ready, 1)
            for pos in range(FIRST_MODS):
                pe.wait_ge(first_landed[pos], 16 * MOD_PIECES)
                for k in range(DC):
                    mm = pe.matmul(psum[:, pos, :], cond_wide[:, k, :], first_mod(pos)[:, k, :], start=(k == 0), stop=(k == DC - 1))
                mm.then_inc(msum_ready, 1)
            with pe.Fori(0, DEPTH) as l:
                g = l * (LAYER_BLOCKS // 4)
                ffn(g, 0, 3 * l, 2 * l, LAYER_MODS * l + FIRST_MODS)
                mixer(l, g, FFN_BLOCKS, 3 * l + 1)
                ffn(g, FFN_BLOCKS + MIX_BLOCKS, 3 * l + 2, 2 * l + 1, LAYER_MODS * l + FIRST_MODS + 12)

            ch = (ch_hi, ch_lo)
            hx = (h_hi, h_lo)

            def turn(dst, src, n):
                for t in range(n):
                    mm = pe.transpose(dst[:, t * P:(t + 1) * P], src[:, t * P:(t + 1) * P], ident[:, :])
                return mm

            def gla_pre(u, glow, width):
                for d in range(2):
                    mm = pe.matmul(pre(d, width), w_decay[0:32, (4 * d + u % 4) * P:(4 * d + u % 4 + 1) * P],
                                   glow[0:32, 0:width], start=True, stop=True)
                mm.then_inc(pre_ps, 1)

            def gla_updates(u, v_src, width):
                pairs = width // P
                kt, vt = (kdT, gvt) if width == T else (kdT_c, vt_c)
                pe.wait_ge(qk_ready, u + 1)
                turn(psum[:, S_BANK, :], v_src, pairs)
                turn(psum[:, T_BANK, :], t_ring[:, 0, :], pairs)
                if u > 4:
                    pe.wait_ge(yg_ready, u - 4)
                turn(psum[:, T_BANK + 1, :], t_ring[:, 1, :], pairs).then_inc(turn_ps, 1)
                pe.wait_ge(turn_ready, u + 1)
                for d in range(2):
                    for c in range(2 * pairs):
                        r = GLA_CHUNK * (c % 2)
                        mm = pe.matmul(update(d, c, width),
                                       kt[r:r + GLA_CHUNK, d, c // 2, :], vt[r:r + GLA_CHUNK, c // 2, :], start=True, stop=True)
                    mm.then_inc(u_ps[d], 1)

            def gla_context(u):
                if len(FILLERS[u]) > 0:
                    products(G2, FILLERS[u][0], hx)
                if u:
                    pe.wait_ge(chain_ready, 2 * u)
                gla_updates(u, gv_c[:, u, :], TC)
                if u < 3:
                    gla_pre(u + 1, glow_c, TC)
                if len(FILLERS[u]) > 1:
                    products(G2, FILLERS[u][1], hx)

            def gla_tokens(h):
                u, pairs = 4 + h, T // P
                products(G2, FILLERS[u][0], hx, between=(lambda: rms_rows(R_GLA + h - 1, T, O_BANK - 1)) if h else None)
                gla_updates(u, gv[:, h % 2, :], T)
                products(G2, FILLERS[u][1], hx)
                pe.wait_ge(chain_ready, 2 * u + 1)
                for d in range(2):
                    for p in range(pairs):
                        mm = pe.matmul(psum[:, S_BANK + d, p * P:(p + 1) * P], kn[:, d, p * P:(p + 1) * P],
                                       qe[:, d, p * P:(p + 1) * P], start=True, stop=True)
                mm.then_inc(a_ps, 1)
                pe.wait_ge(chain_ready, 2 * u + 2)
                pe.wait_ge(am_ready, h + 1)
                out = psum[:, T_BANK, :]
                for p in range(pairs):
                    pe.matmul(out[:, p * P:(p + 1) * P], gvt[:, p, :], am[:, p, :], start=(p == 0), stop=False, skip_group_check=True)
                for d in range(2):
                    for c in range(2 * pairs):
                        cs = slice(c * GLA_CHUNK, (c + 1) * GLA_CHUNK)
                        mm = pe.matmul(out[:, cs], states[:, d, c, :], qe[:, d, cs], start=False,
                                       stop=(d == 1), skip_group_check=True)
                mm.then_inc(og_ps, 1)
                if h < GLA_HEADS - 1:
                    gla_pre(u + 1, krope, T)
                rms_cols(R_GLA + h, T, ssq, O_BANK)

            rms(R_FINAL1)
            rms_cols(R_CTX, TC, act_ring[:, 0, :], T_BANK)
            rms_rows(R_CTX, TC, T_BANK)
            for k in range(3):
                products(G2, CTX_K + k, ch, waits=(ctx_h_ready, 0) if k == 0 else None, width=TC)
            rms_cols(R_X1)
            products(G2, CTX_K + 3, ch, width=TC)
            rms_rows(R_X1)
            products(G2, CTX_K + 4, ch, width=TC)
            products(G2, CTX_K + 5, ch, width=TC)
            products(G2, X_K, hx, waits=(h_ready, 48))
            rms_cols(R_KVC, TC)
            products(G2, X_K + 1, hx)
            rms_rows(R_KVC, TC)
            pe.wait_ge(second_landed, 64)
            pe.wait_ge(ctx_out, 6)
            pe.wait_ge(kvn_ready, 1)
            gla_pre(0, glow_c, TC)
            for u in range(4):
                gla_context(u)
                if u == 1:
                    products(G2, KVX_FILLER, hx, between=lambda: rms_cols(R_KVX, T))
                    rms_rows(R_KVX, T)
                    pe.wait_ge(kvn_ready, 2)
                if u == 2:
                    products(G2, QX_FILLER, hx, between=lambda: rms_cols(R_QX, T))
                    rms_rows(R_QX, T)
                    pe.wait_ge(qn_ready, 1)
            pe.wait_ge(chain_ready, 8)
            pe.wait_ge(lo_ready, 4 * G2 + V_K + 1 + RAW_SLOTS)
            for k in (V_K, V_K + 1):
                pe.wait_ge(out_free[k % 2], 2 * G2 + k // 2 + 1)
            for t in range(TK // P):
                for c in range(KV_LORA_C):
                    wh, wl = (w[:, V_K % 2, c * T:(c + 1) * T] for w in (w_hi, w_lo))
                    kh, kl = (k[:, c, t * P:(t + 1) * P] for k in (kvn_hi, kvn_lo))
                    pe.matmul(psum[:, t, :], kh, wh, start=(c == 0), stop=False)
                    pe.matmul(psum[:, t, :], kh, wl, start=False, stop=False)
                    mm = pe.matmul(psum[:, t, :], kl, wh, start=False, stop=(c == 1))
            mm.then_inc(block_done, 1)
            pe.wait_ge(vals_ready, 1)

            def mla_pair(p):
                k = PAIR_K + p
                if p:
                    pe.wait_ge(m_exp, 8 * p)
                    for s in range(2):
                        pe.wait_ge(m_turned[s], 3 * (2 * p - 1))
                pe.wait_ge(lo_ready, 4 * G2 + k + 1 + RAW_SLOTS)
                for c in range(KV_LORA_C):
                    wh, wl = (w[:, k % 2, (3 + c) * 256:(3 + c) * 256 + P] for w in (w_hi, w_lo))
                    for bank, lo, hi in ((S_BANK, 0, T), (S_BANK + 1, T, TK)):
                        out = psum[:, bank, 0:hi - lo]
                        pe.matmul(out, wh, kvn_hi[:, c, lo:hi], start=(c == 0), stop=False)
                        pe.matmul(out, wh, kvn_lo[:, c, lo:hi], start=False, stop=False)
                        mm = pe.matmul(out, wl, kvn_hi[:, c, lo:hi], start=False, stop=(c == 1))
                mm.then_inc(keys_ps, 1)
                products(G2, k, (qn_hi, qn_lo), ks=range(Q_LORA_C))

            def mla_scores(h, qb):
                u = 4 * h + qb
                if u >= 2:
                    pe.wait_ge(m_exp, u - 1)
                for bank, lo, hi in ((0, 0, T), (1, T, TK)):
                    mm = pe.matmul(psum[:, 2 * (u % 2) + bank, 0:hi - lo], act_ring[0:96, h % 2, qb * P:(qb + 1) * P],
                                   keys[0:96, h % 2, lo:hi], start=True, stop=True)
                mm.then_inc(m_scores, 1)

            def mla_values(h):
                pe.wait_ge(m_norm, h + 1)

                def turn_keys(kt):
                    n = 3 * h + kt // 2
                    if n:
                        pe.wait_ge(m_turned[kt % 2], n)
                    for qb in range(4):
                        mm = pe.transpose(psum[:, S_BANK + kt % 2, qb * P:(qb + 1) * P], mprobs[:, qb, kt * P:(kt + 1) * P], ident[:, :])
                    mm.then_inc(m_turn, 1)

                turn_keys(0)
                turn_keys(1)
                r = 64 * (h % 2)
                for kt in range(6):
                    pe.wait_ge(m_turned[kt % 2], 3 * h + kt // 2 + 1)
                    if kt == 0 and h % 2 == 0 and h >= 4:
                        pe.wait_ge(o_mla_ready, h // 2 - 1)
                    pe.matmul(psum[r:r + 64, T_BANK + (h // 2) % 2, :], vals[:, kt, 64 * h:64 * h + 64], prod[:, kt % 2, :],
                              start=(kt == 0), stop=(kt == 5)).then_inc(m_pv, 1)
                    if kt < 4:
                        turn_keys(kt + 2)

            for h in range(MLA_HEADS):
                if h % 2 == 0:
                    mla_pair(h // 2)
                    pe.wait_ge(keys_ready, h // 2 + 1)
                    if h:
                        mla_values(h - 1)
                    pe.wait_ge(qh_ready, h // 2 + 1)
                    pe.wait_ge(krot_ready, 1)
                mla_scores(h, 0)
                mla_scores(h, 1)
                if h % 2:
                    mla_values(h - 1)
                mla_scores(h, 2)
                mla_scores(h, 3)
            mla_values(MLA_HEADS - 1)

            pe.wait_ge(m_exp, 32)
            gla_pre(4, krope, T)
            for j in range(2):
                products(G2, GLA_K + j, hx)
            pe.wait_ge(g_in, 1)
            pe.wait_ge(o_mla_ready, 4)
            for h in range(GLA_HEADS):
                gla_tokens(h)
            products(G2, FILLERS[7][2], hx, between=lambda: rms_rows(R_GLA + GLA_HEADS - 1, T, O_BANK - 1))

            for mp in range(4):
                k = BRANCH_K + mp
                pe.wait_ge(lo_ready, 4 * G2 + k + 1 + RAW_SLOTS)
                pe.wait_ge(out_free[k % 2], 2 * G2 + k // 2 + 1)
                pe.wait_ge(branch_ready, 1)
                pe.wait_ge(yg_ready, 4)
                if mp >= 2:
                    pe.wait_ge(merged_ready, 2 * mp - 2)
                for j in range(2):
                    for which, (bh, bl) in enumerate(((om_hi, om_lo), (yg_hi, yg_lo))):
                        out = psum[:, (2 * (k % 2) if j == 0 else S_BANK + 2 * (mp % 2)) + which, :]
                        for c in range(4):
                            at = ((j * 2 + which) * 4 + c) * P
                            wh, wl = (w[:, k % 2, at:at + P] for w in (w_hi, w_lo))
                            pe.matmul(out, wh, bh[:, c, :], start=(c == 0), stop=False)
                            pe.matmul(out, wh, bl[:, c, :], start=False, stop=False)
                            mm = pe.matmul(out, wl, bh[:, c, :], start=False, stop=(c == 3))
                mm.then_inc(block_done, 1)
            for j in range(4):
                products(G2, OUT_K + j, hx, waits=(merged_split, 0) if j == 0 else None, half=(j == 3))
            ffn(G2, FFN_K, 7, 4, None, R_X2)
            rms(R_FINAL2)

        @block.scalar
        def _(act):
            def split_hi(g, k):
                act.wait_ge(raw_landed[k % 4], 16 * g + 16 * (k // 4 + 1))
                act.wait_ge(block_done, 4 * g + k + 1)
                act.copy(w_hi[:, k % 2, :], raw[:, k % 4, :]).then_inc(hi_ready, 1)

            def squares(n, q):
                act.wait_ge(sq_used, 4 * n + q + 1)
                for t in range(2):
                    act.wait_ge(x_ready, 8 * n + 2 * q + t + 1)
                    act.activation(sq[:, t, :], x[:, 2 * q + t, :], ACT.Square).then_inc(sq_ready, 1)

            def norm(n, chunks=range(DC)):
                for c in chunks:
                    act.wait_ge(t_ready, 8 * n + c + 1)
                    act.activation(h_hi[:, c, :], t_ring[:, c % 2, :], ACT.Identity, bias=shift[:, c:c + 1]
                                   ).then_inc(h_hi_ready, 1)

            def ffn(g, k0, n, f):
                def third(g, k0, h0, count, last):
                    for j in range(count + 4):
                        k = k0 + j
                        if j < count:
                            act.wait_ge(block_done, 4 * g + k + 3)
                            act.wait_ge(hid_ready, h0 + j + 1)
                            act.activation(act_ring[:, j % 2, :], psum[:, 2 * (k % 2), :], ACT.Silu).then_inc(silu_ready, 1)
                        elif last and j == count + 3:
                            squares(n + 1, 3)
                        split_hi(g, k + 2)
                        if last and count <= j < count + 3:
                            squares(n + 1, j - count)
                norm(n)
                with act.Fori(0, 2) as i:
                    third(g + 3 * i, k0, FC * f + 8 * i, 8, False)
                third(g, k0 + 24, FC * f + 16, 6, True)

            def copies(g, k, out, done, func=ACT.Copy, free=True):
                act.wait_ge(block_done, 4 * g + k + 3)
                for t in range(2):
                    o = act.activation(out[:, t, :], psum[:, 2 * (k % 2) + t, :], func)
                    o.then_inc(done, 1)
                act.drain().then_inc(out_free[k % 2], 1)

            def mixer(l, g, k0, n):
                norm(n)
                def take(j):
                    k = k0 + j
                    if j == LX_J:
                        copies(g, k, lx, lru_in)
                        lam = par[:, LC["lam"]:LC["lam"] + 2]
                        act.wait_ge(par_ready, l + 1)
                        act.activation(small[:, 6, 0:2], lam, ACT.Abs)
                        act.drain()
                        act.activation(small[:, 6, 2:4], small[:, 6, 0:2], ACT.Exp, scale=-1.0)
                        act.drain()
                        act.activation(small[:, 6, 4:6], small[:, 6, 2:4], ACT.Ln, bias=1.0).then_inc(lam_abs, 1)
                    elif j < KV_J:
                        copies(g, k, qT[:, 2 * (j - Q_J):2 * (j - Q_J) + 2, :], q_ready)
                    elif j == KV_J:
                        act.wait_ge(k_ready, l + 1)
                        act.copy(sq[:, 1, :], psum[:, 2 * (k % 2) + 1, :]).then_inc(v_ready, 1)
                        act.drain().then_inc(out_free[k % 2], 1)
                    elif j == SC_J:
                        copies(g, k, z, lru_in)
                    elif j == SB_J:
                        copies(g, k, sb_gate, lru_in)
                    elif j == LG_J:
                        copies(g, k, lg, lru_in, ACT.Gelu_apprx_tanh)
                    split_hi(g, k + 2)

                for j in range(KV_J):
                    take(j)
                act.wait_ge(gates_ps, l + 1)
                for w, name, out in ((0, "gate_a_b", act_ring), (1, "gate_x_b", prod)):
                    for t in range(2):
                        o = act.activation(out[:, t, :], psum[:, S_BANK + 2 * w + t, :], ACT.Sigmoid,
                                           bias=par[:, LC[name] + t:LC[name] + t + 1])
                act.drain().then_inc(gates_ready, 1)
                act.wait_ge(m2_ready, 2 * l + 1)
                for t in range(2):
                    act.activation(lx[:, t, :], act_ring[:, t, :], ACT.Exp, scale=small[:, 7, t:t + 1])
                    o = act.activation(t_ring[:, t, :], act_ring[:, t, :], ACT.Tanh, scale=small[:, 7, t:t + 1])
                act.drain().then_inc(decay_ready, 1)
                act.wait_ge(m2_ready, 2 * l + 2)
                act.activation(t_ring[:, :, :], t_ring[:, :, :], ACT.Sqrt, scale=-1.0).then_inc(mult_ready, 1)
                take(KV_J)
                take(SC_J)
                act.wait_ge(vtok_ps, l + 1)
                act.copy(v_tok[:, :, :].rearrange("p a b -> p (a b)"), psum[:, T_BANK, :]).then_inc(vtok_ready, 1)

                def expo(i):
                    nk = P * min(i // 2 + 1, 2)
                    act.wait_ge(s_ready, 8 * l + i + 1)
                    for hh in range(4):
                        act.activation(probs[:, i % 2, hh, 0:nk], probs[:, i % 2, hh, 0:nk], ACT.Exp,
                                       bias=small[:, i % 2, hh:hh + 1], scale=0.125,
                                       accum_out=small[:, 2 + i % 2, hh:hh + 1])
                    act.activation(small[:, 2 + i % 2, 4:8], small[:, i % 2, 4:8], ACT.Exp)
                    act.drain().then_inc(p_ready, 1)

                def turned(i):
                    blocks = min(i // 2 + 1, 2)
                    for half in range(2):
                        act.wait_ge(pT_ps, 16 * l + 2 * i + half + 1)
                        if half == 0 and i:
                            act.wait_ge(o_ps, 8 * l + i)
                        pt = probsT[:, 4 * half:4 * half + 4, :].rearrange("p (u b) q -> p u b q", b=2)
                        ps = psum[:, T_BANK, :].rearrange("p (u b q) -> p u b q", u=2, b=2)
                        act.copy(pt[:, :, 0:blocks, :], ps[:, :, 0:blocks, :]).then_inc(pT_ready, 1)

                expo(0)
                for i in range(8):
                    if i < 3:
                        take(SX_J + i)
                    turned(i)
                    if i < 7:
                        expo(i + 1)
                for j in range(4):
                    squares(n + 1, j)
                    split_hi(g, k0 + MIX_IN_BLOCKS + j + 2)

            def evac(k, outs, done):
                act.wait_ge(block_done, 4 * G2 + k + 3)
                for t, (dst, func) in enumerate(outs):
                    w = dst.shape[-1]
                    act.activation(dst, psum[:, 2 * (k % 2) + t, 0:w], func)
                act.drain().then_inc(out_free[k % 2], 1)
                if done is not None:
                    act.drain().then_inc(done, 1)
                split_hi(G2, k + 2)

            def filler(k):
                if k in GATE_K:
                    n = GATE_K.index(k)
                    ring = gate_out_c if n < 5 else gate_out
                    if n:
                        act.wait_ge(gate_spilled, 16 * n)
                    evac(k, [(ring[:, 0, :], ACT.Copy), (ring[:, 1, :], ACT.Copy)], None)
                    act.dma_start(gate_spill[:, :].rearrange("p (a n) -> p a n", a=2)[:, :, n * T:(n + 1) * T], ring[:, :, :]
                                  ).then_inc(gate_spilled, 16)
                elif k == X_K + 1:
                    evac(k, [(krope[:, :], ACT.Copy), (qf[:, 0, :], ACT.Copy)], rg_ready)
                elif k == X_K + 2:
                    evac(k, [(qf[:, 1, :], ACT.Copy), (qf[:, 2, :], ACT.Copy)], kvf_ready)
                else:
                    hh, j = (k - GLA_K) // 2, (k - GLA_K) % 2
                    s = hh % 2
                    if hh >= 2:
                        act.wait_ge(yg_ready, hh - 1)
                    if j == 0:
                        evac(k, [(gk[:, s, :], ACT.Copy), (gq[:, s, :], ACT.Copy)], None)
                    else:
                        evac(k, [(gv[:, s, :], ACT.Copy), (gr[:, s, :], ACT.Silu)], g_in)

            def gla_logs(u, width):
                h = u % 4
                b = lambda d: par2[:, C2["b_decay"] + 4 * d + h:C2["b_decay"] + 4 * d + h + 1]
                ring = act_ring[:, :, 0:width]
                act.wait_ge(pre_ps, u + 1)
                for d in range(2):
                    act.activation(act_ring[:, d, 0:width], pre(d, width), ACT.Abs, bias=b(d))
                act.drain()
                act.activation(ring, ring, ACT.Exp, scale=-1.0)
                act.drain()
                act.activation(ring, ring, ACT.Ln, bias=1.0).then_inc(ln_ready, 1)

            def gla_decays(u, width):
                act.wait_ge(cum_ready, u + 1)
                act.activation(t_ring[:, :, 0:width], t_ring[:, :, 0:width], ACT.Exp, scale=1.0 / GATE_NORM).then_inc(exp_ready, 1)
                if width == T:
                    act.activation(kn[:, :, :], act_ring[:, :, :], ACT.Exp, scale=-1.0 / GATE_NORM)
                act.activation(prod[:, :, 0:width], act_ring[:, :, 0:width], ACT.Exp, scale=1.0 / GATE_NORM)
                act.drain().then_inc(decays_ready, 1)

            def gla_turned(u, width):
                act.wait_ge(turn_ps, u + 1)
                kt, vt = (kdT, gvt) if width == T else (kdT_c, vt_c)
                for d in range(2):
                    act.copy(kt[:, d, :, :].rearrange("p a b -> p (a b)"), psum[:, T_BANK + d, 0:width])
                act.copy(vt[:, :, :].rearrange("p a b -> p (a b)"), psum[:, S_BANK, 0:width])
                act.drain().then_inc(turn_ready, 1)

            def gla_context(u):
                gla_decays(u, TC)
                if len(FILLERS[u]) > 0:
                    filler(FILLERS[u][0])
                gla_turned(u, TC)
                if u < 3:
                    gla_logs(u + 1, TC)
                if len(FILLERS[u]) > 1:
                    filler(FILLERS[u][1])

            def gla_tokens(h):
                u = 4 + h
                gla_decays(u, T)
                filler(FILLERS[u][0])
                gla_turned(u, T)
                filler(FILLERS[u][1])
                act.wait_ge(og_ps, h + 1)
                act.activation(ssq[:, :], psum[:, T_BANK, :], ACT.Square)
                act.drain().then_inc(ssq_ready, 1)
                if h:
                    act.wait_ge(yg_ready, h)
                act.copy(o_sb[:, :], psum[:, T_BANK, :]).then_inc(og_ready, 1)
                if h < GLA_HEADS - 1:
                    gla_logs(u + 1, T)

            def mla_act():
                act.wait_ge(gate_spilled, 16 * 5)
                act.wait_ge(block_done, 4 * G2 + V_K + 3)
                for t in range(6):
                    act.copy(vals[:, t, :], psum[:, t, :])
                act.drain().then_inc(out_free[V_K % 2], 1)
                act.drain().then_inc(vals_ready, 1)
                split_hi(G2, V_K + 2)

                def take_turned(h, kt):
                    act.wait_ge(m_turn, 6 * h + kt + 1)
                    if kt >= 2:
                        act.wait_ge(m_pv, 6 * h + kt - 1)
                    act.copy(prod[:, kt % 2, :], psum[:, S_BANK + kt % 2, :]).then_inc(m_turned[0], 1)

                def take_out(p):
                    act.wait_ge(m_pv, 12 * p + 12)
                    act.copy(o_mla[:, p, :], psum[:, T_BANK + p % 2, :]).then_inc(o_mla_ready, 1)

                for h in range(MLA_HEADS):
                    if h % 2 == 0:
                        p = h // 2
                        act.wait_ge(keys_ps, p + 1)
                        for e in range(2):
                            act.copy(keys[0:64, e, 0:T], psum[64 * e:64 * e + 64, S_BANK, :])
                            act.copy(keys[0:64, e, T:TK], psum[64 * e:64 * e + 64, S_BANK + 1, 0:TC])
                        act.drain().then_inc(keys_ready, 1)
                        if p == 0:
                            split_hi(G2, PAIR_K + 2)
                    if h:
                        for kt in (0, 2, 4):
                            take_turned(h - 1, kt)
                        if h % 2 == 0:
                            take_out(h // 2 - 1)
                            split_hi(G2, PAIR_K + h // 2 + 2)
                        act.wait_ge(m_turn, 6 * h)
                    for qb in range(4):
                        act.wait_ge(m_max, 4 * h + qb + 1)
                        s = 2 * (qb % 2)
                        act.activation(mprobs[:, qb, :], psum[:, s:s + 2, :].rearrange("p a b -> p (a b)")[:, 0:TK], ACT.Exp,
                                       bias=small[:, 0, qb:qb + 1], scale=MLA_SCALE, accum_out=small[:, 1, qb:qb + 1]
                                       )
                        act.drain().then_inc(m_exp, 1)
                for kt in (0, 2, 4):
                    take_turned(MLA_HEADS - 1, kt)
                take_out(3)

            def second():
                cpy = ACT.Copy
                act.wait_ge(ctx_landed, 16)
                act.activation(cx_sq[:, :, :], cx[:, :, :], ACT.Square).then_inc(ctx_sq_ready, 1)
                squares(7, 0)
                evac(0, [(kvf_c[:, 0, :], cpy), (kvf_c[:, 1, :], cpy)], ctx_out)
                for q in range(1, 4):
                    squares(7, q)
                evac(1, [(gk_c[:, 0, :], cpy), (gk_c[:, 1, :], cpy)], ctx_out)
                evac(2, [(gk_c[:, 2, :], cpy), (gk_c[:, 3, :], cpy)], ctx_out)
                evac(3, [(gv_c[:, 0, :], cpy), (gv_c[:, 1, :], cpy)], ctx_out)
                norm(6, range(4))
                evac(4, [(gv_c[:, 2, :], cpy), (gv_c[:, 3, :], cpy)], ctx_out)
                norm(6, range(4, DC))
                act.dma_start(x_spill, x[:, :, :].rearrange("p c n -> p (c n)")).then_inc(spilled, 16)
                act.dma_start(rot, a["rot"]).then_inc(rot_landed, 16)
                evac(5, [(glow_c[:, :], cpy)], None)
                for e in range(2):
                    act.copy(keys[64:96, e, T:TK], glow_c[64:96, :])
                act.drain().then_inc(ctx_out, 1)
                act.wait_ge(spilled, 16)
                act.wait_ge(second_landed, 64)
                evac(6, [(kvf[:, 0, :], cpy), (kvf[:, 1, :], cpy)], kvf_ready)
                filler(X_K + 1)
                gla_logs(0, TC)
                for u in range(4):
                    gla_context(u)
                    if u == 1:
                        filler(KVX_FILLER)
                    if u == 2:
                        filler(QX_FILLER)
                mla_act()
                gla_logs(4, T)
                filler(GLA_K)
                filler(GLA_K + 1)
                for h in range(GLA_HEADS):
                    gla_tokens(h)
                filler(FILLERS[7][2])
                act.wait_ge(block_done, 4 * G2 + GATE_K[-1] + 3)
                act.wait_ge(gate_spilled, 16 * DC)
                for mp in range(4):
                    cs = slice(2 * mp * T, 2 * (mp + 1) * T)
                    act.dma_start(sig[:, :, cs], gate_spill[:, :].rearrange("p (a n) -> p a n", a=2)[:, :, cs]).then_inc(sig_back[mp], 16)
                for mp in range(4):
                    act.wait_ge(sig_back[mp], 16)
                    cs = slice(2 * mp * T, 2 * (mp + 1) * T)
                    act.activation(sig[:, :, cs], sig[:, :, cs], ACT.Sigmoid).then_inc(sig_ready, 1)
                    split_hi(G2, BRANCH_K + mp + 2)
                act.wait_ge(merged_split, 8)
                act.dma_start(x[:, :, :].rearrange("p c n -> p (c n)"), x_spill).then_inc(x_back, 16)
                for j in range(4):
                    squares(8, j)
                    split_hi(G2, OUT_K + j + 2)
                norm(7)

                def third(g, k0, c0, count, last):
                    for j in range(count + 4):
                        k = k0 + j
                        if j < count:
                            act.wait_ge(block_done, 4 * g + k + 3)
                            act.wait_ge(conv_ready, c0 + j + 1)
                            act.copy(gpad[:, j % 2, :], psum[:, 2 * (k % 2), :]).then_inc(g_copied, 1)
                        if not last or j < count + 2:
                            split_hi(g, k + 2)
                        if last and j >= count:
                            squares(9, j - count)
                        if j < count:
                            act.wait_ge(conv_ready, c0 + j + 3)
                            act.wait_ge(hid_ready, FC * 4 + c0 + j + 1)
                            act.activation(act_ring[:, j % 2, :], conv[:, j % 2, :], ACT.Gelu,
                                           bias=cpar[:, CONV_COLS * j + 9:CONV_COLS * j + 10]).then_inc(silu_ready, 1)
                with act.Fori(0, 2) as i:
                    third(G2 + 3 * i, FFN_K, 8 * i, 8, False)
                third(G2, FFN_K + 24, 16, 6, True)

            act.wait_ge(cond_landed, 32)
            act.activation(cond[:, :], cond[:, :], ACT.Silu).then_inc(cond_ready, 1)
            for q in range(4):
                squares(0, q)
            for k in range(2):
                split_hi(0, k)
            with act.Fori(0, DEPTH) as l:
                g = l * (LAYER_BLOCKS // 4)
                ffn(g, 0, 3 * l, 2 * l)
                mixer(l, g, FFN_BLOCKS, 3 * l + 1)
                ffn(g, FFN_BLOCKS + MIX_BLOCKS, 3 * l + 2, 2 * l + 1)
            second()

        @block.vector
        def _(dve):
            def mod_partial(pos):
                dve.tensor_copy(cond_now[:, :], cond[:, bass.ds(8 * pos, 8)])
                for piece in range(MOD_PIECES):
                    for u in range(MOD_K):
                        k = MOD_K * piece + u
                        dve.drain()
                        if u == 0:
                            dve.wait_ge(mod_landed[piece % 2], 32 * (pos - FIRST_MODS) + 16 * (piece // 2 + 1))
                        w = mod_raw[:, piece % 2, u, :]
                        if k == 0:
                            o = dve.tensor_scalar(mod_acc[:, :], w, cond_now[:, 0:1], None, ALU.mult)
                        else:
                            o = dve.scalar_tensor_tensor(mod_acc[:, :], w, cond_now[:, k:k + 1], mod_acc[:, :], ALU.mult, ALU.add)
                    if piece < MOD_PIECES - 1:
                        o.then_inc(mod_used, 1)
                o.then_inc(mod_used, 1)
                dve.drain()
                dve.tensor_copy(mod_parts[:, 0, :], mod_acc[:, :])
                dve.drain()
                dve.tensor_tensor(mod_parts[:, 1, :], mod_acc[:, :], mod_parts[:, 0, :].bitcast(F32), ALU.subtract
                                  ).then_inc(macc_ready, 1)

            def mod_take(pos, bank=O_BANK):
                dve.wait_ge(msum_ready, pos + 1)
                for t in range(4):
                    dve.tensor_tensor_reduce(mod_acc[:, t * P:(t + 1) * P], psum[:, bank, t * P:(t + 1) * P], ident[:, :],
                                             1.0, 0.0, ALU.mult, ALU.add, cond_now[:, t:t + 1])
                dve.drain()
                dve.tensor_tensor(mods[:, bass.ds(4 * pos, 4)], cond_now[:, 0:4], mod_b[:, bass.ds(4 * pos, 4)], ALU.add)
                dve.drain()

            def add_squares(n, q):
                if q == 0:
                    dve.wait_ge(sq_ready, 8 * n + 2)
                    dve.tensor_tensor(ssq[:, :], sq[:, 0, :], sq[:, 1, :], ALU.add)
                else:
                    dve.wait_ge(sq_ready, 8 * n + 2 * q + 1)
                    dve.tensor_tensor(ssq[:, :], ssq[:, :], sq[:, 0, :], ALU.add)
                    dve.drain()
                    dve.wait_ge(sq_ready, 8 * n + 2 * q + 2)
                    dve.tensor_tensor(ssq[:, :], ssq[:, :], sq[:, 1, :], ALU.add)
                o = dve.drain().then_inc(sq_used, 1)
                if q == 3:
                    dve.drain().then_inc(ssq_ready, 1)

            def rms_var(n, width=T, dim=D, bank=S_BANK):
                dve.wait_ge(cols_ready, n + 1)
                dve.tensor_scalar(var[:, 0:width // P], psum[:, bank, 0:width // P], 1.0 / dim, EPS, ALU.mult, ALU.add).then_inc(var_ready, 1)

            def rms_diag(n, width=T):
                dve.wait_ge(rstd_ready, n + 1)
                for t in range(width // P):
                    dve.tensor_scalar(diag[:, t, :], ident[:, :], rstd[:, t:t + 1], None, ALU.mult)
                dve.drain().then_inc(diag_ready, 1)

            def rms(n, width=T, dim=D, bank=S_BANK):
                rms_var(n, width, dim, bank)
                rms_diag(n, width)
                dve.wait_ge(rb_ready, n + 1)

            def norm(n, at, gain, half, r=None, cols=None):
                at_shift, at_scale, at_gate = cols or (at, at + 8, at + 16)
                dve.tensor_copy(shift[:, :], mods[:, bass.ds(at_shift, 8)])
                if not half:
                    dve.tensor_copy(gate[:, :], mods[:, bass.ds(at_gate, 8)])
                dve.tensor_scalar(a_col[:, :], mods[:, bass.ds(at_scale, 8)], 1.0, None, ALU.add)
                dve.drain()
                dve.tensor_tensor(a_col[:, :], a_col[:, :], gains[:, bass.ds(gain, 8)], ALU.mult)
                rms(n if r is None else r)

                def lo(c):
                    dve.wait_ge(h_hi_ready, 8 * n + c + 1)
                    dve.scalar_tensor_tensor(h_lo[:, c, :], t_ring[:, c % 2, :], shift[:, c:c + 1], h_hi[:, c, :].bitcast(F32),
                                             ALU.add, ALU.subtract).then_inc(h_ready, 1)
                for c in range(DC):
                    dve.scalar_tensor_tensor(t_ring[:, c % 2, :], x[:, c, :], a_col[:, c:c + 1], psum[:, S_BANK + 1, :],
                                             ALU.mult, ALU.mult).then_inc(t_ready, 1)
                    if c:
                        lo(c - 1)
                    dve.drain()
                lo(DC - 1)

            def add_to_x(g, k, q, n=None, at=None):
                dve.drain()
                if n is not None and q == 3:
                    dve.wait_ge(half_done, n if at is None else at)
                    dve.scalar_tensor_tensor(x[:, 6, :], psum[:, 2 * (k % 2), :], gate[:, 6:7], x[:, 6, :],
                                             ALU.mult, ALU.add).then_inc(x_ready, 1)
                    dve.wait_ge(sq_ready, 8 * n + 7)
                    dve.tensor_tensor(ssq[:, :], ssq[:, :], sq[:, 0, :], ALU.add)
                    dve.wait_ge(block_done, 4 * g + k + 3)
                    dve.scalar_tensor_tensor(x[:, 7, :], psum[:, 2 * (k % 2) + 1, :], gate[:, 7:8], x[:, 7, :],
                                             ALU.mult, ALU.add).then_inc(x_ready, 1)
                    dve.drain().then_inc(out_free[k % 2], 1)
                    dve.wait_ge(sq_ready, 8 * n + 8)
                    dve.tensor_tensor(ssq[:, :], ssq[:, :], sq[:, 1, :], ALU.add)
                    dve.drain().then_inc(sq_used, 1)
                    dve.drain().then_inc(ssq_ready, 1)
                    return
                dve.wait_ge(block_done, 4 * g + k + 3)
                for t in range(2):
                    m = 2 * q + t
                    o = dve.scalar_tensor_tensor(x[:, m, :], psum[:, 2 * (k % 2) + t, :], gate[:, m:m + 1], x[:, m, :],
                                                 ALU.mult, ALU.add)
                    if n is not None:
                        o.then_inc(x_ready, 1)
                dve.drain().then_inc(out_free[k % 2], 1)
                if n is not None:
                    add_squares(n, q)

            def ffn(g, k0, n, f, pos, at_gate):
                def third(g, k0, h0, pos, count, last):
                    for j in range(count + 4):
                        k = k0 + j
                        if j == 5:
                            dve.tensor_scalar(gate[:, :], mods[:, bass.ds(at_gate, 8)], 0.5, None, ALU.mult)
                        if j < count:
                            dve.wait_ge(silu_ready, h0 + j + 1)
                            dve.tensor_tensor(prod[:, j % 2, :], act_ring[:, j % 2, :], psum[:, 2 * (k % 2) + 1, :],
                                              ALU.mult).then_inc(out_free[k % 2], 1)
                            dve.drain()
                            dve.tensor_copy(hid_hi[:, j, :], prod[:, j % 2, :])
                            dve.drain()
                            dve.tensor_tensor(hid_lo[:, j, :], prod[:, j % 2, :], hid_hi[:, j, :].bitcast(F32),
                                              ALU.subtract).then_inc(hid_ready, 1)
                        else:
                            add_to_x(g, k, j - count, n + 1 if last else None)
                        if j in (2, 4, 6, 8):
                            mod_take(pos + j // 2 - 1)
                        if j in (0, 2, 4, 6):
                            mod_partial(pos + j // 2)
                with dve.Fori(0, 2) as i:
                    third(g + 3 * i, k0, FC * f + 8 * i, pos + 4 * i, 8, False)
                third(g, k0 + 24, FC * f + 16, pos + 8, 6, True)

            def split_y(c, src, done):
                dve.tensor_copy(h_hi[:, c, :], src)
                dve.drain()
                dve.tensor_tensor(h_lo[:, c, :], src, h_hi[:, c, :].bitcast(F32), ALU.subtract).then_inc(done, 1)

            def mixer(l, g, k0, n):
                kv, kx = k0 + KV_J, k0 + SX_J
                pcol = lambda name, j: par[:, LC[name] + j:LC[name] + j + 1]
                dve.wait_ge(lru_in, 8 * l + 2)
                for t in range(2):
                    dve.tensor_scalar(xc[:, t, :], lx[:, t, :], pcol("lru_w", 3 * 2 + t), pcol("lru_b", t), ALU.mult, ALU.add)
                for s in range(1, 4):
                    dve.drain()
                    for t in range(2):
                        dve.scalar_tensor_tensor(xc[:, t, s:T], lx[:, t, 0:T - s], pcol("lru_w", (3 - s) * 2 + t), xc[:, t, s:T],
                                                 ALU.mult, ALU.add)
                dve.drain().then_inc(xc_ready, 1)
                dve.wait_ge(lam_abs, l + 1)
                lam = par[:, LC["lam"]:LC["lam"] + 2]
                dve.tensor_scalar(small[:, 7, 2:4], lam, -1.0, 0.0, ALU.mult, ALU.max)
                dve.drain()
                dve.tensor_tensor(small[:, 7, 4:6], small[:, 7, 2:4], small[:, 6, 4:6], ALU.add)
                dve.drain()
                dve.tensor_scalar(small[:, 7, 0:2], small[:, 7, 4:6], -8.0, None, ALU.mult)
                dve.drain().then_inc(m2_ready, 1)
                dve.wait_ge(decay_ready, l + 1)
                dve.tensor_tensor(sq[:, :, :], lx[:, :, :], lx[:, :, :], ALU.mult)
                dve.drain()
                dve.scalar_tensor_tensor(t_ring[:, :, :], sq[:, :, :], 1.0, t_ring[:, :, :], ALU.add, ALU.mult)
                dve.drain().then_inc(m2_ready, 1)
                dve.tensor_tensor(prod[:, :, :], prod[:, :, :], xc[:, :, :], ALU.mult)
                dve.wait_ge(block_done, 4 * g + kv + 3)
                ps = psum[:, 2 * (kv % 2), :]
                for e in range(2):
                    for r in range(2):
                        dve.tensor_copy(k_dup[64 * r:64 * r + 64, e, :], ps[64 * e:64 * e + 64, :])
                dve.drain().then_inc(k_ready, 1)
                dve.wait_ge(mult_ready, l + 1)
                dve.memset(t_ring[:, :, 0:1], 1.0)

                def recur():
                    dve.drain()
                    dve.tensor_tensor(prod[:, :, :], prod[:, :, :], t_ring[:, :, :], ALU.mult)
                    dve.drain()
                    for t in range(2):
                        dve.tensor_tensor_scan(xc[:, t, :], lx[:, t, :], prod[:, t, :], 0.0, ALU.mult, ALU.add)

                def conv_z():
                    dve.wait_ge(lru_in, 8 * l + 4)
                    dve.wait_ge(block_done, 4 * g + kx + 3)
                    for t in range(2):
                        dve.tensor_tensor(z[:, t, :], z[:, t, :], psum[:, 2 * (kx % 2) + t, :], ALU.mult)
                    dve.drain().then_inc(out_free[kx % 2], 1)
                    for t in range(2):
                        dve.tensor_scalar(sq[:, t, :], z[:, t, :], pcol("sc_w", 2 * 2 + t), None, ALU.mult)
                    for s in range(1, 3):
                        dve.drain()
                        for t in range(2):
                            dve.scalar_tensor_tensor(sq[:, t, s:T], z[:, t, 0:T - s], pcol("sc_w", (2 - s) * 2 + t), sq[:, t, s:T],
                                                     ALU.mult, ALU.add)
                    dve.drain()

                def gate_z():
                    dve.wait_ge(lru_in, 8 * l + 6)
                    dve.tensor_tensor(z[:, :, :], sq[:, :, :], sb_gate[:, :, :], ALU.mult)
                    dve.drain()

                def gate_lru():
                    dve.wait_ge(lru_in, 8 * l + 8)
                    dve.tensor_tensor(lg[:, :, :], lg[:, :, :], xc[:, :, :], ALU.mult)
                    dve.drain()

                def bias_max(i):
                    n, kv = i // 2, i % 2
                    nk = P * min(n + 1, 2)
                    dve.wait_ge(scores_ps, 8 * l + i + 1)
                    if i >= 2:
                        dve.wait_ge(pT_ps, 16 * l + 2 * (i - 2) + 2)
                    for hh in range(4):
                        c0 = (hh // 2) * 2 * WINDOW
                        dve.scalar_tensor_tensor(probs[:, i % 2, hh, 0:nk], alibi[:, 2 * WINDOW - nk:], -8.0 * alibi_slope(4 * kv + hh),
                                                 psum[:, S_BANK + hh % 2, c0:c0 + nk], ALU.mult, ALU.add)
                    dve.drain()
                    mx, sink = small[:, 4, 0:4], par[:, LC["sink"] + 4 * kv:LC["sink"] + 4 * kv + 4]
                    dve.tensor_reduce(mx, probs[:, i % 2, :, 0:nk], AX.X, ALU.max)
                    dve.drain()
                    dve.scalar_tensor_tensor(small[:, 4, 4:8], mx, 0.125, sink, ALU.mult, ALU.max)
                    dve.drain()
                    dve.tensor_scalar(small[:, i % 2, 0:4], small[:, 4, 4:8], -1.0, None, ALU.mult)
                    dve.tensor_tensor(small[:, i % 2, 4:8], sink, small[:, 4, 4:8], ALU.subtract)
                    dve.drain().then_inc(s_ready, 1)

                def normalise(i):
                    nk = P * min(i // 2 + 1, 2)
                    dve.wait_ge(p_ready, 8 * l + i + 1)
                    dve.tensor_tensor(small[:, 5, 0:4], small[:, 2 + i % 2, 0:4], small[:, 2 + i % 2, 4:8], ALU.add)
                    dve.drain()
                    dve.reciprocal(small[:, 5, 4:8], small[:, 5, 0:4])
                    dve.drain()
                    for hh in range(4):
                        dve.tensor_scalar(probs[:, i % 2, hh, 0:nk], probs[:, i % 2, hh, 0:nk], small[:, 5, 4 + hh:5 + hh],
                                          None, ALU.mult)
                    dve.drain().then_inc(pn_ready, 1)

                def take_out(i):
                    n, kv = i // 2, i % 2
                    dve.wait_ge(o_ps, 8 * l + i + 1)
                    o = psum[:, O_BANK, 0:2 * P].rearrange("p (c q) -> p c q", c=2)
                    if i < EARLY:
                        dve.tensor_copy(qT[:, 2 * kv:2 * kv + 2, n * P:(n + 1) * P], o)
                        dve.drain().then_inc(o_taken, 1)
                    else:
                        split_out(i, o)
                        dve.drain().then_inc(o_taken, 1)

                def split_out(i, o):
                    n, kv = i // 2, i % 2
                    hi, lo = (t[:, 2 * kv:2 * kv + 2, n * P:(n + 1) * P] for t in (h_hi, h_lo))
                    dve.tensor_copy(hi, o)
                    dve.drain()
                    dve.tensor_tensor(lo, o, hi.bitcast(F32), ALU.subtract).then_inc(y_ready, 1)

                def split_early(i):
                    n, kv = i // 2, i % 2
                    split_out(i, qT[:, 2 * kv:2 * kv + 2, n * P:(n + 1) * P])

                EARLY = 3
                bias_max(0)
                recur()
                normalise(0)
                bias_max(1)
                take_out(0)
                normalise(1)
                conv_z()
                bias_max(2)
                take_out(1)
                normalise(2)
                gate_z()
                bias_max(3)
                take_out(2)
                normalise(3)
                dve.wait_ge(block_done, 4 * g + k0 + LG_J + 3)
                bias_max(4)
                take_out(3)
                for i in range(4, 8):
                    if i > 4:
                        take_out(i - 1)
                    normalise(i)
                    if i < 7:
                        bias_max(i + 1)
                    if i == 4:
                        gate_lru()
                    if i < 7:
                        split_early(i - 4)
                        split_y(4 + i - 4, (lg[:, 0, :], lg[:, 1, :], z[:, 0, :])[i - 4], y_ready)
                    else:
                        split_y(7, z[:, 1, :], y_ready)
                take_out(7)
                for j in range(4):
                    add_to_x(g, k0 + MIX_IN_BLOCKS + j, j, n + 1)

            def split(hi, lo, src):
                dve.tensor_copy(hi, src)
                dve.drain()
                return dve.tensor_tensor(lo, src, hi.bitcast(F32), ALU.subtract)

            def norm_split(r, src, hi, lo, gain, chunks, width, dim, done, meanwhile=None):
                for c in range(chunks):
                    if c == 0:
                        dve.tensor_tensor(ssq[:, 0:width], src[:, 0, :], src[:, 0, :], ALU.mult)
                    else:
                        dve.drain()
                        dve.tensor_tensor(sq[:, 1, 0:width], src[:, c, :], src[:, c, :], ALU.mult)
                        dve.drain()
                        dve.tensor_tensor(ssq[:, 0:width], ssq[:, 0:width], sq[:, 1, 0:width], ALU.add)
                dve.drain().then_inc(ssq_ready, 1)
                rms_var(r, width, dim)
                rms_diag(r, width)
                if meanwhile is not None:
                    gla_cumulate(meanwhile, TC)
                dve.wait_ge(rb_ready, r + 1)
                for c in range(chunks):
                    dve.scalar_tensor_tensor(src[:, c, :], src[:, c, :], par2[:, gain + c:gain + c + 1],
                                             psum[:, S_BANK + 1, 0:width], ALU.mult, ALU.mult)
                dve.drain()
                split(hi, lo, src)
                dve.drain().then_inc(done, 1)

            def whole_norm(gain, chunks=range(DC)):
                for c in chunks:
                    dve.scalar_tensor_tensor(x[:, c, :], x[:, c, :], gains[:, gain + c:gain + c + 1], psum[:, S_BANK + 1, :],
                                             ALU.mult, ALU.mult).then_inc(x_ready, 1)

            def final_and_ctx_norm():
                dve.tensor_scalar(a_col[:, :], mods[:, 80:88], 1.0, None, ALU.add)
                rms_var(R_FINAL1)
                dve.drain()
                dve.tensor_tensor(a_col[:, :], a_col[:, :], gains[:, 56:64], ALU.mult)
                rms_diag(R_FINAL1)
                dve.wait_ge(ctx_landed, 16)
                dve.wait_ge(ctx_sq_ready, 1)
                dve.tensor_reduce(act_ring[:, 0, 0:TC], cx_sq[:, :, :].rearrange("p c t -> p t c"), AX.X, ALU.add)
                dve.drain().then_inc(ssq_ready, 1)
                dve.wait_ge(rb_ready, R_FINAL1 + 1)
                rms_var(R_CTX, TC, D, T_BANK)
                whole_norm(48, range(2))
                rms_diag(R_CTX, TC)
                whole_norm(48, (2,))
                dve.wait_ge(rb_ready, R_CTX + 1)
                for c in range(DC):
                    dve.drain()
                    dve.scalar_tensor_tensor(cx[:, c, :], cx[:, c, :], a_col[:, c:c + 1], psum[:, T_BANK + 1, 0:TC], ALU.mult, ALU.mult)
                    dve.drain()
                    dve.tensor_scalar(ch_hi[:, c, :], cx[:, c, :], mods[:, 72 + c:73 + c], None, ALU.add)
                    dve.drain()
                    dve.scalar_tensor_tensor(ch_lo[:, c, :], cx[:, c, :], mods[:, 72 + c:73 + c], ch_hi[:, c, :].bitcast(F32),
                                             ALU.add, ALU.subtract).then_inc(ctx_h_ready, 1)
                whole_norm(48, range(3, DC))

            def gla_cumulate(u, width):
                h, chunks = u % 4, width // GLA_CHUNK
                b = lambda d: par2[:, C2["b_decay"] + 4 * d + h:C2["b_decay"] + 4 * d + h + 1]
                W = slice(0, width)
                dve.wait_ge(ln_ready, u + 1)
                for d in range(2):
                    dve.tensor_scalar(t_ring[:, d, W], pre(d, width), b(d), 0.0, ALU.add, ALU.min)
                dve.drain()
                dve.tensor_tensor(prod[:, :, W], t_ring[:, :, W], act_ring[:, :, W], ALU.subtract)
                dve.drain()
                dve.tensor_tensor_scan(act_ring[:, 0, W], resets[:, 0, W], prod[:, 0, W], 0.0, ALU.mult, ALU.add)
                back = slice(width - 1, None, -1)
                dve.tensor_tensor_scan(act_ring[:, 1, back], resets[:, 1, back], prod[:, 1, back], 0.0, ALU.mult, ALU.add)
                dve.drain()
                for d in range(2):
                    cum = act_ring[:, d, W].rearrange("p (c t) -> p c t", t=GLA_CHUNK)
                    total = cum[:, :, GLA_CHUNK - 1:GLA_CHUNK] if d == 0 else cum[:, :, 0:1]
                    dve.tensor_tensor(t_ring[:, d, W].rearrange("p (c t) -> p c t", t=GLA_CHUNK),
                                      total.broadcast_to([P, chunks, GLA_CHUNK]), cum, ALU.subtract)
                dve.drain().then_inc(cum_ready, 1)

            def gla_weigh(u, width, ks, qs):
                W = slice(0, width)
                dve.wait_ge(exp_ready, u + 1)
                for d in range(2):
                    dve.tensor_tensor(t_ring[:, d, W], t_ring[:, d, W], ks, ALU.mult)
                dve.drain().then_inc(qk_ready, 1)
                dve.wait_ge(decays_ready, u + 1)
                if qs is not None:
                    for d in range(2):
                        dve.scalar_tensor_tensor(qe[:, d, :], qs, GLA_QSCALE, prod[:, d, :], ALU.mult, ALU.mult)
                        dve.tensor_tensor(kn[:, d, :], kn[:, d, :], ks, ALU.mult)
                    dve.drain()

            def gla_chain(u, width):
                h, chunks, full = u % 4, width // GLA_CHUNK, width == T
                for d in range(2):
                    dve.wait_ge(u_ps[d if full else 1], u + 1)
                    order = list(range(chunks)) if d == 0 else list(range(chunks))[::-1]
                    last = s0[:, 4 * d + h, :]
                    if full:
                        dve.tensor_copy(states[:, d, order[0], :], last)
                        dve.drain()
                    for i, c in enumerate(order):
                        kv = update(d, c, width)
                        e = c * GLA_CHUNK + (GLA_CHUNK - 1 if d == 0 else 0)
                        if full:
                            if i + 1 < chunks:
                                dve.scalar_tensor_tensor(states[:, d, order[i + 1], :], states[:, d, c, :], prod[:, d, e:e + 1], kv,
                                                         ALU.mult, ALU.add)
                                dve.drain()
                        elif i == 0:
                            dve.tensor_copy(last, kv)
                            dve.drain()
                        else:
                            dve.scalar_tensor_tensor(last, last, prod[:, d, e:e + 1], kv, ALU.mult, ALU.add)
                            dve.drain()
                    dve.drain().then_inc(chain_ready, 1)

            def gla_context(u):
                if u < 2:
                    gla_cumulate(u, TC)
                gla_weigh(u, TC, gk_c[:, u, :], None)
                gla_chain(u, TC)

            def gla_out(h):
                dve.wait_ge(rb_ready, R_GLA + h + 1)
                dve.wait_ge(og_ready, h + 1)
                dve.scalar_tensor_tensor(y_gla[:, h, :], o_sb[:, :], par2[:, C2["gla_norm"]:C2["gla_norm"] + 1],
                                         psum[:, O_BANK, :], ALU.mult, ALU.mult)
                dve.drain()
                dve.tensor_tensor(y_gla[:, h, :], y_gla[:, h, :], gr[:, h % 2, :], ALU.mult)
                dve.drain().then_inc(yg_ready, 1)

            def gla_tokens(h):
                u = 4 + h
                gla_chain(u, T)
                dve.wait_ge(a_ps, h + 1)
                for d, out in ((0, am[:, :, :]), (1, t_ring[:, 0, :].rearrange("p (a b) -> p a b", b=P))):
                    dve.tensor_tensor(out, psum[:, S_BANK + d, :].rearrange("p (a b) -> p a b", b=P),
                                      masks[:, d:d + 1, :].broadcast_to([P, 4, P]), ALU.mult)
                dve.drain()
                dve.tensor_tensor(am[:, :, :], am[:, :, :], t_ring[:, 0, :].rearrange("p (a b) -> p a b", b=P), ALU.add
                                  ).then_inc(am_ready, 1)
                dve.drain()
                last = h == GLA_HEADS - 1
                if last:
                    for c in range(4):
                        split(om_hi[:, c, :], om_lo[:, c, :], o_mla[:, c, :])
                    dve.drain()
                rms_var(R_GLA + h, T, P, O_BANK)
                rms_diag(R_GLA + h)
                if last:
                    for c in range(GLA_HEADS - 1):
                        split(yg_hi[:, c, :], yg_lo[:, c, :], y_gla[:, c, :])
                    gla_out(h)
                    split(yg_hi[:, h, :], yg_lo[:, h, :], y_gla[:, h, :])
                    dve.drain().then_inc(branch_ready, 1)
                else:
                    gla_cumulate(u + 1, T)
                    gla_out(h)
                    gla_weigh(u + 1, T, gk[:, (h + 1) % 2, :], gq[:, (h + 1) % 2, :])

            def rotate(dst, src, src2):
                dve.tensor_tensor(t_ring[64:96, 0, :], src, rot[64:96, :], ALU.mult)
                dve.tensor_tensor(t_ring[64:96, 1, :], src2, rot[96:128, :], ALU.mult)
                dve.drain()
                dve.tensor_tensor(dst, t_ring[64:96, 0, :], t_ring[64:96, 1, :], ALU.add)
                dve.drain()

            def mla():
                dve.wait_ge(rot_landed, 16)
                for e in range(2):
                    rotate(keys[64:96, e, 0:T], krope[64:96, :], krope[96:128, :])
                dve.drain().then_inc(krot_ready, 1)

                def row_max(h, qb):
                    u = 4 * h + qb
                    dve.wait_ge(m_scores, u + 1)
                    s = 2 * (u % 2)
                    dve.tensor_reduce(small[:, 2, qb:qb + 1], psum[:, s:s + 2, :].rearrange("p a b -> p (a b)")[:, 0:TK], AX.X, ALU.max)
                    dve.drain()
                    dve.tensor_scalar(small[:, 0, qb:qb + 1], small[:, 2, qb:qb + 1], -MLA_SCALE, None, ALU.mult).then_inc(m_max, 1)

                def take_turned(h, kt):
                    dve.wait_ge(m_turn, 6 * h + kt + 1)
                    if kt >= 2:
                        dve.wait_ge(m_pv, 6 * h + kt - 1)
                    dve.tensor_copy(prod[:, kt % 2, :], psum[:, S_BANK + kt % 2, :]).then_inc(m_turned[1], 1)

                for h in range(MLA_HEADS):
                    if h % 2 == 0:
                        k = PAIR_K + h // 2
                        dve.wait_ge(block_done, 4 * G2 + k + 3)
                        for e in range(2):
                            ps = psum[:, 2 * (k % 2) + e, :]
                            dve.tensor_copy(act_ring[0:64, e, :], ps[0:64, :])
                            rotate(act_ring[64:96, e, :], ps[64:96, :], ps[96:128, :])
                            if h and e == 0:
                                take_turned(h - 1, 1)
                        dve.drain().then_inc(out_free[k % 2], 1)
                        dve.drain().then_inc(qh_ready, 1)
                    if h and h % 2 == 0:
                        for kt in (3, 5):
                            take_turned(h - 1, kt)
                    row_max(h, 0)
                    row_max(h, 1)
                    if h % 2:
                        for kt in (1, 3, 5):
                            take_turned(h - 1, kt)
                    row_max(h, 2)
                    row_max(h, 3)
                    dve.wait_ge(m_exp, 4 * h + 4)
                    dve.reciprocal(small[:, 3, 0:4], small[:, 1, 0:4])
                    dve.drain()
                    for qb in range(4):
                        dve.tensor_scalar(mprobs[:, qb, :], mprobs[:, qb, :], small[:, 3, qb:qb + 1], None, ALU.mult)
                    dve.drain().then_inc(m_norm, 1)
                for kt in (1, 3, 5):
                    take_turned(MLA_HEADS - 1, kt)

            def merge():
                for mp in range(4):
                    k = BRANCH_K + mp
                    dve.wait_ge(sig_ready, mp + 1)
                    dve.wait_ge(block_done, 4 * G2 + k + 3)
                    for j in range(2):
                        bank = 2 * (k % 2) if j == 0 else S_BANK + 2 * (mp % 2)
                        for which in range(2):
                            dve.tensor_tensor(t_ring[:, which, :], sig[:, which, (2 * mp + j) * T:(2 * mp + j + 1) * T], psum[:, bank + which, :], ALU.mult)
                        dve.drain()
                        dve.tensor_tensor(merged[:, 2 * mp + j, :], t_ring[:, 0, :], t_ring[:, 1, :], ALU.add)
                        dve.drain().then_inc(merged_ready, 1)
                    dve.drain().then_inc(out_free[k % 2], 1)
                    for c in (2 * mp, 2 * mp + 1):
                        split(h_hi[:, c, :], h_lo[:, c, :], merged[:, c, :]).then_inc(merged_split, 1)

            def conv_ffn():
                def third(g, k0, c0, count, last):
                    cols = CONV_COLS * count
                    dve.tensor_copy(cpar[:, 0:cols], par2[:, bass.ds(C2["conv"] + CONV_COLS * c0, cols)])
                    for j in range(count + 4):
                        k = k0 + j
                        if j < count:
                            tap = lambda i: cpar[:, CONV_COLS * j + i:CONV_COLS * j + i + 1]
                            src = gpad[:, j % 2, :].rearrange("p (r c) -> p r c", c=GRID_W)
                            dst = conv[:, j % 2, :].rearrange("p (r c) -> p r c", c=GRID_W)
                            rows = T // GRID_W
                            dve.drain()
                            dve.wait_ge(g_copied, c0 + j + 1)
                            dve.tensor_scalar(conv[:, j % 2, :], gpad[:, j % 2, :], tap(4), None, ALU.mult)
                            for dy in (-1, 0, 1):
                                for dx in (-1, 0, 1):
                                    if dy or dx:
                                        rs, cs = slice(max(0, -dy), rows - max(0, dy)), slice(max(0, -dx), GRID_W - max(0, dx))
                                        rr = slice(max(0, dy), rows - max(0, -dy))
                                        cc = slice(max(0, dx), GRID_W - max(0, -dx))
                                        dve.drain()
                                        dve.scalar_tensor_tensor(dst[:, rs, cs], src[:, rr, cc], tap(3 * (dy + 1) + dx + 1),
                                                                 dst[:, rs, cs], ALU.mult, ALU.add)
                            dve.drain().then_inc(conv_ready, 1)
                            dve.wait_ge(silu_ready, FC * 4 + c0 + j + 1)
                            dve.tensor_tensor(prod[:, j % 2, :], act_ring[:, j % 2, :], psum[:, 2 * (k % 2) + 1, :],
                                              ALU.mult).then_inc(out_free[k % 2], 1)
                            dve.drain()
                            split(hid_hi[:, j, :], hid_lo[:, j, :], prod[:, j % 2, :]).then_inc(hid_ready, 1)
                        else:
                            add_to_x(g, k, j - count, 9 if last else None, 8)
                with dve.Fori(0, 2) as i:
                    third(G2 + 3 * i, FFN_K, 8 * i, 8, False)
                third(G2, FFN_K + 24, 16, 6, True)

            def second():
                final_and_ctx_norm()
                for q in range(4):
                    add_squares(7, q)
                norm(6, None, 56, False, R_X1, (192, 200, 184))
                dve.wait_ge(ctx_out, 1)
                dve.wait_ge(second_landed, 64)
                norm_split(R_KVC, kvf_c[:, :, :], kvn_hi[:, :, T:TK], kvn_lo[:, :, T:TK], C2["kv_norm"], 2, TC, 2 * P, kvn_ready)
                for u in range(4):
                    gla_context(u)
                    if u == 1:
                        dve.wait_ge(kvf_ready, 2)
                        norm_split(R_KVX, kvf[:, :, :], kvn_hi[:, :, 0:T], kvn_lo[:, :, 0:T], C2["kv_norm"], 2, T, 2 * P, kvn_ready, 2)
                    if u == 2:
                        dve.wait_ge(rg_ready, 1)
                        norm_split(R_QX, qf[:, :, :], qn_hi[:, :, :], qn_lo[:, :, :], C2["q_norm"], 3, T, 3 * P, qn_ready, 3)
                mla()
                gla_cumulate(4, T)
                gla_weigh(4, T, gk[:, 0, :], gq[:, 0, :])
                for h in range(GLA_HEADS):
                    gla_tokens(h)
                merge()
                dve.wait_ge(x_back, 16)
                for j in range(4):
                    add_to_x(G2, OUT_K + j, j, 8, 7)
                norm(7, None, 64, False, R_X2, (88, 168, 176))
                conv_ffn()
                rms(R_FINAL2)
                whole_norm(72)

            dve.drain().then_inc(mod_used, 2)
            dve.drain().then_inc(conv_ready, 2)
            dve.drain().then_inc(out_free[0], 1)
            dve.drain().then_inc(out_free[1], 1)
            dve.drain().then_inc(sq_used, 1)
            dve.drain().then_inc(hid_ready, 2)
            dve.wait_ge(cond_ready, 1)
            dve.wait_ge(consts_ready, 1)
            dve.tensor_copy(ones_r[:, :], ones[:, :])
            for k in range(DC):
                dve.tensor_scalar(cond_wide[:, k, :], ones[:, :], cond[:, k:k + 1], None, ALU.mult)
            dve.drain().then_inc(wide_ready, 1)
            dve.wait_ge(x_landed, 16)
            dve.drain().then_inc(x_ready, 8)
            for q in range(4):
                add_squares(0, q)
            for pos in range(FIRST_MODS):
                if pos == 0:
                    dve.wait_ge(consts_landed, 16 * 5)
                mod_take(pos, pos)
            with dve.Fori(0, DEPTH) as l:
                g = l * (LAYER_BLOCKS // 4)
                at = 4 * LAYER_MODS * l
                dve.tensor_copy(par[:, :], layer_par[:, bass.ds(NLP * l, NLP)])
                dve.tensor_copy(gate_w[:, :, :].rearrange("p a b -> p (a b)"), gates_all[:, bass.ds(4 * P * l, 4 * P)])
                dve.drain().then_inc(par_ready, 1)
                norm(3 * l, at, 24 * l, True)
                ffn(g, 0, 3 * l, 2 * l, LAYER_MODS * l + FIRST_MODS, at + 16)
                norm(3 * l + 1, at + 24, 24 * l + 8, False)
                mixer(l, g, FFN_BLOCKS, 3 * l + 1)
                norm(3 * l + 2, at + 48, 24 * l + 16, True)
                ffn(g, FFN_BLOCKS + MIX_BLOCKS, 3 * l + 2, 2 * l + 1, LAYER_MODS * l + FIRST_MODS + 12, at + 64)
            second()


def columns(np, v):
    return np.asarray(v).reshape(-1, P).T


def pair_blocks(np, w):
    return w.reshape(KC, P, -1, BLOCK_COLS).transpose(2, 1, 0, 3).reshape(-1, P, BLOCK)


def ffn_blocks(np, gu, down, first=0, second=D_FF):
    both = np.stack([gu[:, first:first + D_FF].reshape(D, FC, P), gu[:, second:second + D_FF].reshape(D, FC, P)], 2)
    ups = pair_blocks(np, both.reshape(D, FC * BLOCK_COLS))
    out, at = [], 0
    for n in THIRDS:
        rows = down[at * P:(at + n) * P]
        if n < KC:
            rows = np.concatenate([rows, np.zeros(((KC - n) * P, D), rows.dtype)], 0)
        out += [ups[at:at + n], pair_blocks(np, rows)]
        at += n
    return out


def second_blocks(np, i):
    w = i["w_in_2"][0]
    at, parts = 0, {}
    for name, n in (("q", 384), ("kv", 256), ("rope", 32), ("gq", 512), ("gk", 512), ("gv", 512), ("gr", 512), ("glow", 32), ("gate", 2048)):
        parts[name] = w[:, at:at + n]
        at += n
    partner = np.concatenate([np.arange(8, 16), np.arange(0, 8), np.arange(24, 32), np.arange(16, 24)])
    rg = np.concatenate([parts["glow"], parts["glow"], parts["rope"], parts["rope"][:, partner]], 1)
    blocks = [pair_blocks(np, np.concatenate([parts["kv"], parts["gk"], parts["gv"], rg, rg], 1)),
              pair_blocks(np, np.concatenate([parts["kv"], rg, parts["q"]], 1))]
    ukv = i["w_ukv_2"][0].reshape(2, P, MLA_HEADS, 2, 64)
    gates = parts["gate"].reshape(D, 2, DC, P)
    gates = [pair_blocks(np, gates[:, :, c].reshape(D, 2 * P)) for c in range(DC)]
    blocks += gates[:5]
    v = np.zeros((P, 4, T), w.dtype)
    v[:, 0:2] = ukv[:, :, :, 1].reshape(2, P, T).transpose(1, 0, 2)
    blocks.append(v.reshape(1, P, BLOCK))
    uq = i["w_uq_2"][0].reshape(3, P, MLA_HEADS, NOPE + ROPE)
    for p in range(4):
        b = np.zeros((P, KC, 2, P), w.dtype)
        for e in range(2):
            q = uq[:, :, 2 * p + e]
            b[:, 0:3, e, :] = np.concatenate([q, q[:, :, NOPE:][:, :, partner]], 2).transpose(1, 0, 2)
        b[:, 3:5, 0, :] = ukv[:, :, 2 * p:2 * p + 2, 0].reshape(2, P, P).transpose(1, 0, 2)
        blocks.append(b.reshape(1, P, BLOCK))
    for h in range(GLA_HEADS):
        blocks.append(pair_blocks(np, np.concatenate([parts[n][:, h * P:(h + 1) * P] for n in ("gk", "gq", "gv", "gr")], 1)))
    blocks += gates[5:]
    branches = [i[n][0].reshape(4, P, DC, P) for n in ("w_br_mla_2", "w_br_gla_2")]
    for mp in range(4):
        blocks.append(np.stack([branches[which][:, :, 2 * mp + j].transpose(1, 0, 2) for j in range(2) for which in range(2)], 1)
                      .reshape(1, P, BLOCK))
    blocks.append(pair_blocks(np, i["w_out_2"][0]))
    return blocks + ffn_blocks(np, i["w_up_2"][0], i["w_down_2"][0], first=D_FF, second=0)


def second_tables(np, i):
    a = {}
    a["ctxT"] = i["ctx_2"].reshape(TC, DC, P).transpose(2, 1, 0).reshape(P, DC * TC)
    conv = np.concatenate([i["conv_w_2"][0].reshape(9, D_FF), i["conv_b_2"]], 0).reshape(CONV_COLS, FC, P).transpose(2, 1, 0)
    a["par2"] = np.concatenate([columns(np, i["q_norm_g_2"]), columns(np, i["kv_norm_g_2"]), columns(np, i["gla_norm_g_2"]),
                                columns(np, i["gla_b_decay_2"]), conv.reshape(P, FC * CONV_COLS)], 1)
    wd = np.zeros((2, 16, 2, 512), i["x"].dtype)
    for d in range(2):
        wd[d, :, d] = i["gla_w_decay_2"][0, d]
    a["w_decay"] = wd.reshape(32, 1024)
    t = np.arange(P)
    same = t[:, None] // GLA_CHUNK == t[None] // GLA_CHUNK
    a["masks"] = np.concatenate([same & (t[:, None] <= t[None]), same & (t[:, None] >= t[None])], 1).astype(np.float32)
    tt = np.arange(T) % GLA_CHUNK
    a["resets"] = np.broadcast_to(np.concatenate([tt != 0, tt != GLA_CHUNK - 1])[None], (P, 2 * T)).astype(np.float32)
    tok = np.arange(T)
    inv = (np.float32(10000.0) ** (-np.arange(0, 16, 2, dtype=np.float32) / np.float32(16))).astype(np.float32)
    ang = [(p.astype(np.float32)[None] * inv[:, None]) for p in (tok // GRID_W, tok % GRID_W)]
    rot = np.zeros((P, T), np.float32)
    for ax in range(2):
        for half in range(2):
            r = 64 + 16 * ax + 8 * half
            rot[r:r + 8] = np.cos(ang[ax])
            rot[32 + r:40 + r] = np.sin(ang[ax]) * (1 if half else -1)
    a["rot"] = rot
    return a


def layout(np, i):
    a = {}
    a["xT"] = np.asarray(i["x"]).reshape(T, DC, P).transpose(2, 1, 0).reshape(P, DC * T)
    blocks = []
    for l in range(DEPTH):
        blocks += ffn_blocks(np, i["w_ffn1_gu"][l], i["w_ffn1_down"][l])
        w = i["w_in"][l]
        blocks.append(pair_blocks(np, np.concatenate([w[:, 768:1024], w[:, 0:768], w[:, 1536:1792], w[:, 1792:2048], w[:, 1280:1536], w[:, 1024:1280]], 1)))
        blocks.append(pair_blocks(np, i["w_out"][l]))
        blocks += ffn_blocks(np, i["w_ffn2_gu"][l], i["w_ffn2_down"][l])
    blocks += second_blocks(np, i)
    a["weights"] = np.concatenate(blocks, 0)

    pos = []
    for l in range(DEPTH):
        pos += [("w_mod", l, c) for c in range(18)]
        extra = [(2, 0), (2, 1), (2, 2), (2, 3), (1, 6), (1, 7)] if l == 0 else [(1, 8), (1, 9), (1, 10), (1, 11), (1, 4), (1, 5)]
        pos += [("w_ada_2", who, c) for who, c in extra]
    pos += [("w_ada_2", 1, c) for c in range(4)]
    ws, bs, cs = [], [], []
    for name, l, c in pos:
        first = name == "w_mod"
        w, b = (i["w_mod"][l], i["b_mod"][l]) if first else (i["w_ada_2"][0], i["b_ada_2"][0])
        cond = i["c"] if first else (i["c_2"] if l == 1 else i["c_ctx_2"])
        ws.append(w[:, c * MOD_COLS:(c + 1) * MOD_COLS].reshape(MOD_PIECES, MOD_K, P, MOD_COLS).transpose(0, 2, 1, 3)
                  .reshape(MOD_PIECES, P, MOD_K * MOD_COLS))
        bs.append(columns(np, b[c * MOD_COLS:(c + 1) * MOD_COLS]))
        cs.append(columns(np, cond))
    a["mod_w"] = np.stack(ws)
    a["mod_b"] = np.concatenate(bs, 1)
    a["cond"] = np.concatenate(cs, 1)
    a["gains"] = np.concatenate([columns(np, i["g_norm"][l, s]) for l in range(DEPTH) for s in range(3)]
                                + [columns(np, i[n]) for n in ("g_final", "norm1_g_2", "norm2_g_2", "final_g_2")], 1)
    lp, gw = [], []
    for l in range(DEPTH):
        lp += [np.broadcast_to(i["attn_sinks"][l][None], (P, HEADS)), columns(np, i["lru_conv_w"][l]), columns(np, i["lru_conv_b"][l]),
               columns(np, i["lru_gate_a_b"][l]), columns(np, i["lru_gate_x_b"][l]), columns(np, i["lru_lambda"][l]),
               columns(np, i["sc_conv_w"][l])]
        for w in (i["lru_gate_a_w"][l], i["lru_gate_x_w"][l]):
            for t in range(2):
                m = np.zeros((P, P), w.dtype)
                m[:64, :64], m[64:, 64:] = w[2 * t], w[2 * t + 1]
                gw.append(m)
    a["layer_par"] = np.concatenate(lp, 1)
    a["lru_gates"] = np.concatenate(gw, 1)
    a.update(second_tables(np, i))
    a["ident"] = np.eye(P, dtype=np.float32)
    dist = np.arange(P)[:, None] + WINDOW - np.arange(2 * WINDOW)[None]
    a["alibi"] = np.where((dist >= 0) & (dist < WINDOW), dist, 1e30).astype(np.float32)
    return {k: np.ascontiguousarray(v) for k, v in a.items()}


_OUTS = [((P, DC * T), "float32")]


def kernel(**inputs):
    import numpy as np
    import concourse.bacc as bacc
    from concourse.bass_utils import run_bass_kernel_spmd

    nc = bacc.Bacc("TRN2", target_bir_lowering=False, num_devices=1)
    arrays = layout(np, {k: np.asarray(v) for k, v in inputs.items()})
    args = {k: nc.dram_tensor(f"in_{k}_dram", v.shape, mybir.dt.from_np(v.dtype), kind="ExternalInput").ap()
            for k, v in arrays.items()}
    args["out"] = nc.dram_tensor("out_0_dram", _OUTS[0][0], F32, kind="ExternalOutput").ap()
    program(nc, args)
    r = run_bass_kernel_spmd(nc, [{f"in_{k}_dram": v for k, v in arrays.items()}], core_ids=[0])
    y = r.results[0]["out_0_dram"]
    return y.reshape(P, DC, T).transpose(2, 1, 0).reshape(1, T, D)
```
